# Optimizing a Trainium2 kernel written in Bass

```python
import math
import jax
import jax.numpy as jnp
from jax import lax
import numpy as np

D_MODEL = 1024
BATCH = 1
SEQ = 256
DEPTH = 2

GRID_W = 64
CTX_LEN = 256
HEAD_DIM = 64
ROPE_PAIRS_PER_AXIS = HEAD_DIM // 4
ROPE_THETA = 10000.0
EPS = 1e-6
Q_BLOCK = 128

NA_HEADS = 8
WIN_ROWS = 8
WIN_COLS = 16
GQA_HEADS = 8
GQA_KV_HEADS = 2
NA_W = NA_HEADS * HEAD_DIM
GQA_Q_W = GQA_HEADS * HEAD_DIM
GQA_KV_W = GQA_KV_HEADS * HEAD_DIM
AB_SPLITS = [NA_W, 2 * NA_W, 3 * NA_W, 3 * NA_W + GQA_Q_W, 3 * NA_W + GQA_Q_W + GQA_KV_W]
AB_IN = 3 * NA_W + GQA_Q_W + 2 * GQA_KV_W
AB_OUT = NA_W + GQA_Q_W

DIFF_HEADS = D_MODEL // (2 * HEAD_DIM)
DIFF_W = DIFF_HEADS * 2 * HEAD_DIM
DIFF_IN = 3 * DIFF_W

N_EXPERTS = 64
TOP_K = 8
D_EXPERT = D_MODEL // 4
ROUTED_SCALE = 2.5
MOE_BLOCK = 128

N_EVEN = (DEPTH + 1) // 2
N_ODD = DEPTH // 2

kernel_name = 'hybrid_na_gqa_diffattn_moe_dit'

def rms_norm(x, g):
    xf = x.astype(jnp.float32)
    y = xf * lax.rsqrt(jnp.mean(xf * xf, axis=-1, keepdims=True) + EPS)
    return (y * g.astype(jnp.float32)).astype(x.dtype)

def modulate(h, shift, scale):
    return h * (1.0 + scale) + shift

def to_heads(t, n_heads):
    b, s, _ = t.shape
    return t.reshape(b, s, n_heads, -1).transpose(0, 2, 1, 3)

def from_heads(t):
    b, h, s, d = t.shape
    return t.transpose(0, 2, 1, 3).reshape(b, s, h * d)

def axial_rope(n):
    t = jnp.arange(n, dtype=jnp.int32)
    row = (t // GRID_W).astype(jnp.float32)
    col = (t % GRID_W).astype(jnp.float32)
    inv_freq = ROPE_THETA ** (-jnp.arange(ROPE_PAIRS_PER_AXIS, dtype=jnp.float32) / ROPE_PAIRS_PER_AXIS)
    ang = jnp.concatenate([row[:, None] * inv_freq, col[:, None] * inv_freq], axis=-1)
    return jnp.cos(ang), jnp.sin(ang)

def apply_rope(x, cos, sin):
    xf = x.astype(jnp.float32)
    x1, x2 = xf[..., 0::2], xf[..., 1::2]
    out = jnp.stack([x1 * cos - x2 * sin, x1 * sin + x2 * cos], axis=-1).reshape(x.shape)
    return out.astype(x.dtype)

def gqa_attention(q, k, v):
    b, g, r, nq, d = q.shape
    blk = min(Q_BLOCK, nq)
    nb = nq // blk
    qb = jnp.moveaxis(q.reshape(b, g, r, nb, blk, d), 3, 0)
    scale = d ** -0.5

    def one_block(qblk):
        s = jnp.einsum('bgrqd,bgsd->bgrqs', qblk, k).astype(jnp.float32) * scale
        p = jax.nn.softmax(s, axis=-1).astype(v.dtype)
        return jnp.einsum('bgrqs,bgsd->bgrqd', p, v)

    o = lax.map(one_block, qb)
    return jnp.moveaxis(o, 0, 3).reshape(b, g * r, nq, d)

def neighbourhood_attention(q, k, v, k_ctx, v_ctx, rpb):
    b, h, n, d = q.shape
    rows = n // GRID_W
    kr = min(WIN_ROWS, rows)
    kc = WIN_COLS
    scale = d ** -0.5
    qg = q.reshape(b, h, rows, GRID_W, d)
    kg = k.reshape(b, h, rows, GRID_W, d)
    vg = v.reshape(b, h, rows, GRID_W, d)
    cols = jnp.arange(GRID_W, dtype=jnp.int32)
    col_start = jnp.clip(cols - kc // 2, 0, GRID_W - kc)
    col_idx = col_start[:, None] + jnp.arange(kc, dtype=jnp.int32)[None, :]
    col_bias_idx = col_idx - cols[:, None] + WIN_COLS - 1
    rpb_cols = rpb[:, :, col_bias_idx]

    def one_row(r):
        rs = jnp.clip(r - kr // 2, 0, rows - kr)
        k_rows = lax.dynamic_slice_in_dim(kg, rs, kr, axis=2)
        v_rows = lax.dynamic_slice_in_dim(vg, rs, kr, axis=2)
        k_win = k_rows[:, :, :, col_idx]
        v_win = v_rows[:, :, :, col_idx]
        q_row = lax.dynamic_index_in_dim(qg, r, axis=2, keepdims=False)
        row_bias_idx = rs + jnp.arange(kr, dtype=jnp.int32) - r + WIN_ROWS - 1
        bias = rpb_cols[:, row_bias_idx].transpose(0, 2, 1, 3).astype(jnp.float32)
        s_loc = jnp.einsum('bhqd,bhiqjd->bhqij', q_row, k_win).astype(jnp.float32) * scale + bias[None]
        s_ctx = jnp.einsum('bhqd,bhsd->bhqs', q_row, k_ctx).astype(jnp.float32) * scale
        s = jnp.concatenate([s_loc.reshape(b, h, GRID_W, kr * kc), s_ctx], axis=-1)
        p = jax.nn.softmax(s, axis=-1).astype(v.dtype)
        p_loc = p[..., :kr * kc].reshape(b, h, GRID_W, kr, kc)
        p_ctx = p[..., kr * kc:]
        return (jnp.einsum('bhqij,bhiqjd->bhqd', p_loc, v_win)
                + jnp.einsum('bhqs,bhsd->bhqd', p_ctx, v_ctx))

    o = lax.map(one_row, jnp.arange(rows, dtype=jnp.int32))
    return o.transpose(1, 2, 0, 3, 4).reshape(b, h, n, d)

def diff_attention(q, k, v, lam):
    b, h, _, nq, d = q.shape
    blk = min(Q_BLOCK, nq)
    nb = nq // blk
    qb = jnp.moveaxis(q.reshape(b, h, 2, nb, blk, d), 3, 0)
    scale = d ** -0.5

    def one_block(qblk):
        s = jnp.einsum('bhcqd,bhcsd->bhcqs', qblk, k).astype(jnp.float32) * scale
        p = jax.nn.softmax(s, axis=-1)
        pd = (p[:, :, 0] - lam * p[:, :, 1]).astype(v.dtype)
        return jnp.einsum('bhqs,bhse->bhqe', pd, v)

    o = lax.map(one_block, qb)
    return jnp.moveaxis(o, 0, 2).reshape(b, h, nq, 2 * d)

def group_q(q):
    b, h, s, d = q.shape
    return q.reshape(b, GQA_KV_HEADS, h // GQA_KV_HEADS, s, d)

def na_gqa_mixer(h_ctx, h_lat, w_in, w_out, rpb, q_gain, k_gain, cos, sin, need_ctx):
    qa_c, ka_c, va_c, qb_c, kb_c, vb_c = jnp.split(h_ctx @ w_in, AB_SPLITS, axis=-1)
    qa, ka, va, qb, kb, vb = jnp.split(h_lat @ w_in, AB_SPLITS, axis=-1)
    ka_c, va_c = to_heads(ka_c, NA_HEADS), to_heads(va_c, NA_HEADS)
    kb_c = rms_norm(to_heads(kb_c, GQA_KV_HEADS), k_gain)
    vb_c = to_heads(vb_c, GQA_KV_HEADS)
    qa, ka, va = to_heads(qa, NA_HEADS), to_heads(ka, NA_HEADS), to_heads(va, NA_HEADS)
    qb = apply_rope(rms_norm(to_heads(qb, GQA_HEADS), q_gain), cos, sin)
    kb = apply_rope(rms_norm(to_heads(kb, GQA_KV_HEADS), k_gain), cos, sin)
    vb = to_heads(vb, GQA_KV_HEADS)
    o_a = neighbourhood_attention(qa, ka, va, ka_c, va_c, rpb)
    o_b = gqa_attention(group_q(qb), jnp.concatenate([kb_c, kb], axis=2),
                        jnp.concatenate([vb_c, vb], axis=2))
    o_lat = from_heads(jnp.concatenate([o_a, o_b], axis=1)) @ w_out
    o_ctx = None
    if need_ctx:
        o_a_c = gqa_attention(to_heads(qa_c, NA_HEADS)[:, :, None], ka_c, va_c)
        qb_c = rms_norm(to_heads(qb_c, GQA_HEADS), q_gain)
        o_b_c = gqa_attention(group_q(qb_c), kb_c, vb_c)
        o_ctx = from_heads(jnp.concatenate([o_a_c, o_b_c], axis=1)) @ w_out
    return o_ctx, o_lat

def diff_mixer(h_ctx, h_lat, w_in, w_out, lq1, lk1, lq2, lk2, sub_gain, lam_init, cos, sin, need_ctx):
    f32 = jnp.float32
    lam = (jnp.exp(jnp.sum(lq1.astype(f32) * lk1.astype(f32)))
           - jnp.exp(jnp.sum(lq2.astype(f32) * lk2.astype(f32))) + lam_init)

    def project(hs):
        b, s, _ = hs.shape
        q, k, v = jnp.split(hs @ w_in, 3, axis=-1)
        q = q.reshape(b, s, DIFF_HEADS, 2, HEAD_DIM).transpose(0, 2, 3, 1, 4)
        k = k.reshape(b, s, DIFF_HEADS, 2, HEAD_DIM).transpose(0, 2, 3, 1, 4)
        return q, k, to_heads(v, DIFF_HEADS)

    def finish(o):
        return from_heads(rms_norm(o, sub_gain) * (1.0 - lam_init)) @ w_out

    q_c, k_c, v_c = project(h_ctx)
    q, k, v = project(h_lat)
    q, k = apply_rope(q, cos, sin), apply_rope(k, cos, sin)
    k_all = jnp.concatenate([k_c, k], axis=3)
    v_all = jnp.concatenate([v_c, v], axis=2)
    o_lat = finish(diff_attention(q, k_all, v_all, lam))
    o_ctx = finish(diff_attention(q_c, k_c, v_c, lam)) if need_ctx else None
    return o_ctx, o_lat

def moe_ffn(h, router_w, router_bias, w_gate, w_up, w_down, sh_gate, sh_up, sh_down):
    t, d = h.shape
    scores = jax.nn.sigmoid(h.astype(jnp.float32) @ router_w.astype(jnp.float32))
    _, idx = lax.top_k(scores + router_bias.astype(jnp.float32), TOP_K)
    s_sel = jnp.take_along_axis(scores, idx, axis=-1)
    gates = s_sel / jnp.sum(s_sel, axis=-1, keepdims=True) * ROUTED_SCALE
    a = t * TOP_K
    e_flat = idx.reshape(a).astype(jnp.int32)
    tok_flat = jnp.arange(a, dtype=jnp.int32) // TOP_K
    g_flat = gates.reshape(a)
    order = jnp.argsort(e_flat)
    e_sorted, tok_sorted, g_sorted = e_flat[order], tok_flat[order], g_flat[order]
    counts = jnp.bincount(e_flat, length=N_EXPERTS).astype(jnp.int32)
    starts = jnp.cumsum(counts) - counts
    padded = (counts + MOE_BLOCK - 1) // MOE_BLOCK * MOE_BLOCK
    pad_ends = jnp.cumsum(padded)
    pad_starts = pad_ends - padded
    dest = pad_starts[e_sorted] + jnp.arange(a, dtype=jnp.int32) - starts[e_sorted]
    n_blocks = (a + N_EXPERTS * (MOE_BLOCK - 1) + MOE_BLOCK - 1) // MOE_BLOCK
    n_pad = n_blocks * MOE_BLOCK
    buf_tok = jnp.full((n_pad,), t, dtype=jnp.int32).at[dest].set(tok_sorted)
    buf_gate = jnp.zeros((n_pad,), jnp.float32).at[dest].set(g_sorted)
    block_starts = jnp.arange(n_blocks, dtype=jnp.int32) * MOE_BLOCK
    blk_expert = jnp.minimum(jnp.searchsorted(pad_ends, block_starts, side='right'), N_EXPERTS - 1)
    h_pad = jnp.concatenate([h, jnp.zeros((1, d), h.dtype)], axis=0)

    def expert_block(args):
        tok, e = args
        xb = h_pad[tok]
        hid = jax.nn.silu(xb @ w_gate[e]) * (xb @ w_up[e])
        return hid @ w_down[e]

    y = lax.map(expert_block, (buf_tok.reshape(n_blocks, MOE_BLOCK), blk_expert))
    y = y.reshape(n_pad, d) * buf_gate[:, None].astype(y.dtype)
    routed = jax.ops.segment_sum(y, buf_tok, num_segments=t + 1)[:t]
    shared = (jax.nn.silu(h @ sh_gate) * (h @ sh_up)) @ sh_down
    return routed + shared

def setup_inputs(seed: int = 0) -> dict:
    key = jax.random.key(seed)
    keys = jax.random.split(key, 29)
    D, E, F = D_MODEL, N_EXPERTS, D_EXPERT

    def normal(i, shape, scale):
        return jax.random.normal(keys[i], shape, jnp.float32) * scale

    def gain(i, shape):
        return 1.0 + normal(i, shape, 0.05)

    return {
        'x': normal(0, (BATCH, SEQ, D), 1.0),
        'c': normal(1, (BATCH, D), 1.0),
        'ctx': normal(2, (BATCH, CTX_LEN, D), 1.0),
        'c_ctx': normal(3, (D,), 1.0),
        'ada_w': normal(4, (DEPTH, D, 6 * D), 0.5 * D ** -0.5),
        'ada_b': normal(5, (DEPTH, 6 * D), 0.02),
        'norm_mix': gain(6, (DEPTH, D)),
        'norm_ffn': gain(7, (DEPTH, D)),
        'ab_w_in': normal(8, (N_EVEN, D, AB_IN), D ** -0.5),
        'ab_w_out': normal(9, (N_EVEN, AB_OUT, D), AB_OUT ** -0.5),
        'na_rpb': normal(10, (N_EVEN, NA_HEADS, 2 * WIN_ROWS - 1, 2 * WIN_COLS - 1), 0.05),
        'gqa_q_gain': gain(11, (N_EVEN, HEAD_DIM)),
        'gqa_k_gain': gain(12, (N_EVEN, HEAD_DIM)),
        'diff_w_in': normal(13, (N_ODD, D, DIFF_IN), D ** -0.5),
        'diff_w_out': normal(14, (N_ODD, DIFF_W, D), DIFF_W ** -0.5),
        'diff_lq1': normal(15, (N_ODD, HEAD_DIM), 0.1),
        'diff_lk1': normal(16, (N_ODD, HEAD_DIM), 0.1),
        'diff_lq2': normal(17, (N_ODD, HEAD_DIM), 0.1),
        'diff_lk2': normal(18, (N_ODD, HEAD_DIM), 0.1),
        'diff_sub_gain': gain(19, (N_ODD, 2 * HEAD_DIM)),
        'router_w': normal(20, (DEPTH, D, E), D ** -0.5),
        'router_bias': normal(21, (DEPTH, E), 0.01),
        'expert_w_gate': normal(22, (DEPTH, E, D, F), D ** -0.5),
        'expert_w_up': normal(23, (DEPTH, E, D, F), D ** -0.5),
        'expert_w_down': normal(24, (DEPTH, E, F, D), F ** -0.5),
        'shared_w_gate': normal(25, (DEPTH, D, F), D ** -0.5),
        'shared_w_up': normal(26, (DEPTH, D, F), D ** -0.5),
        'shared_w_down': normal(27, (DEPTH, F, D), F ** -0.5),
        'final_norm': gain(28, (D,)),
    }

def reference(x, c, ctx, c_ctx, ada_w, ada_b, norm_mix, norm_ffn, ab_w_in, ab_w_out, na_rpb,
              gqa_q_gain, gqa_k_gain, diff_w_in, diff_w_out, diff_lq1, diff_lk1, diff_lq2, diff_lk2,
              diff_sub_gain, router_w, router_bias, expert_w_gate, expert_w_up, expert_w_down,
              shared_w_gate, shared_w_up, shared_w_down, final_norm):
    b, n, d = x.shape
    L = ctx.shape[1]
    cos, sin = axial_rope(n)
    silu_c = jax.nn.silu(c)
    silu_cc = jax.nn.silu(c_ctx)
    xc = ctx
    for l in range(DEPTH):
        last = l == DEPTH - 1
        i = l // 2
        mod = silu_c @ ada_w[l] + ada_b[l]
        mod_c = silu_cc @ ada_w[l] + ada_b[l]
        sh_m, sc_m, g_m, sh_f, sc_f, g_f = jnp.split(mod[:, None, :], 6, axis=-1)
        sh_mc, sc_mc, g_mc, sh_fc, sc_fc, g_fc = jnp.split(mod_c, 6, axis=-1)
        h = modulate(rms_norm(x, norm_mix[l]), sh_m, sc_m)
        hc = modulate(rms_norm(xc, norm_mix[l]), sh_mc, sc_mc)
        if l % 2 == 0:
            o_c, o = na_gqa_mixer(hc, h, ab_w_in[i], ab_w_out[i], na_rpb[i], gqa_q_gain[i],
                                  gqa_k_gain[i], cos, sin, not last)
        else:
            lam_init = 0.8 - 0.6 * math.exp(-0.3 * l)
            o_c, o = diff_mixer(hc, h, diff_w_in[i], diff_w_out[i], diff_lq1[i], diff_lk1[i],
                                diff_lq2[i], diff_lk2[i], diff_sub_gain[i], lam_init, cos, sin, not last)
        x = x + g_m * o
        moe_args = (router_w[l], router_bias[l], expert_w_gate[l], expert_w_up[l], expert_w_down[l],
                    shared_w_gate[l], shared_w_up[l], shared_w_down[l])
        if last:
            h = modulate(rms_norm(x, norm_ffn[l]), sh_f, sc_f)
            x = x + g_f * moe_ffn(h.reshape(b * n, d), *moe_args).reshape(b, n, d)
        else:
            xc = xc + g_mc * o_c
            h = modulate(rms_norm(x, norm_ffn[l]), sh_f, sc_f)
            hc = modulate(rms_norm(xc, norm_ffn[l]), sh_fc, sc_fc)
            tokens = jnp.concatenate([hc, h], axis=1).reshape(b * (L + n), d)
            y = moe_ffn(tokens, *moe_args).reshape(b, L + n, d)
            xc = xc + g_fc * y[:, :L]
            x = x + g_f * y[:, L:]
    return rms_norm(x, final_norm)


_drawn_inputs = setup_inputs


def setup_inputs(seed=0):
    import zlib

    import numpy as np

    out = dict(_drawn_inputs(seed))
    spreads = {}
    factors = {'na_rpb': 8.0,
     'gqa_q_gain': 5.254,
     'gqa_k_gain': 6.732,
     'diff_lk1': 2.781,
     'diff_lk2': 3.674,
     'diff_sub_gain': 3.006}
    for name, (base, spread) in spreads.items():
        noise = np.random.default_rng([zlib.crc32(name.encode()), seed]).standard_normal(out[name].shape)
        drawn = base * np.exp(spread * noise) if base else spread * noise
        out[name] = jnp.asarray(drawn.astype(out[name].dtype))
    for name, factor in factors.items():
        out[name] = (out[name] * factor).astype(out[name].dtype)
    return out
```

```python
from contextlib import ExitStack

import numpy as np

import concourse.bass as bass
from concourse import mybir

F32 = mybir.dt.float32
BF16 = mybir.dt.bfloat16
I32 = mybir.dt.int32
ALU = mybir.AluOpType
ACT = mybir.ActivationFunctionType
AX = mybir.AxisListType.X

P = 128
D = 1024
KD = D // P
CTX = 256
LAT = 256
GRID_W = 64
WIN_COLS = 16
WIN_ROWS = 8
HEAD = 64
NA_HEADS = 8
GQA_HEADS = 8
GQA_KV = 2
HEADS = NA_HEADS + GQA_HEADS
DIFF_HEADS = 8
EPS = 1e-6
SCALE = HEAD ** -0.5
E = 64
TOP_K = 8
F = D // 4
KF = F // P
ROUTED_SCALE = 2.5
LAM_INIT = 0.8 - 0.6 * float(np.exp(-0.3))
STREAMS = 2
TILES = (CTX + LAT) // P
SLOTS = 128
BIG = 16384
MASKED = -1e30
NA_ROWS = LAT // GRID_W
REL = NA_ROWS + 2
ROPE = HEAD // 2

CONST = {}
_at = 0
for _name, _n in (("ident", P), ("flip", P), ("before", P), ("ones", P), ("iota", 512), ("pick", 2),
                  ("na_mask", GRID_W), ("cos", 2 * ROPE), ("sin", 2 * ROPE), ("tok_hi", TILES),
                  ("dest_hi", TILES), ("tok_lo", 1), ("dest_lo", 1)):
    CONST[_name] = (_at, _at + _n)
    _at += _n
CONST_W = _at


def constants():
    c = np.zeros((P, CONST_W), np.float32)

    def put(name, a):
        c[:, CONST[name][0]:CONST[name][1]] = a

    p = np.arange(P)
    put("ident", np.eye(P))
    flip = np.zeros((P, P))
    for half in range(2):
        for i in range(GRID_W):
            flip[half * GRID_W + i, half * GRID_W + GRID_W - 1 - i] = 1.0
    put("flip", flip)
    put("before", p[:, None] < p[None, :])
    put("ones", np.ones((P, P)))
    put("iota", np.tile(np.arange(512), (P, 1)))
    pick = np.zeros((P, 2))
    for g in range(4):
        pick[32 * g, 0] = pick[32 * g + 1, 1] = 1.0
    put("pick", pick)
    col = GRID_W - 1 - p % GRID_W
    start = np.clip(col - WIN_COLS // 2, 0, GRID_W - WIN_COLS)
    key = np.arange(GRID_W)
    inside = (key[None] >= start[:, None]) & (key[None] < start[:, None] + WIN_COLS)
    put("na_mask", np.where(inside, 0.0, MASKED))
    t = np.arange(LAT)
    pairs = HEAD // 4
    freq = (np.float32(10000.0) ** (-np.arange(pairs, dtype=np.float32) / np.float32(pairs))).astype(np.float32)
    row, column = (t // GRID_W).astype(np.float32), (t % GRID_W).astype(np.float32)
    angle = np.concatenate([row[:, None] * freq, column[:, None] * freq], axis=-1).astype(np.float32)
    put("cos", np.cos(angle).reshape(2, P, ROPE).transpose(1, 0, 2).reshape(P, -1))
    put("sin", np.sin(angle).reshape(2, P, ROPE).transpose(1, 0, 2).reshape(P, -1))
    put("tok_hi", np.tile(P * np.arange(TILES) - BIG, (P, 1)))
    put("dest_hi", np.tile(TOP_K * P * np.arange(TILES) - BIG, (P, 1)))
    put("tok_lo", p[:, None])
    put("dest_lo", TOP_K * p[:, None])
    return c


class Stage:

    def __init__(self, nc, name):
        self.nc, self.name, self.sems, self.stack = nc, name, [], ExitStack()

    def __enter__(self):
        return self

    def sb(self, name, shape, dt=F32):
        return self.stack.enter_context(self.nc.sbuf_tensor(f"{self.name}_{name}", shape, dt))

    def sem(self, name):
        s = self.stack.enter_context(self.nc.semaphore(f"{self.name}_{name}"))
        self.sems.append(s)
        return s

    def pool_sem(self, name):
        return self.nc.alloc_semaphore(f"{self.name}_{name}")

    def __exit__(self, *a):
        if a[0] is None:
            with self.nc.Block() as block:
                @block.sync
                def _(sp):
                    for s in self.sems:
                        sp.sem_clear(s)
        self.stack.close()


class Chain:

    def __init__(self, eng, sem):
        self.eng, self.sem, self.n = eng, sem, 0

    def __call__(self, ins):
        self.n += 1
        ins.then_inc(self.sem, 1)
        self.eng.wait_ge(self.sem, self.n)


class Core:

    def __init__(self, nc, ctx):
        def sb(name, shape, dt=F32):
            return ctx.enter_context(nc.sbuf_tensor(name, shape, dt))

        self.nc = nc
        self.x = sb("x_res", [P, TILES, D])
        self.const = sb("const", [P, CONST_W])
        self.cols = sb("cols", [P, P])
        self.mod = sb("mod", [P, 2, 6 * KD, STREAMS])
        self.amp = sb("amp", [P, 2, 2, STREAMS, KD])
        self.hT = sb("hT", [P, KD, TILES * P])
        self.ps = ctx.enter_context(nc.psum_tensor("ps", [P, 8, 512], F32))

    def c(self, name):
        return self.const[:, CONST[name][0]:CONST[name][1]]

    def gate_column(self, layer, which, stream, k):
        return self.mod[:, layer, (2 + 3 * which) * KD + k, stream:stream + 1]

    def shift_column(self, layer, which, stream, k):
        return self.mod[:, layer, 3 * which * KD + k, stream:stream + 1]


def modulation(core, a):
    nc = core.nc
    COLS = 512
    NB = 6 * D // COLS
    RING = 4
    with Stage(nc, "adaln") as st:
        w = st.sb("w", [P, RING, KD, COLS])
        rows = st.sb("rows", [P, P])
        cond = st.sb("cond", [P, STREAMS, KD])
        tmp = st.sb("tmp", [P, 2, STREAMS * KD])
        silu = st.sb("silu", [P, KD, 32])
        part = st.sb("part", [P, 2, COLS])
        loaded = [st.sem(f"loaded{i}") for i in range(RING)]
        const_in, rows_in, cond_in = st.sem("const_in"), st.sem("rows_in"), st.sem("cond_in")
        x_in = st.sem("x_in")
        e_ready, silu_ready = st.sem("e_ready"), st.sem("silu_ready")
        sums_ready, part_ready = st.sem("sums_ready"), st.sem("part_ready")
        colsum_ready, col_done = st.sem("colsum_ready"), st.sem("col_done")
        rowsT, own = st.sem("rowsT"), st.sem("own")
        w_view = a["ada_w"].rearrange("l (p k) (b n) -> l b p k n", k=KD, n=COLS)
        blocks = 2 * NB
        with nc.Block() as block:
            @block.sync
            def _(sp):
                sp.dma_start(cond[:, 0, :], a["c_ctx"].rearrange("(p k) -> p k", k=KD)).then_inc(cond_in, 16)
                sp.dma_start(cond[:, 1, :], a["c"].rearrange("o (p k) -> (o p) k", k=KD)).then_inc(cond_in, 16)
                for n in range(RING):
                    sp.dma_start(w[:, n], w_view[0, n]).then_inc(loaded[n], 16)
                sp.dma_start(core.const[:], a["consts"]).then_inc(const_in, 16)
                nb = 2 * 6 * KD
                sp.dma_start(rows[0:nb, :], a["ada_b"].rearrange("l (j p) -> (l j) p", p=P)).then_inc(rows_in, 16)
                sp.dma_start(rows[nb:nb + 16, :], a["norm_mix"].rearrange("l (j p) -> (l j) p", p=P)).then_inc(rows_in, 16)
                sp.dma_start(rows[nb + 16:nb + 32, :], a["norm_ffn"].rearrange("l (j p) -> (l j) p", p=P)).then_inc(rows_in, 16)
                sp.dma_start(core.x[:, 0:2], a["ctx"].rearrange("o (t p) d -> p (o t) d", p=P)).then_inc(x_in, 16)
                sp.dma_start(core.x[:, 2:4], a["x"].rearrange("o (t p) d -> p (o t) d", p=P)).then_inc(x_in, 16)
                for n in range(RING, blocks):
                    sp.wait_ge(sums_ready, n - RING + 1)
                    sp.dma_start(w[:, n % RING], w_view[n // NB, n % NB]).then_inc(loaded[n % RING], 16)
                sp.wait_ge(x_in, 32)

            @block.scalar
            def _(act):
                act.wait_ge(cond_in, 32)
                nc.scalar.activation(tmp[:, 0, :], cond[:].rearrange("p s k -> p (s k)"), ACT.Exp,
                                     scale=-1.0).then_inc(e_ready, 1)

            @block.tensor
            def _(pe):
                pe.wait_ge(silu_ready, 1)

                def column_sums(n):
                    pe.wait_ge(part_ready, n + 1)
                    pe.wait_ge(const_in, 16)
                    if n >= 2:
                        pe.wait_ge(col_done, n - 1)
                    for j in range(4):
                        mm = nc.tensor.matmul(core.ps[:, 4 + n % 2, 2 * j:2 * j + 2],
                                              part[:, n % 2, j * P:(j + 1) * P], core.c("pick"),
                                              start=True, stop=True)
                    mm.then_inc(colsum_ready, 1)

                for n in range(blocks):
                    pe.wait_ge(loaded[n % RING], 16 * (n // RING + 1))
                    if n >= 4:
                        pe.wait_ge(part_ready, n - 3)
                    for k in range(KD):
                        g = 32 * (k % 4)
                        mm = nc.tensor.matmul(core.ps[g:g + 32, n % 4, :], silu[:, k, :], w[:, n % RING, k, :],
                                              start=k < 4, stop=k >= 4, skip_group_check=True, tile_position=(0, g))
                    mm.then_inc(sums_ready, 1)
                    if n >= 1:
                        column_sums(n - 1)
                column_sums(blocks - 1)
                pe.wait_ge(rows_in, 48)
                nc.tensor.transpose(core.ps[:, 6, 0:P], rows[:], core.c("ident")).then_inc(rowsT, 1)

            @block.vector
            def _(dve):
                link = Chain(dve, own)
                link(nc.vector.memset(silu[:], 0.0))
                dve.wait_ge(e_ready, 1)
                link(nc.vector.tensor_scalar(tmp[:, 1, :], tmp[:, 0, :], 1.0, None, ALU.add))
                link(nc.vector.reciprocal(tmp[:, 0, :], tmp[:, 1, :]))
                nc.vector.tensor_tensor(silu[:, :, 0:STREAMS].rearrange("p k s -> p s k"), cond[:],
                                        tmp[:, 0, :].rearrange("p (s k) -> p s k", s=STREAMS),
                                        ALU.mult).then_inc(silu_ready, 1)
                modf = core.mod[:].rearrange("p l j s -> p (l j s)")

                def take_columns(n):
                    dve.wait_ge(colsum_ready, n + 1)
                    nc.vector.tensor_copy(modf[:, 8 * n:8 * n + 8], core.ps[:, 4 + n % 2, 0:8]).then_inc(col_done, 1)

                for n in range(blocks):
                    dve.wait_ge(sums_ready, n + 1)
                    if n >= 2:
                        dve.wait_ge(colsum_ready, n - 1)
                    nc.vector.tensor_copy(part[:, n % 2, :], core.ps[:, n % 4, :]).then_inc(part_ready, 1)
                    if n >= 1:
                        take_columns(n - 1)
                take_columns(blocks - 1)
                dve.wait_ge(rowsT, 1)
                link(nc.vector.tensor_copy(core.cols[:], core.ps[:, 6, 0:P]))
                dve.wait_ge(col_done, blocks)
                for s in range(STREAMS):
                    m = core.mod[:, :, :, s].rearrange("p l j -> p (l j)")
                    link(nc.vector.tensor_tensor(m, m, core.cols[:, 0:12 * KD], ALU.add))
                for layer in range(2):
                    for which in range(2):
                        gain = core.cols[:, 12 * KD + 16 * which + KD * layer:][:, 0:KD]
                        for s in range(STREAMS):
                            scale = core.mod[:, layer, (3 * which + 1) * KD:(3 * which + 2) * KD, s]
                            link(nc.vector.scalar_tensor_tensor(out=core.amp[:, layer, which, s, :], in0=scale,
                                                                scalar=1.0, in1=gain, op0=ALU.add, op1=ALU.mult))


def rms_rows(core, tiles, out, ss, rs, sq_ready, root_ready, var_ready):
    nc, n = core.nc, len(tiles)

    def on_act(act):
        for i, t in enumerate(tiles):
            ins = nc.scalar.activation(out[:, i, :], core.x[:, t, :], ACT.Square, accum_out=ss[:, i:i + 1])
        ins.then_inc(sq_ready, 1)
        act.wait_ge(var_ready, 1)
        nc.scalar.activation(rs[:, 1, 0:n], rs[:, 0, 0:n], ACT.Sqrt).then_inc(root_ready, 1)

    def on_dve(dve, link, row_ready):
        dve.wait_ge(sq_ready, 1)
        nc.vector.tensor_scalar(rs[:, 0, 0:n], ss[:, 0:n], 1.0 / D, EPS, ALU.mult, ALU.add).then_inc(var_ready, 1)
        dve.wait_ge(root_ready, 1)
        link(nc.vector.reciprocal(rs[:, 2, 0:n], rs[:, 1, 0:n]))
        for i, t in enumerate(tiles):
            nc.vector.tensor_scalar(out[:, i, :], core.x[:, t, :], rs[:, 2, i:i + 1], None,
                                    ALU.mult).then_inc(row_ready, 1)

    return on_act, on_dve


def norm_transpose(core, layer, which, streams):
    nc = core.nc
    name = f"norm{layer}{which}"
    tiles = [2 * s + i for s in streams for i in range(2)]
    with Stage(nc, name) as st:
        xn = st.sb("xn", [P, len(tiles), D])
        ss, rs = st.sb("ss", [P, TILES]), st.sb("rs", [P, 3, TILES])
        sq_ready, var_ready, root_ready = st.sem("sq"), st.sem("var"), st.sem("root")
        row_ready, turned, taken = st.sem("row"), st.sem("turned"), [st.sem("taken_dve"), st.sem("taken_act")]
        own = st.sem("own")
        items = [(i, s, k) for i, s in enumerate(streams) for k in range(KD)]
        on_act, on_dve = rms_rows(core, tiles, xn, ss, rs, sq_ready, root_ready, var_ready)

        def scaled(n, engine):
            i, s, k = items[n]
            return (core.hT[:, k, s * CTX:s * CTX + CTX], core.ps[:, n % 8, 0:CTX],
                    core.amp[:, layer, which, s, k:k + 1], core.shift_column(layer, which, s, k))

        with nc.Block() as block:
            @block.scalar
            def _(act):
                on_act(act)
                for n in range(1, len(items), 2):
                    act.wait_ge(turned, n + 1)
                    out, src, amp, shift = scaled(n, act)
                    nc.scalar.activation(out, src, ACT.Identity, scale=amp, bias=shift).then_inc(taken[1], 1)

            @block.tensor
            def _(pe):
                for n, (i, s, k) in enumerate(items):
                    pe.wait_ge(row_ready, 2 * i + 2)
                    if n >= 8:
                        pe.wait_ge(taken[n % 2], (n - 8) // 2 + 1)
                    for j in range(2):
                        mm = nc.tensor.transpose(core.ps[:, n % 8, j * P:(j + 1) * P],
                                                 xn[:, 2 * i + j, k * P:(k + 1) * P], core.c("ident"))
                    mm.then_inc(turned, 1)

            @block.vector
            def _(dve):
                link = Chain(dve, own)
                on_dve(dve, link, row_ready)
                for n in range(0, len(items), 2):
                    dve.wait_ge(turned, n + 1)
                    out, src, amp, shift = scaled(n, dve)
                    nc.vector.tensor_scalar(out, src, amp, shift, ALU.mult, ALU.add).then_inc(taken[0], 1)




def project_even(core, a, w):
    nc = core.nc
    COLS = 512
    widths = [COLS] * 4 + [2 * GQA_KV * HEAD]
    RING = 3
    with Stage(nc, "proj0") as st:
        wb = st.sb("w", [P, RING, KD, COLS])
        loaded = [st.sem(f"loaded{i}") for i in range(RING)]
        summed, taken = st.sem("summed"), [st.sem("taken_dve"), st.sem("taken_act")]
        w_view = a["ab_w_in"].rearrange("o (k p) n -> p (o k) n", p=P)
        items = [(b, j) for b in range(len(widths)) for j in range(4)]

        def load(sp, b):
            sp.dma_start(wb[:, b % RING, :, 0:widths[b]], w_view[:, :, b * COLS:b * COLS + widths[b]]).then_inc(
                loaded[b % RING], 16)

        def target(b, j):
            if b < 2:
                return (w.qaT, w.kaT)[b][:, j, :], COLS
            if b == 4:
                return w.kvb[:, j, :], widths[4]
            return (w.va, w.qb)[b - 2][:, j, :], COLS

        with nc.Block() as block:
            @block.sync
            def _(sp):
                for b in range(len(widths)):
                    if b >= RING:
                        sp.wait_ge(summed, 4 * (b - RING + 1))
                    load(sp, b)

            @block.tensor
            def _(pe):
                for n, (b, j) in enumerate(items):
                    if j == 0:
                        pe.wait_ge(loaded[b % RING], 16 * (b // RING + 1))
                    if n >= 8:
                        pe.wait_ge(taken[n % 2], (n - 8) // 2 + 1)
                    for k in range(KD):
                        if b < 2:
                            lhs, rhs = wb[:, b % RING, k, j * P:(j + 1) * P], core.hT[:, k, :]
                        else:
                            lhs, rhs = core.hT[:, k, j * P:(j + 1) * P], wb[:, b % RING, k, 0:widths[b]]
                        mm = nc.tensor.matmul(core.ps[:, n % 8, 0:widths[b]], lhs, rhs, start=k == 0,
                                              stop=k == KD - 1)
                    mm.then_inc(summed, 1)

            @block.vector
            def _(dve):
                for n in range(0, len(items), 2):
                    out, wide = target(*items[n])
                    dve.wait_ge(summed, n + 1)
                    nc.vector.tensor_scalar(out, core.ps[:, n % 8, 0:wide], SCALE if items[n][0] == 0 else 1.0,
                                            None, ALU.mult).then_inc(taken[0], 1)

            @block.scalar
            def _(act):
                for n in range(1, len(items), 2):
                    out, wide = target(*items[n])
                    act.wait_ge(summed, n + 1)
                    nc.scalar.activation(out, core.ps[:, n % 8, 0:wide], ACT.Copy,
                                         scale=SCALE if items[n][0] == 0 else 1.0).then_inc(taken[1], 1)


def rotate(nc, link, pairs, tmp, cos, sin):
    heads = pairs.shape[1]
    even, odd = pairs[:, :, :, 0], pairs[:, :, :, 1]
    t = [tmp[:, i, 0:heads * ROPE].rearrange("p (h r) -> p h r", h=heads) for i in range(4)]
    c = cos.rearrange("p (o r) -> p o r", o=1).to_broadcast([P, heads, ROPE])
    s = sin.rearrange("p (o r) -> p o r", o=1).to_broadcast([P, heads, ROPE])
    nc.vector.tensor_tensor(t[0], even, c, ALU.mult)
    nc.vector.tensor_tensor(t[1], odd, s, ALU.mult)
    nc.vector.tensor_tensor(t[2], even, s, ALU.mult)
    link(nc.vector.tensor_tensor(t[3], odd, c, ALU.mult))
    nc.vector.tensor_tensor(even, t[0], t[1], ALU.subtract)
    link(nc.vector.tensor_tensor(odd, t[2], t[3], ALU.add))


def qk_norm_rope(core, a, w):
    nc = core.nc
    with Stage(nc, "qknorm") as st:
        gain = st.sb("gain", [P, 2, HEAD])
        sq = st.sb("sq", [P, TILES, GQA_HEADS * HEAD])
        ss = st.sb("ss", [P, 4, TILES * GQA_HEADS])
        sk = st.sb("sk", [P, 4, TILES * GQA_KV])
        tmp = st.sb("tmp", [P, 4, GQA_HEADS * ROPE])
        kdup = st.sb("kdup", [P, TILES, GQA_KV, 2, HEAD])
        gains_in, own = st.sem("gains_in"), st.sem("own")
        var_ready, root_ready = st.sem("var_ready"), st.sem("root_ready")
        q_tile, k_ready = st.sem("q_tile"), st.sem("k_ready")
        turned, taken = st.sem("turned"), [st.sem("taken_dve"), st.sem("taken_act")]
        rpb_sem, rpb_ready = st.pool_sem("rpb_sem"), st.sem("rpb_ready")
        rows = 2 * WIN_ROWS - 1
        pad = st.sb("rpb_pad", [NA_HEADS * rows, P])
        q = w.qb
        k = w.kvb[:, :, 0:GQA_KV * HEAD]
        items = [("q", c) for c in range(4)] + [("k", g) for g in range(GQA_KV)]
        with nc.Block() as block:
            @block.sync
            def _(sp):
                sp.dma_start(gain[:, 0, :], a["gqa_q_gain"].to_broadcast([P, HEAD])).then_inc(gains_in, 16)
                sp.dma_start(gain[:, 1, :], a["gqa_k_gain"].to_broadcast([P, HEAD])).then_inc(gains_in, 16)

            @block.gpsimd
            def _(pool):
                nc.gpsimd.memset(pad[:], 0.0).then_inc(rpb_ready, 1)
                pool.wait_ge(rpb_ready, 1)
                pool.dma_start(pad[:, GRID_W - WIN_COLS:GRID_W + WIN_COLS - 1],
                               a["na_rpb"].rearrange("o h r c -> (o h r) c")).then_inc(rpb_sem, 16)
                pool.wait_ge(rpb_sem, 16)
                pool.dma_start(w.rpb_rows, pad[:]).then_inc(rpb_sem, 16)
                pool.wait_ge(rpb_sem, 32)
                for half in range(2):
                    for h in range(NA_HEADS):
                        start = (h * rows + WIN_ROWS - 1 - 2 - half) * P
                        src = bass.AP(w.rpb_rows.tensor, start, [[1, GRID_W], [P, REL], [1, GRID_W]])
                        pool.dma_start(w.bias[half * GRID_W:(half + 1) * GRID_W, h], src).then_inc(rpb_sem, 16)
                pool.wait_ge(rpb_sem, 32 + 16 * 2 * NA_HEADS)
                m = core.c("na_mask").rearrange("p (o c) -> p o c", o=1).to_broadcast([P, NA_HEADS * REL, GRID_W])
                b = w.bias[:].rearrange("p h u c -> p (h u) c")
                nc.gpsimd.tensor_tensor(b, b, m, ALU.add).then_inc(rpb_ready, 1)

            @block.scalar
            def _(act):
                act.wait_ge(var_ready, 1)
                nc.scalar.activation(ss[:, 2, :], ss[:, 1, :], ACT.Sqrt)
                nc.scalar.activation(sk[:, 2, :], sk[:, 1, :], ACT.Sqrt).then_inc(root_ready, 1)
                for n in range(1, len(items), 2):
                    act.wait_ge(turned, n + 1)
                    kind, c = items[n]
                    nc.scalar.copy((w.qbT if kind == "q" else w.kbT)[:, c, :], core.ps[:, n, :]).then_inc(taken[1], 1)

            @block.vector
            def _(dve):
                link = Chain(dve, own)
                nq, nk = GQA_HEADS * HEAD, GQA_KV * HEAD
                nc.vector.tensor_tensor(sq[:], q[:], q[:], ALU.mult)
                link(nc.vector.tensor_tensor(kdup[:].rearrange("p t g u d -> p t (g u d)")[:, :, 0:nk], k, k, ALU.mult))
                nc.vector.tensor_reduce(ss[:, 0, :], sq[:].rearrange("p t (h d) -> p (t h) d", d=HEAD), AX, ALU.add)
                link(nc.vector.tensor_reduce(sk[:, 0, :].rearrange("p (t g) -> p t g", t=TILES),
                                             kdup[:].rearrange("p t g u d -> p t (g u d)")[:, :, 0:nk]
                                             .rearrange("p t (g d) -> p t g d", d=HEAD), AX, ALU.add))
                nc.vector.tensor_scalar(ss[:, 1, :], ss[:, 0, :], 1.0 / HEAD, EPS, ALU.mult, ALU.add)
                nc.vector.tensor_scalar(sk[:, 1, :], sk[:, 0, :], 1.0 / HEAD, EPS, ALU.mult,
                                        ALU.add).then_inc(var_ready, 1)
                dve.wait_ge(gains_in, 32)
                link(nc.vector.tensor_scalar(gain[:, 0, :], gain[:, 0, :], SCALE, None, ALU.mult))
                dve.wait_ge(root_ready, 1)
                nc.vector.reciprocal(ss[:, 3, :], ss[:, 2, :])
                link(nc.vector.reciprocal(sk[:, 3, :], sk[:, 2, :]))
                for t in range(TILES):
                    qt = q[:, t, :].rearrange("p (h d) -> p h d", d=HEAD)
                    kt = k[:, t, :].rearrange("p (h d) -> p h d", d=HEAD)
                    for x, heads, r, g in ((qt, GQA_HEADS, ss, 0), (kt, GQA_KV, sk, 1)):
                        rb = r[:, 3, t * heads:(t + 1) * heads].rearrange("p (h o) -> p h o", o=1)
                        link(nc.vector.tensor_tensor(x, x, rb.to_broadcast([P, heads, HEAD]), ALU.mult))
                        gb = gain[:, g, :].rearrange("p (o d) -> p o d", o=1).to_broadcast([P, heads, HEAD])
                        link(nc.vector.tensor_tensor(x, x, gb, ALU.mult))
                        if t >= 2:
                            cos = core.c("cos")[:, (t - 2) * ROPE:(t - 1) * ROPE]
                            sin = core.c("sin")[:, (t - 2) * ROPE:(t - 1) * ROPE]
                            rotate(nc, link, x.rearrange("p h (r two) -> p h r two", two=2), tmp, cos, sin)
                    ins = nc.vector.tensor_copy(kdup[:, t], kt.rearrange("p g (o d) -> p g o d", o=1)
                                                .to_broadcast([P, GQA_KV, 2, HEAD]))
                    link(ins)
                nc.vector.engine_nop().then_inc(q_tile, 1)
                for n in range(0, len(items), 2):
                    dve.wait_ge(turned, n + 1)
                    kind, c = items[n]
                    nc.vector.tensor_copy((w.qbT if kind == "q" else w.kbT)[:, c, :], core.ps[:, n, :]).then_inc(taken[0], 1)

            @block.tensor
            def _(pe):
                pe.wait_ge(q_tile, 1)
                for n, (kind, c) in enumerate(items):
                    for t in range(TILES):
                        src = q[:, t, c * P:(c + 1) * P] if kind == "q" else \
                            kdup[:, t, c].rearrange("p u d -> p (u d)")
                        mm = nc.tensor.transpose(core.ps[:, n, t * P:(t + 1) * P], src, core.c("ident"))
                    mm.then_inc(turned, 1)


def attend_even(core, w):
    nc = core.nc
    with Stage(nc, "attn0") as st:
        p = st.sb("p", [P, 4, 512])
        pn = st.sb("pn", [P, 4, 512])
        pT = st.sb("pT", [P, 4, 4, CTX])
        mx = st.sb("mx", [P, 4, 4])
        scored, max_ready, exp_ready, recip_ready, norm_ready = (
            st.sem(n) for n in ("scored", "max_ready", "exp_ready", "recip_ready", "norm_ready"))
        turned, pT_ready, summed, out_done = st.sem("turned"), st.sem("pT_ready"), st.sem("summed"), st.sem("out_done")
        own = st.sem("own")
        items = [(h, s, i) for h in range(HEADS) for s in range(STREAMS) for i in range(2)]

        def keys(s):
            return CTX if s == 0 else CTX + LAT

        def operands(h):
            base = HEAD * (h % 2)
            if h < NA_HEADS:
                return base, w.qaT[:, h // 2], w.kaT[:, h // 2]
            j = h - NA_HEADS
            return base, w.qbT[:, j // 2], w.kbT[:, j // (GQA_HEADS // GQA_KV)]

        def values(h, kt):
            if h < NA_HEADS:
                return w.va[:, kt, h * HEAD:(h + 1) * HEAD]
            g = (h - NA_HEADS) // (GQA_HEADS // GQA_KV)
            return w.kvb[:, kt, (GQA_KV + g) * HEAD:(GQA_KV + g + 1) * HEAD]

        with nc.Block() as block:
            @block.tensor
            def _(pe):
                def score(n):
                    h, s, i = items[n]
                    t = 2 * s + i
                    base, qT, kT = operands(h)
                    if n >= 2:
                        pe.wait_ge(exp_ready, n - 1)
                    local = h < NA_HEADS and s == 1
                    mm = nc.tensor.matmul(core.ps[:, n % 2, 0:keys(s)], qT[base:base + HEAD, t * P:(t + 1) * P],
                                          kT[base:base + HEAD, 0:keys(s)], start=True, stop=not local,
                                          skip_group_check=True)
                    if local:
                        bias = w.bias[:, h, 2 - 2 * i:2 - 2 * i + NA_ROWS, :].rearrange("p u c -> p (u c)")
                        mm = nc.tensor.matmul(core.ps[:, n % 2, CTX:CTX + LAT], core.c("flip"), bias, start=False,
                                              stop=True, skip_group_check=True)
                    mm.then_inc(scored, 1)

                def turn(n):
                    h, s, i = items[n]
                    pe.wait_ge(norm_ready, n + 1)
                    if n >= 2:
                        pe.wait_ge(pT_ready, n - 1)
                    for kt in range(keys(s) // P):
                        mm = nc.tensor.transpose(core.ps[:, 2 + n % 2, kt * P:(kt + 1) * P],
                                                 pn[:, n % 4, kt * P:(kt + 1) * P], core.c("ident"))
                    mm.then_inc(turned, 1)

                def weigh(m):
                    h, s, _ = items[2 * m]
                    base = HEAD * (h % 2)
                    pe.wait_ge(pT_ready, 2 * m + 2)
                    if m >= 2:
                        pe.wait_ge(out_done, m - 1)
                    for kt in range(keys(s) // P):
                        mm = nc.tensor.matmul(core.ps[base:base + HEAD, 4 + m % 2, 0:CTX], values(h, kt),
                                              pT[:, m % 4, kt, :], start=kt == 0, stop=kt == keys(s) // P - 1)
                    mm.then_inc(summed, 1)

                N = len(items)
                for n in range(N + 6):
                    if n < N:
                        score(n)
                    if 3 <= n < N + 3:
                        turn(n - 3)
                    if n >= 6 and n % 2 == 1:
                        weigh((n - 6) // 2)
                weigh(N // 2 - 1) if (N + 5 - 6) // 2 < N // 2 - 1 else None

            @block.vector
            def _(dve):
                def take_max(n):
                    dve.wait_ge(scored, n + 1)
                    if n >= 4:
                        dve.wait_ge(norm_ready, n - 3)
                    nk = keys(items[n][1])
                    nc.vector.tensor_reduce(mx[:, n % 4, 0:1], core.ps[:, n % 2, 0:nk], AX, ALU.max).then_inc(own, 1)
                    dve.wait_ge(own, n + 1)
                    nc.vector.tensor_scalar(mx[:, n % 4, 1:2], mx[:, n % 4, 0:1], -1.0, None,
                                            ALU.mult).then_inc(max_ready, 1)

                def recip(n):
                    dve.wait_ge(exp_ready, n + 1)
                    nc.vector.reciprocal(mx[:, n % 4, 3:4], mx[:, n % 4, 2:3]).then_inc(recip_ready, 1)

                def take_turned(n):
                    nk = keys(items[n][1])
                    m = n // 2
                    dve.wait_ge(turned, n + 1)
                    if m >= 4:
                        dve.wait_ge(summed, m - 3)
                    nc.vector.tensor_copy(pT[:, m % 4, 0:nk // P, (n % 2) * P:(n % 2 + 1) * P],
                                          core.ps[:, 2 + n % 2, 0:nk].rearrange("p (k q) -> p k q", q=P)
                                          ).then_inc(pT_ready, 1)

                for n in range(len(items) + 3):
                    if n < len(items):
                        take_max(n)
                    if 1 <= n <= len(items):
                        recip(n - 1)
                    if n >= 3:
                        take_turned(n - 3)

            @block.scalar
            def _(act):
                def take_out(m):
                    h, s, _ = items[2 * m]
                    base = HEAD * (h % 2)
                    act.wait_ge(summed, m + 1)
                    nc.scalar.copy(w.oT[base:base + HEAD, h // 2, s * CTX:(s + 1) * CTX],
                                   core.ps[base:base + HEAD, 4 + m % 2, 0:CTX]).then_inc(out_done, 1)

                N = len(items)
                for n in range(N):
                    nk = keys(items[n][1])
                    act.wait_ge(max_ready, n + 1)
                    nc.scalar.activation(p[:, n % 4, 0:nk], core.ps[:, n % 2, 0:nk], ACT.Exp, bias=mx[:, n % 4, 1:2],
                                         accum_out=mx[:, n % 4, 2:3]).then_inc(exp_ready, 1)
                    if n >= 9 and n % 2 == 1:
                        take_out((n - 9) // 2)
                for m in range((N - 1 - 9) // 2 + 1, N // 2):
                    take_out(m)

            @block.gpsimd
            def _(pool):
                for n in range(len(items)):
                    nk = keys(items[n][1])
                    pool.wait_ge(recip_ready, n + 1)
                    if n >= 4:
                        pool.wait_ge(turned, n - 3)
                    nc.gpsimd.tensor_scalar(pn[:, n % 4, 0:nk], p[:, n % 4, 0:nk], mx[:, n % 4, 3:4], None,
                                            ALU.mult).then_inc(norm_ready, 1)


def project_out(core, a, layer, which_w, w, tiles, oT_at):
    nc = core.nc
    streams = sorted({t // 2 for t in tiles})
    with Stage(nc, f"out{layer}") as st:
        wo = st.sb("wo", [P, 2, KD, 512])
        diag = st.sb("diag", [P, len(streams), KD, P])
        grow = st.sb("grow", [P, len(streams), D])
        prod = st.sb("prod", [P, 2, 512])
        loaded = [st.sem("loaded0"), st.sem("loaded1")]
        diag_ready, spread, gates_ready = st.sem("diag_ready"), st.sem("spread"), st.sem("gates_ready")
        summed, added, own = st.sem("summed"), st.sem("added"), st.sem("own")
        w_view = a[which_w].rearrange("o (k p) n -> p (o k) n", p=P)
        items = [(half, t) for half in range(2) for t in tiles]
        with nc.Block() as block:
            @block.sync
            def _(sp):
                for half in range(2):
                    sp.dma_start(wo[:, half], w_view[:, :, half * 512:(half + 1) * 512]).then_inc(loaded[half], 16)

            @block.tensor
            def _(pe):
                for i, s in enumerate(streams):
                    pe.wait_ge(diag_ready, i + 1)
                    for half in range(2):
                        for k in range(4):
                            mm = nc.tensor.matmul(core.ps[:, 6 + half, k * P:(k + 1) * P], core.c("ones"),
                                                  diag[:, i, 4 * half + k, :], start=True, stop=True)
                    mm.then_inc(spread, 1)
                    pe.wait_ge(gates_ready, i + 1)
                for n, (half, t) in enumerate(items):
                    pe.wait_ge(loaded[half], 16)
                    if n >= 6:
                        pe.wait_ge(added, n - 5)
                    for k in range(KD):
                        mm = nc.tensor.matmul(core.ps[:, n % 6, :], w.oT[:, k, oT_at(t)], wo[:, half, k, :],
                                              start=k == 0, stop=k == KD - 1)
                    mm.then_inc(summed, 1)

            @block.vector
            def _(dve):
                for i, s in enumerate(streams):
                    for k in range(KD):
                        ins = nc.vector.tensor_scalar(diag[:, i, k, :], core.c("ident"),
                                                      core.gate_column(layer, 0, s, k), None, ALU.mult)
                    ins.then_inc(diag_ready, 1)
                for i, s in enumerate(streams):
                    dve.wait_ge(spread, i + 1)
                    nc.vector.tensor_copy(grow[:, i, :].rearrange("p (h c) -> p h c", h=2),
                                          core.ps[:, 6:8, :]).then_inc(gates_ready, 1)
                for n, (half, t) in enumerate(items):
                    dve.wait_ge(summed, n + 1)
                    dve.wait_ge(gates_ready, len(streams))
                    cols = slice(half * 512, (half + 1) * 512)
                    nc.vector.tensor_tensor(prod[:, n % 2, :], core.ps[:, n % 6, :],
                                            grow[:, streams.index(t // 2), cols], ALU.mult).then_inc(own, 1)
                    dve.wait_ge(own, n + 1)
                    nc.vector.tensor_tensor(core.x[:, t, cols], core.x[:, t, cols], prod[:, n % 2, :],
                                            ALU.add).then_inc(added, 1)


class EvenBuffers:

    def __init__(self, nc, stack):
        def sb(name, shape):
            return stack.enter_context(nc.sbuf_tensor(name, shape, F32))

        self.qaT, self.kaT = sb("qaT", [P, 4, 512]), sb("kaT", [P, 4, 512])
        self.va, self.qb = sb("va", [P, TILES, 512]), sb("qb", [P, TILES, 512])
        self.kvb = sb("kvb", [P, TILES, 2 * GQA_KV * HEAD])
        self.qbT, self.kbT = sb("qbT", [P, 4, 512]), sb("kbT", [P, GQA_KV, 512])
        self.bias = sb("na_bias", [P, NA_HEADS, REL, GRID_W])
        self.oT = sb("oT", [P, KD, 512])
        self.rpb_rows = nc.dram_tensor("rpb_rows", (NA_HEADS * (2 * WIN_ROWS - 1), P), F32, kind="Internal").ap()


def layer_even(core, a):
    with ExitStack() as stack:
        w = EvenBuffers(core.nc, stack)
        norm_transpose(core, 0, 0, [0, 1])
        project_even(core, a, w)
        qk_norm_rope(core, a, w)
        attend_even(core, w)
        project_out(core, a, 0, "ab_w_out", w, list(range(TILES)), lambda t: slice(t * P, (t + 1) * P))


def route(core, a, r, layer, tiles):
    nc = core.nc
    NT, t0 = len(tiles), tiles[0]
    with Stage(nc, f"route{layer}") as st:
        hrow = st.sb("hrow", [P, NT, D])
        rw = st.sb("rw", [P, KD, E])
        wgu = st.sb("wgu", [P, KD, 2, F])
        wd = st.sb("wd", [P, KF, D])
        bias = st.sb("bias", [P, E])
        score, picked, mask, gate = (st.sb(n, [P, NT, E]) for n in ("score", "picked", "mask", "gate"))
        work = st.sb("work", [P, NT, E])
        top = st.sb("top", [P, NT, 8])
        tot = st.sb("tot", [P, 2, NT])
        part = st.sb("part", [P, NT, E], BF16)
        cnt = st.sb("cnt", [P, 2])
        sg, hid = st.sb("sg", [P, 2, F]), st.sb("hid", [P, 2, F])
        hidT = st.sb("hidT", [P, 2, KF, P])
        rw_in, bias_in, wgu_in, wd_in = (st.sem(n) for n in ("rw_in", "bias_in", "wgu_in", "wd_in"))
        logits, e_ready, mask_ready, placed, counted = (
            st.sem(n) for n in ("logits", "e_ready", "mask_ready", "placed", "counted"))
        turned, taken, rows_out = st.sem("turned"), [st.sem("taken_dve"), st.sem("taken_act")], st.sem("rows_out")
        gu_ready, silu_ready, hid_ready = st.sem("gu_ready"), st.sem("silu_ready"), st.sem("hid_ready")
        hidT_turned, hidT_ready, down_ready = st.sem("hidT_turned"), st.sem("hidT_ready"), st.sem("down_ready")
        down_taken, own, parts_ready = st.sem("down_taken"), st.sem("own"), st.sem("parts_ready")
        back = [(i, half) for i in range(NT) for half in range(2)]
        with nc.Block() as block:
            @block.sync
            def _(sp):
                sp.dma_start(rw[:], a["router_w"][layer].rearrange("(k p) e -> p k e", p=P)).then_inc(rw_in, 16)
                sp.dma_start(bias[:], a["router_bias"][layer:layer + 1, :].to_broadcast([P, E])).then_inc(bias_in, 16)
                sp.dma_start(wgu[:, :, 0, :], a["shared_w_gate"][layer].rearrange("(k p) f -> p k f", p=P)).then_inc(wgu_in, 16)
                sp.dma_start(wgu[:, :, 1, :], a["shared_w_up"][layer].rearrange("(k p) f -> p k f", p=P)).then_inc(wgu_in, 16)
                sp.dma_start(wd[:], a["shared_w_down"][layer].rearrange("(k p) d -> p k d", p=P)).then_inc(wd_in, 16)
                for i in range(NT):
                    sp.wait_ge(taken[0], i + 1)
                    sp.wait_ge(taken[1], i + 1)
                    sp.dma_start(r.h_rows[i * P:(i + 1) * P, :], hrow[:, i, :]).then_inc(rows_out, 16)
                sp.wait_ge(rows_out, 16 * NT)

            @block.tensor
            def _(pe):
                def h(k, i):
                    return core.hT[:, k, (t0 + i) * P:(t0 + i + 1) * P]

                pe.wait_ge(rw_in, 16)
                for i in range(NT):
                    for k in range(KD):
                        mm = nc.tensor.matmul(core.ps[:, 0, i * E:(i + 1) * E], h(k, i), rw[:, k, :],
                                              start=k == 0, stop=k == KD - 1)
                mm.then_inc(logits, 1)
                for n, (i, half) in enumerate(back):
                    if n >= 2:
                        pe.wait_ge(taken[n % 2], (n - 2) // 2 + 1)
                    for k in range(4):
                        mm = nc.tensor.transpose(core.ps[:, 1 + n % 2, k * P:(k + 1) * P], h(4 * half + k, i),
                                                 core.c("ident"))
                    mm.then_inc(turned, 1)

                def gate_up(i):
                    pe.wait_ge(wgu_in, 32)
                    if i >= 1:
                        pe.wait_ge(hid_ready, i)
                    for k in range(KD):
                        mm = nc.tensor.matmul(core.ps[:, 4, :], h(k, i), wgu[:, k].rearrange("p g f -> p (g f)"),
                                              start=k == 0, stop=k == KD - 1)
                    mm.then_inc(gu_ready, 1)

                def down(i):
                    pe.wait_ge(hid_ready, i + 1)
                    if i >= 1:
                        pe.wait_ge(hidT_ready, i)
                    for k in range(KF):
                        mm = nc.tensor.transpose(core.ps[:, 5, k * P:(k + 1) * P], hid[:, i % 2, k * P:(k + 1) * P],
                                                 core.c("ident"))
                    mm.then_inc(hidT_turned, 1)
                    pe.wait_ge(hidT_ready, i + 1)
                    pe.wait_ge(wd_in, 16)
                    if i >= 1:
                        pe.wait_ge(down_taken, i)
                    for half in range(2):
                        for k in range(KF):
                            mm = nc.tensor.matmul(core.ps[:, 6 + half, :], hidT[:, i % 2, k, :],
                                                  wd[:, k, half * 512:(half + 1) * 512], start=k == 0, stop=k == KF - 1)
                    mm.then_inc(down_ready, 1)

                for i in range(NT):
                    gate_up(i)
                    if i == 0:
                        pe.wait_ge(mask_ready, 1)
                        for i2 in range(NT):
                            for j in range(i2 + 1):
                                mm = nc.tensor.matmul(core.ps[:, 3, i2 * E:(i2 + 1) * E],
                                                      core.c("before") if j == i2 else core.c("ones"), mask[:, j, :],
                                                      start=j == 0, stop=j == i2)
                        mm.then_inc(placed, 1)
                        for j in range(NT):
                            mm = nc.tensor.matmul(core.ps[:, 0, 0:E], core.c("ones"), mask[:, j, :], start=j == 0,
                                                  stop=j == NT - 1)
                        mm.then_inc(counted, 1)
                    down(i)

            @block.scalar
            def _(act):
                act.wait_ge(logits, 1)
                nc.scalar.activation(score[:].rearrange("p t e -> p (t e)"), core.ps[:, 0, 0:NT * E], ACT.Exp,
                                     scale=-1.0).then_inc(e_ready, 1)
                for i in range(NT):
                    act.wait_ge(turned, 2 * i + 2)
                    nc.scalar.copy(hrow[:, i, 512:D], core.ps[:, 2, :]).then_inc(taken[1], 1)
                for i in range(NT):
                    act.wait_ge(gu_ready, i + 1)
                    nc.scalar.activation(sg[:, i % 2, :], core.ps[:, 4, 0:F], ACT.Silu).then_inc(silu_ready, 1)

            @block.vector
            def _(dve):
                link = Chain(dve, own)
                dve.wait_ge(e_ready, 1)
                link(nc.vector.tensor_scalar(score[:], score[:], 1.0, None, ALU.add))
                link(nc.vector.reciprocal(score[:], score[:]))
                dve.wait_ge(bias_in, 16)
                link(nc.vector.tensor_tensor(picked[:], score[:], bias[:].rearrange("p (o e) -> p o e", o=1)
                                             .to_broadcast([P, NT, E]), ALU.add))
                for i in range(NT):
                    ins = nc.vector.max(top[:, i, :], picked[:, i, :])
                link(ins)
                for i in range(NT):
                    ins = nc.vector.match_replace(work[:, i, :], top[:, i, :], picked[:, i, :], MASKED)
                link(ins)
                nc.vector.tensor_tensor(mask[:], picked[:], work[:], ALU.not_equal).then_inc(mask_ready, 1)
                dve.wait_ge(mask_ready, 1)
                link(nc.vector.tensor_tensor(gate[:], score[:], mask[:], ALU.mult))
                link(nc.vector.tensor_reduce(tot[:, 0, :], gate[:], AX, ALU.add))
                link(nc.vector.reciprocal(tot[:, 1, :], tot[:, 0, :]))
                link(nc.vector.tensor_tensor(gate[:], gate[:], tot[:, 1, :].rearrange("p (t o) -> p t o", o=1)
                                             .to_broadcast([P, NT, E]), ALU.mult))
                link(nc.vector.tensor_scalar(gate[:], gate[:], ROUTED_SCALE, None, ALU.mult))
                for i in range(NT):
                    dve.wait_ge(turned, 2 * i + 1)
                    nc.vector.tensor_copy(hrow[:, i, 0:512], core.ps[:, 1, :]).then_inc(taken[0], 1)

                def hidden(i):
                    dve.wait_ge(silu_ready, i + 1)
                    nc.vector.tensor_tensor(hid[:, i % 2, :], sg[:, i % 2, :], core.ps[:, 4, F:2 * F],
                                            ALU.mult).then_inc(hid_ready, 1)
                    dve.wait_ge(hidT_turned, i + 1)
                    nc.vector.tensor_copy(hidT[:, i % 2].rearrange("p k c -> p (k c)"),
                                          core.ps[:, 5, 0:F]).then_inc(hidT_ready, 1)
                    dve.wait_ge(down_ready, i + 1)
                    nc.vector.tensor_copy(r.shared[:, i, :].rearrange("p (h c) -> p h c", h=2),
                                          core.ps[:, 6:8, :]).then_inc(down_taken, 1)

                dve.wait_ge(placed, 1)
                pos = core.ps[:, 3, 0:NT * E].rearrange("p (t e) -> p t e", e=E)
                link(nc.vector.scalar_tensor_tensor(out=work[:], in0=pos, scalar=1.0, in1=mask[:], op0=ALU.add,
                                                    op1=ALU.mult))
                link(nc.vector.tensor_scalar(r.place[:], work[:], -1.0, None, ALU.add))
                dve.wait_ge(counted, 1)
                link(nc.vector.tensor_reduce(cnt[:, 0:1], core.ps[:, 0, 0:E], AX, ALU.max))
                link(nc.vector.tensor_copy(r.longest[:], cnt[:, 0:1]))
                for i in range(NT):
                    ins = nc.vector.tensor_tensor_scan(work[:, i, :], core.c("ones")[:, 0:E], mask[:, i, :], 0.0,
                                                       ALU.mult, ALU.add)
                link(ins)
                info = r.slot_info
                nc.vector.tensor_scalar(info[:, :, :, 2, 2], work[:], -1.0, None, ALU.add)
                link(nc.vector.tensor_copy(info[:, :, :, 0, 0], gate[:]))
                link(nc.vector.tensor_tensor(gate[:], gate[:], info[:, :, :, 0, 0], ALU.subtract))
                link(nc.vector.tensor_copy(info[:, :, :, 0, 1], gate[:]))
                link(nc.vector.tensor_tensor(gate[:], gate[:], info[:, :, :, 0, 1], ALU.subtract))
                link(nc.vector.tensor_copy(info[:, :, :, 0, 2], gate[:]))
                nc.vector.memset(info[:, :, :, 1, 2], 0.0)
                for i in range(NT):
                    for c, name in ((1, "tok"), (2, "dest")):
                        for s, v in ((0, core.c(name + "_hi")[:, i:i + 1]), (1, core.c(name + "_lo"))):
                            ins = nc.vector.tensor_copy(info[:, i, :, c, s], v.to_broadcast([P, E]))
                link(ins)
                for i in range(NT):
                    hidden(i)


class Routing:

    def __init__(self, core, stack, layer, NT):
        nc = core.nc

        def sb(name, shape, dt=F32):
            return stack.enter_context(nc.sbuf_tensor(f"{name}{layer}", shape, dt))

        self.place = sb("place", [P, NT, E])
        self.slot_info = sb("slot_info", [P, NT, E, 3, 3], BF16)
        self.shared = sb("shared", [P, NT, D])
        self.longest = sb("longest", [P, 1], I32)
        self.h_rows = nc.dram_tensor(f"h_rows{layer}", (NT * P, D), F32, kind="Internal").ap()
        self.y_rows = nc.dram_tensor(f"y_rows{layer}", (NT * P * TOP_K, D), F32, kind="Internal").ap()


RING = 4
GROUP = 8
GROUPS = E // GROUP


def experts(core, a, r, layer, tiles):
    nc = core.nc
    NT = len(tiles)
    T = NT * P
    with Stage(nc, f"moe{layer}") as st:
        wgu = st.sb("wgu", [P, RING, 2, KD * F])
        wd = st.sb("wd", [P, RING, KF * D])
        onehot = st.sb("onehot", [P, 2, NT, SLOTS], BF16)
        info = st.sb("info", [P, GROUP, 3])
        index = st.sb("index", [P, GROUP, 2], I32)
        xs = st.sb("xs", [P, RING, D])
        xT = st.sb("xT", [P, 2, KD, SLOTS])
        sg, hid = st.sb("sg", [P, 2, F]), st.sb("hid", [P, 2, F])
        hidT = st.sb("hidT", [P, 2, KF, SLOTS])
        y = st.sb("y", [P, 2, D])
        w_in = [st.sem(f"w_in{i}") for i in range(RING)]
        gathered = [st.pool_sem(f"gathered{i}") for i in range(RING)]
        scattered = [st.pool_sem(f"scattered{i}") for i in range(2)]
        cleared, gathers, scatters = st.sem("cleared"), st.sem("gathers"), st.sem("scatters")
        hot_ready, info_sum, info_ready, index_ready = (
            st.sem(n) for n in ("hot_ready", "info_sum", "info_ready", "index_ready"))
        x_turned, xT_dve, xT_act = st.sem("x_turned"), st.sem("xT_dve"), st.sem("xT_act")
        gu_ready, silu_ready, hid_ready = st.sem("gu_ready"), st.sem("silu_ready"), st.sem("hid_ready")
        hid_turned, hidT_ready, down_ready = st.sem("hid_turned"), st.sem("hidT_ready"), st.sem("down_ready")
        y_dve, y_act = st.sem("y_dve"), st.sem("y_act")

        def grouped(t):
            return t[layer].rearrange("(g s) (p k) f -> s g p (k f)", s=GROUP, p=P)

        w_src = [(grouped(a["expert_w_gate"]), 0), (grouped(a["expert_w_up"]), 1), (grouped(a["expert_w_down"]), 2)]

        bounds = []

        def sp_step(sp, g, s, base, first):
            if not first:
                sp.wait_ge(down_ready, base + GROUP * g + s - RING + 1)
            for src, i in w_src:
                v = src[s, g] if isinstance(g, int) else src[s, bass.ds(g, 1)].rearrange("o p n -> (o p) n")
                sp.dma_start(wd[:, s % RING, :] if i == 2 else wgu[:, s % RING, i, :], v).then_inc(w_in[s % RING], 16)

        def pool_gather(pool, g, s, base, first):
            n = base + GROUP * g + s
            if not first:
                pool.wait_ge(x_turned, n - RING + 1)
            pool.wait_ge(index_ready, n + 1)
            pool.sem_inc(gathers, 1)
            pool.indirect_dma_start(out=xs[:, s % RING, :], out_offset=None, in_=r.h_rows,
                                    in_offset=bass.IndirectOffsetOnAxis(ap=index[:, s, 0:1], axis=0),
                                    bounds_check=bounds[0], oob_is_err=False).then_inc(gathered[s % RING], 16)

        def pool_scatter(pool, g, s, base):
            n = base + GROUP * g + s
            pool.wait_ge(y_dve, n + 1)
            pool.wait_ge(y_act, n + 1)
            pool.sem_inc(scatters, 1)
            pool.indirect_dma_start(out=r.y_rows, out_offset=bass.IndirectOffsetOnAxis(ap=index[:, s, 1:2], axis=0),
                                    in_=y[:, s % 2, :], in_offset=None, bounds_check=bounds[1],
                                    oob_is_err=False).then_inc(scattered[s % 2], 16)

        def dve_hot(dve, g, s, base, block_at, first):
            n = base + GROUP * g + s
            if not first:
                dve.wait_ge(info_sum, n - 1)
            iota = core.c("iota")
            slots = iota[:, block_at * SLOTS:(block_at + 1) * SLOTS] if isinstance(block_at, int) else \
                iota[:, bass.ds(block_at * SLOTS, SLOTS)]
            e = GROUP * g + s
            for i in range(NT):
                where = r.place[:, i, e:e + 1] if isinstance(g, int) else r.place[:, i, bass.ds(e, 1)]
                ins = nc.vector.tensor_scalar(onehot[:, s % 2, i, :], slots, where, None, ALU.is_equal)
            ins.then_inc(hot_ready, 1)

        def pe_info(pe, g, s, base, first):
            n = base + GROUP * g + s
            pe.wait_ge(hot_ready, n + 1)
            if not first:
                pe.wait_ge(info_ready, n)
            flat = r.slot_info[:].rearrange("p t e c s -> p t (e c s)")
            for i in range(NT):
                at = 9 * (GROUP * g + s)
                rhs = flat[:, i, at:at + 9] if isinstance(g, int) else flat[:, i, bass.ds(at, 9)]
                mm = nc.tensor.matmul(core.ps[:, 7, 0:9], onehot[:, s % 2, i, :], rhs, start=i == 0, stop=i == NT - 1)
            mm.then_inc(info_sum, 1)

        def dve_info(dve, g, s, base, first):
            n = base + GROUP * g + s
            dve.wait_ge(info_sum, n + 1)
            if not first:
                dve.wait_ge(scattered[s % 2], 8 * (base + GROUP * g) + 16 * (s // 2) + 16 - 8 * GROUP)
            nc.vector.tensor_reduce(info[:, s, :], core.ps[:, 7, 0:9].rearrange("p (c s) -> p c s", s=3), AX,
                                    ALU.add).then_inc(info_ready, 1)
            dve.wait_ge(info_ready, n + 1)
            nc.vector.tensor_scalar(index[:, s, :], info[:, s, 1:3], float(BIG), None, ALU.add).then_inc(index_ready, 1)

        def pe_turn(pe, g, s, base, first):
            n = base + GROUP * g + s
            pe.wait_ge(gathered[s % RING], 4 * (base + GROUP * g) + 16 * (s // RING) + 16)
            if not first:
                pe.wait_ge(xT_dve, n)
                pe.wait_ge(xT_act, n)
            for k in range(KD):
                mm = nc.tensor.transpose(core.ps[:, 4 + k // 4, (k % 4) * P:(k % 4 + 1) * P],
                                         xs[:, s % RING, k:D:KD], core.c("ident"))
            mm.then_inc(x_turned, 1)

        def take_x(eng, bank, g, s, base, first):
            n = base + GROUP * g + s
            eng.wait_ge(x_turned, n + 1)
            if not first:
                eng.wait_ge(gu_ready, n - 1)
            out = xT[:, s % 2, 4 * bank:4 * bank + 4, :].rearrange("p k c -> p (k c)")
            if bank == 0:
                nc.vector.tensor_copy(out, core.ps[:, 4, :]).then_inc(xT_dve, 1)
            else:
                nc.scalar.copy(out, core.ps[:, 5, :]).then_inc(xT_act, 1)

        def pe_gate_up(pe, g, s, base, first):
            n = base + GROUP * g + s
            pe.wait_ge(w_in[s % RING], 12 * (base + GROUP * g) + 48 * (s // RING) + 48)
            pe.wait_ge(xT_dve, n + 1)
            pe.wait_ge(xT_act, n + 1)
            if not first:
                pe.wait_ge(hid_ready, n - 1)
            w = wgu[:, s % RING].rearrange("p i (k f) -> p k i f", f=F)
            for k in range(KD):
                mm = nc.tensor.matmul(core.ps[:, s % 2, :], xT[:, s % 2, k, :], w[:, k], start=k == 0,
                                      stop=k == KD - 1)
            mm.then_inc(gu_ready, 1)

        def act_silu(act, g, s, base, first):
            n = base + GROUP * g + s
            act.wait_ge(gu_ready, n + 1)
            if not first:
                act.wait_ge(hid_ready, n - 1)
            nc.scalar.activation(sg[:, s % 2, :], core.ps[:, s % 2, 0:F], ACT.Silu).then_inc(silu_ready, 1)

        def dve_hidden(dve, g, s, base, first):
            n = base + GROUP * g + s
            dve.wait_ge(silu_ready, n + 1)
            if not first:
                dve.wait_ge(hid_turned, n - 1)
            nc.vector.tensor_tensor(hid[:, s % 2, :], sg[:, s % 2, :], core.ps[:, s % 2, F:2 * F],
                                    ALU.mult).then_inc(hid_ready, 1)

        def pe_turn_hidden(pe, g, s, base, first):
            n = base + GROUP * g + s
            pe.wait_ge(hid_ready, n + 1)
            if not first:
                pe.wait_ge(hidT_ready, n)
            for k in range(KF):
                mm = nc.tensor.transpose(core.ps[:, 6, k * P:(k + 1) * P], hid[:, s % 2, k:F:KF], core.c("ident"))
            mm.then_inc(hid_turned, 1)

        def dve_take_hidden(dve, g, s, base, first):
            n = base + GROUP * g + s
            dve.wait_ge(hid_turned, n + 1)
            if not first:
                dve.wait_ge(down_ready, n - 1)
            nc.vector.tensor_copy(hidT[:, s % 2].rearrange("p k c -> p (k c)"), core.ps[:, 6, 0:F]).then_inc(hidT_ready, 1)

        def pe_down(pe, g, s, base, first):
            n = base + GROUP * g + s
            pe.wait_ge(hidT_ready, n + 1)
            if not first:
                pe.wait_ge(y_dve, n)
                pe.wait_ge(y_act, n)
            for half in range(2):
                for k in range(KF):
                    mm = nc.tensor.matmul(core.ps[:, 2 + half, :], hidT[:, s % 2, k, :],
                                          wd[:, s % RING, k * D + half * 512:k * D + half * 512 + 512], start=k == 0,
                                          stop=k == KF - 1)
            mm.then_inc(down_ready, 1)

        def take_y(eng, half, g, s, base, first):
            n = base + GROUP * g + s
            eng.wait_ge(down_ready, n + 1)
            if not first:
                eng.wait_ge(scattered[s % 2], 8 * (base + GROUP * g) + 16 * (s // 2))
            out, src, gate = y[:, s % 2, half * 512:(half + 1) * 512], core.ps[:, 2 + half, :], info[:, s, 0:1]
            if half == 0:
                nc.vector.tensor_scalar(out, src, gate, None, ALU.mult).then_inc(y_dve, 1)
            else:
                nc.scalar.activation(out, src, ACT.Copy, scale=gate).then_inc(y_act, 1)

        def at(g, s, ahead):
            return g + (s + ahead) // GROUP, (s + ahead) % GROUP

        def run(eng, step):
            for s in range(GROUP):
                step(0, s, s)
            with eng.Fori(1, GROUPS - 1) as g:
                for s in range(GROUP):
                    step(g, s, None)
            for s in range(GROUP):
                step(GROUPS - 1, s, E - GROUP + s)

        def inside(e, ahead):
            return e is None or 0 <= e + ahead < E

        def early(e, ahead, ring, base_is_zero):
            return base_is_zero and e is not None and e + ahead < ring

        def sp_pass(sp, base, z):
            def step(g, s, e):
                sp_step(sp, g, s, base, early(e, 0, RING, z))
            run(sp, step)

        def pool_pass(pool, base, z):
            for e in range(2):
                pool_gather(pool, 0, e, base, early(e, 0, RING, z))

            def step(g, s, e):
                if inside(e, 2):
                    pool_gather(pool, *at(g, s, 2), base, early(e, 2, RING, z))
                if inside(e, -2):
                    pool_scatter(pool, *at(g, s, -2), base)
            run(pool, step)
            for s in range(GROUP - 2, GROUP):
                pool_scatter(pool, GROUPS - 1, s, base)

        def dve_pass(dve, base, z, blk):
            def hot(e, g, s):
                dve_hot(dve, g, s, base, blk, early(e, 0, 2, z))

            def slots(e, g, s):
                dve_info(dve, g, s, base, early(e, 0, GROUP, z))

            for e in range(2):
                hot(e, 0, e)
                slots(e, 0, e)
            hot(2, 0, 2)
            take_x(dve, 0, 0, 0, base, z)

            def step(g, s, e):
                up = (lambda k: None) if e is None else (lambda k: e + k)
                if inside(e, 2):
                    slots(up(2), *at(g, s, 2))
                if inside(e, 3):
                    hot(up(3), *at(g, s, 3))
                if inside(e, 1):
                    take_x(dve, 0, *at(g, s, 1), base, early(e, 1, 2, z))
                dve_hidden(dve, g, s, base, early(e, 0, 2, z))
                if inside(e, -1):
                    take_y(dve, 0, *at(g, s, -1), base, early(e, -1, 2, z))
                dve_take_hidden(dve, g, s, base, early(e, 0, 2, z))
            run(dve, step)
            take_y(dve, 0, GROUPS - 1, GROUP - 1, base, False)

        def act_pass(act, base, z):
            take_x(act, 1, 0, 0, base, z)

            def step(g, s, e):
                if inside(e, 1):
                    take_x(act, 1, *at(g, s, 1), base, early(e, 1, 2, z))
                act_silu(act, g, s, base, early(e, 0, 2, z))
                if inside(e, -1):
                    take_y(act, 1, *at(g, s, -1), base, early(e, -1, 2, z))
            run(act, step)
            take_y(act, 1, GROUPS - 1, GROUP - 1, base, False)

        def pe_pass(pe, base, z):
            for e in range(2):
                pe_info(pe, 0, e, base, early(e, 0, 1, z))
            pe_turn(pe, 0, 0, base, z)

            def step(g, s, e):
                if inside(e, 2):
                    pe_info(pe, *at(g, s, 2), base, early(e, 2, 1, z))
                if inside(e, 1):
                    pe_turn(pe, *at(g, s, 1), base, early(e, 1, 1, z))
                pe_gate_up(pe, g, s, base, early(e, 0, 2, z))
                if inside(e, -1):
                    pe_down(pe, *at(g, s, -1), base, early(e, -1, 1, z))
                pe_turn_hidden(pe, g, s, base, early(e, 0, 1, z))
            run(pe, step)
            pe_down(pe, GROUPS - 1, GROUP - 1, base, False)

        def further(eng, body):
            longest = eng.value_load(r.longest[0:1, 0:1], min_val=0, max_val=T)
            with eng.If(longest > SLOTS):
                with eng.Fori(1, T // SLOTS) as b:
                    body(b * E, b)

        with nc.Block() as block:
            @block.sync
            def _(sp):
                sp_pass(sp, 0, True)
                further(sp, lambda base, b: sp_pass(sp, base, False))

            @block.gpsimd
            def _(pool):
                last_row, last_out = pool.to_reg(T - 1), pool.to_reg(T * TOP_K - 1)
                bounds[:] = [last_row, last_out]
                pool.wait_ge(cleared, 1)
                pool_pass(pool, 0, True)
                further(pool, lambda base, b: pool_pass(pool, base, False))
                for i in range(2):
                    pool.wait_ge(scattered[i], 16 * (E // 2))

            @block.scalar
            def _(act):
                act_pass(act, 0, True)
                further(act, lambda base, b: act_pass(act, base, False))

            @block.vector
            def _(dve):
                nc.vector.memset(xs[:], 0.0).then_inc(cleared, 1)
                dve_pass(dve, 0, True, 0)
                further(dve, lambda base, b: dve_pass(dve, base, False, b))

            @block.tensor
            def _(pe):
                pe_pass(pe, 0, True)
                further(pe, lambda base, b: pe_pass(pe, base, False))


def combine(core, r, layer, tiles):
    nc = core.nc
    streams = sorted({t // 2 for t in tiles})
    with Stage(nc, f"combine{layer}") as st:
        yr = st.sb("yr", [P, 2, TOP_K, D])
        diag = st.sb("diag", [P, KD, P])
        grow = st.sb("grow", [P, len(streams), D])
        y_in = [st.sem("y_in0"), st.sem("y_in1")]
        diag_ready, spread, gates_ready = st.sem("diag_ready"), st.sem("spread"), st.sem("gates_ready")
        own, summed, pool_own, pool_summed = st.sem("own"), st.sem("summed"), st.sem("pool_own"), st.sem("pool_summed")
        y_view = r.y_rows.rearrange("(t p k) d -> t p k d", p=P, k=TOP_K)
        with nc.Block() as block:
            @block.sync
            def _(sp):
                for i in range(len(tiles)):
                    if i >= 2:
                        sp.wait_ge(summed, i - 1)
                    sp.dma_start(yr[:, i % 2], y_view[i]).then_inc(y_in[i % 2], 16)

            @block.tensor
            def _(pe):
                for i in range(len(streams)):
                    pe.wait_ge(diag_ready, i + 1)
                    if i >= 1:
                        pe.wait_ge(gates_ready, i)
                    for k in range(KD):
                        mm = nc.tensor.matmul(core.ps[:, k // 4, (k % 4) * P:(k % 4 + 1) * P], core.c("ones"),
                                              diag[:, k, :], start=True, stop=True)
                    mm.then_inc(spread, 1)

            @block.gpsimd
            def _(pool):
                link = Chain(pool, pool_own)
                for i in range(len(tiles)):
                    pool.wait_ge(y_in[i % 2], 16 * (i // 2 + 1))
                    v = yr[:, i % 2]
                    link(nc.gpsimd.tensor_tensor(v[:, 0], v[:, 0], v[:, 1], ALU.add))
                    nc.gpsimd.tensor_tensor(v[:, 0], v[:, 0], v[:, 2], ALU.add).then_inc(pool_summed, 1)

            @block.vector
            def _(dve):
                link = Chain(dve, own)
                for i, s in enumerate(streams):
                    if i >= 1:
                        dve.wait_ge(spread, i)
                    for k in range(KD):
                        ins = nc.vector.tensor_scalar(diag[:, k, :], core.c("ident"), core.gate_column(layer, 1, s, k),
                                                      None, ALU.mult)
                    ins.then_inc(diag_ready, 1)
                    dve.wait_ge(spread, i + 1)
                    nc.vector.tensor_copy(grow[:, i, :].rearrange("p (h c) -> p h c", h=2),
                                          core.ps[:, 0:2, :]).then_inc(gates_ready, 1)
                for i, t in enumerate(tiles):
                    dve.wait_ge(y_in[i % 2], 16 * (i // 2 + 1))
                    v = yr[:, i % 2]
                    link(nc.vector.tensor_tensor(v[:, 4:6], v[:, 4:6], v[:, 6:8], ALU.add))
                    nc.vector.tensor_tensor(v[:, 3], v[:, 3], r.shared[:, i, :], ALU.add)
                    link(nc.vector.tensor_tensor(v[:, 4], v[:, 4], v[:, 5], ALU.add))
                    link(nc.vector.tensor_tensor(v[:, 3], v[:, 3], v[:, 4], ALU.add))
                    dve.wait_ge(pool_summed, i + 1)
                    link(nc.vector.tensor_tensor(v[:, 3], v[:, 3], v[:, 0], ALU.add))
                    if i == 0:
                        dve.wait_ge(gates_ready, len(streams))
                    link(nc.vector.tensor_tensor(v[:, 3], v[:, 3], grow[:, streams.index(t // 2), :], ALU.mult))
                    nc.vector.tensor_tensor(core.x[:, t, :], core.x[:, t, :], v[:, 3], ALU.add).then_inc(summed, 1)


def moe(core, a, layer, tiles):
    norm_transpose(core, layer, 1, sorted({t // 2 for t in tiles}))
    with ExitStack() as stack:
        r = Routing(core, stack, layer, len(tiles))
        route(core, a, r, layer, tiles)
        experts(core, a, r, layer, tiles)
        combine(core, r, layer, tiles)


def project_odd(core, a, w):
    nc = core.nc
    COLS = 512
    RING = 3
    with Stage(nc, "proj1") as st:
        wb = st.sb("w", [P, RING, KD, COLS])
        loaded = [st.sem(f"loaded{i}") for i in range(RING)]
        summed, taken = st.sem("summed"), [st.sem("taken_dve"), st.sem("taken_act")]
        w_view = a["diff_w_in"].rearrange("o (k p) n -> p (o k) n", p=P)
        blocks = 3 * D // COLS
        items = [(b, t) for b in range(blocks) for t in (range(2, TILES) if b < 2 else range(TILES))]

        def target(b, t):
            cols = slice((b % 2) * COLS, (b % 2 + 1) * COLS)
            return w.q[:, t - 2, cols] if b < 2 else (w.k if b < 4 else w.v)[:, t, cols]

        with nc.Block() as block:
            @block.sync
            def _(sp):
                for b in range(blocks):
                    if b >= RING:
                        sp.wait_ge(summed, sum(1 for x, _ in items if x <= b - RING))
                    sp.dma_start(wb[:, b % RING], w_view[:, :, b * COLS:(b + 1) * COLS]).then_inc(loaded[b % RING], 16)

            @block.tensor
            def _(pe):
                for n, (b, t) in enumerate(items):
                    pe.wait_ge(loaded[b % RING], 16 * (b // RING + 1))
                    if n >= 8:
                        pe.wait_ge(taken[n % 2], (n - 8) // 2 + 1)
                    for k in range(KD):
                        mm = nc.tensor.matmul(core.ps[:, n % 8, :], core.hT[:, k, t * P:(t + 1) * P],
                                              wb[:, b % RING, k, :], start=k == 0, stop=k == KD - 1)
                    mm.then_inc(summed, 1)

            @block.vector
            def _(dve):
                for n in range(0, len(items), 2):
                    dve.wait_ge(summed, n + 1)
                    nc.vector.tensor_scalar(target(*items[n]), core.ps[:, n % 8, :],
                                            SCALE if items[n][0] < 2 else 1.0, None, ALU.mult).then_inc(taken[0], 1)

            @block.scalar
            def _(act):
                for n in range(1, len(items), 2):
                    act.wait_ge(summed, n + 1)
                    nc.scalar.activation(target(*items[n]), core.ps[:, n % 8, :], ACT.Copy,
                                         scale=SCALE if items[n][0] < 2 else 1.0).then_inc(taken[1], 1)


def rope_odd(core, a, w):
    nc = core.nc
    with Stage(nc, "rope1") as st:
        tmp = st.sb("tmp", [P, 4, 16 * ROPE])
        lam = st.sb("lam", [P, 4, HEAD])
        dots = st.sb("dots", [P, 4])
        lam_in, own, rotated = st.sem("lam_in"), st.sem("own"), st.sem("rotated")
        dots_ready, exps_ready = st.sem("dots_ready"), st.sem("exps_ready")
        turned, taken = st.sem("turned"), [st.sem("taken_dve"), st.sem("taken_act")]
        items = [("k", c, 0) for c in range(KD)] + [("k", c, 1) for c in range(KD)] + [("q", c, 1) for c in range(KD)]

        def target(kind, c, s):
            return w.kT[:, c, s * CTX:(s + 1) * CTX] if kind == "k" else w.qT[:, c, :]

        with nc.Block() as block:
            @block.sync
            def _(sp):
                for i, name in enumerate(("diff_lq1", "diff_lk1", "diff_lq2", "diff_lk2")):
                    sp.dma_start(lam[:, i, :], a[name].to_broadcast([P, HEAD])).then_inc(lam_in, 16)
                sp.dma_start(w.sub_gain[:], a["diff_sub_gain"].to_broadcast([P, 2 * HEAD])).then_inc(lam_in, 16)

            @block.tensor
            def _(pe):
                for n, (kind, c, s) in enumerate(items):
                    if n == KD:
                        pe.wait_ge(rotated, 2)
                    if n == 2 * KD:
                        pe.wait_ge(rotated, 4)
                    if n >= 8:
                        pe.wait_ge(taken[n % 2], (n - 8) // 2 + 1)
                    for j in range(2):
                        src = w.k[:, 2 * s + j] if kind == "k" else w.q[:, j]
                        mm = nc.tensor.transpose(core.ps[:, n % 8, j * P:(j + 1) * P], src[:, c * P:(c + 1) * P],
                                                 core.c("ident"))
                    mm.then_inc(turned, 1)

            @block.scalar
            def _(act):
                act.wait_ge(dots_ready, 1)
                nc.scalar.activation(dots[:, 2:4], dots[:, 0:2], ACT.Exp).then_inc(exps_ready, 1)
                for n in range(1, len(items), 2):
                    act.wait_ge(turned, n + 1)
                    nc.scalar.copy(target(*items[n]), core.ps[:, n % 8, 0:CTX]).then_inc(taken[1], 1)

            @block.vector
            def _(dve):
                link = Chain(dve, own)

                def take(n):
                    dve.wait_ge(turned, n + 1)
                    nc.vector.tensor_copy(target(*items[n]), core.ps[:, n % 8, 0:CTX]).then_inc(taken[0], 1)

                for x in (w.k[:, 2:4], w.q):
                    for t in range(2):
                        cos = core.c("cos")[:, t * ROPE:(t + 1) * ROPE]
                        sin = core.c("sin")[:, t * ROPE:(t + 1) * ROPE]
                        rotate(nc, link, x[:, t, :].rearrange("p (h r two) -> p h r two", r=ROPE, two=2), tmp, cos, sin)
                        nc.vector.engine_nop().then_inc(rotated, 1)
                        for n in range(0, KD, 2):
                            if x is not w.q and t == 0:
                                take(n)
                dve.wait_ge(lam_in, 16 * 5)
                for i in range(2):
                    link(nc.vector.tensor_tensor(lam[:, 2 * i, :], lam[:, 2 * i, :], lam[:, 2 * i + 1, :], ALU.mult))
                    ins = nc.vector.tensor_reduce(dots[:, i:i + 1], lam[:, 2 * i, :], AX, ALU.add)
                ins.then_inc(dots_ready, 1)
                link(nc.vector.tensor_scalar(w.sub_gain[:], w.sub_gain[:], 1.0 - LAM_INIT, None, ALU.mult))
                dve.wait_ge(exps_ready, 1)
                link(nc.vector.tensor_tensor(dots[:, 0:1], dots[:, 3:4], dots[:, 2:3], ALU.subtract))
                link(nc.vector.tensor_scalar(w.neg_lam[:], dots[:, 0:1], -LAM_INIT, None, ALU.add))
                for n in range(KD, len(items), 2):
                    take(n)


def attend_odd(core, w):
    nc = core.nc
    KEYS = CTX + LAT
    with Stage(nc, "attn1") as st:
        p = st.sb("p", [P, 2, 2, KEYS])
        pd = st.sb("pd", [P, 2, KEYS])
        pT = st.sb("pT", [P, 2, 4, P])
        mx = st.sb("mx", [P, 2, 2, 2])
        sm = st.sb("sm", [P, 2, 4])
        names = ("scored", "max_own", "max_ready", "exp_ready", "recip_ready", "scaled", "mixed", "turned",
                 "pT_ready", "summed", "o_taken")
        (scored, max_own, max_ready, exp_ready, recip_ready, scaled, mixed, turned, pT_ready, summed,
         o_taken) = (st.sem(n) for n in names)
        items = [(h, t) for h in range(DIFF_HEADS) for t in range(2)]
        N = len(items)
        with nc.Block() as block:
            @block.tensor
            def _(pe):
                def score(n):
                    h, t = items[n]
                    if n >= 1:
                        pe.wait_ge(exp_ready, n)
                    for c in range(2):
                        base = HEAD * c
                        mm = nc.tensor.matmul(core.ps[:, c, :], w.qT[base:base + HEAD, h, t * P:(t + 1) * P],
                                              w.kT[base:base + HEAD, h, :], start=True, stop=True)
                    mm.then_inc(scored, 1)

                def turn(n):
                    pe.wait_ge(mixed, n + 1)
                    if n >= 2:
                        pe.wait_ge(pT_ready, n - 1)
                    for kt in range(4):
                        mm = nc.tensor.transpose(core.ps[:, 2 + n % 2, kt * P:(kt + 1) * P],
                                                 pd[:, n % 2, kt * P:(kt + 1) * P], core.c("ident"))
                    mm.then_inc(turned, 1)

                def weigh(n):
                    h, t = items[n]
                    pe.wait_ge(pT_ready, n + 1)
                    if n >= 2:
                        pe.wait_ge(o_taken, n - 1)
                    for kt in range(4):
                        mm = nc.tensor.matmul(core.ps[:, 4 + n % 2, 0:P], pT[:, n % 2, kt, :],
                                              w.v[:, kt, h * P:(h + 1) * P], start=kt == 0, stop=kt == 3)
                    mm.then_inc(summed, 1)

                for n in range(N + 2):
                    if n < N:
                        score(n)
                    if 1 <= n < N + 1:
                        turn(n - 1)
                    if 2 <= n:
                        weigh(n - 2)

            @block.scalar
            def _(act):
                def exps(n):
                    if n >= 2:
                        act.wait_ge(mixed, n - 1)
                    act.wait_ge(max_ready, n + 1)
                    for c in range(2):
                        ins = nc.scalar.activation(p[:, n % 2, c, :], core.ps[:, c, :], ACT.Exp,
                                                   bias=mx[:, n % 2, 1, c:c + 1], accum_out=sm[:, n % 2, c:c + 1])
                    ins.then_inc(exp_ready, 1)

                def take_turned(n):
                    act.wait_ge(turned, n + 1)
                    if n >= 2:
                        act.wait_ge(summed, n - 1)
                    nc.scalar.copy(pT[:, n % 2].rearrange("p k q -> p (k q)"), core.ps[:, 2 + n % 2, :]).then_inc(pT_ready, 1)

                for n in range(N + 1):
                    if n < N:
                        exps(n)
                    if n >= 1:
                        take_turned(n - 1)

            @block.gpsimd
            def _(pool):
                for n in range(N):
                    pool.wait_ge(recip_ready, n + 1)
                    nc.gpsimd.tensor_scalar(p[:, n % 2, 1, :], p[:, n % 2, 1, :], sm[:, n % 2, 3:4], w.neg_lam[:, 0:1],
                                            ALU.mult, ALU.mult).then_inc(scaled, 1)

            @block.vector
            def _(dve):
                def take_max(n):
                    dve.wait_ge(scored, n + 1)
                    nc.vector.tensor_reduce(mx[:, n % 2, 0, :], core.ps[:, 0:2, :], AX, ALU.max).then_inc(max_own, 1)
                    dve.wait_ge(max_own, n + 1)
                    nc.vector.tensor_scalar(mx[:, n % 2, 1, :], mx[:, n % 2, 0, :], -1.0, None, ALU.mult).then_inc(max_ready, 1)

                def recip(n):
                    dve.wait_ge(exp_ready, n + 1)
                    nc.vector.reciprocal(sm[:, n % 2, 2:4], sm[:, n % 2, 0:2]).then_inc(recip_ready, 1)

                def mix(n):
                    dve.wait_ge(scaled, n + 1)
                    if n >= 2:
                        dve.wait_ge(turned, n - 1)
                    nc.vector.scalar_tensor_tensor(out=pd[:, n % 2, :], in0=p[:, n % 2, 0, :], scalar=sm[:, n % 2, 2:3],
                                                   in1=p[:, n % 2, 1, :], op0=ALU.mult, op1=ALU.add).then_inc(mixed, 1)

                def take_out(n):
                    h, t = items[n]
                    dve.wait_ge(summed, n + 1)
                    nc.vector.tensor_copy(w.o[:, t, h, :], core.ps[:, 4 + n % 2, 0:P]).then_inc(o_taken, 1)

                for n in range(N + 3):
                    if n < N:
                        take_max(n)
                        recip(n)
                        mix(n)
                    if 3 <= n:
                        take_out(n - 3)


def norm_heads(core, w):
    nc = core.nc
    H = DIFF_HEADS
    with Stage(nc, "subnorm") as st:
        sq = st.sb("sq", [P, 2 * H, 2 * HEAD])
        rs = st.sb("rs", [P, 4, 2 * H])
        own, var_ready, root_ready, o_ready, turned, taken = (
            st.sem(n) for n in ("own", "var_ready", "root_ready", "o_ready", "turned", "taken"))
        o = w.o[:].rearrange("p t h d -> p (t h) d")
        with nc.Block() as block:
            @block.vector
            def _(dve):
                link = Chain(dve, own)
                link(nc.vector.tensor_tensor(sq[:], o, o, ALU.mult))
                link(nc.vector.tensor_reduce(rs[:, 0, :], sq[:], AX, ALU.add))
                nc.vector.tensor_scalar(rs[:, 1, :], rs[:, 0, :], 1.0 / P, EPS, ALU.mult, ALU.add).then_inc(var_ready, 1)
                dve.wait_ge(root_ready, 1)
                link(nc.vector.reciprocal(rs[:, 3, :], rs[:, 2, :]))
                for t in range(2):
                    for h in range(H):
                        n = t * H + h
                        ins = nc.vector.scalar_tensor_tensor(out=sq[:, n, :], in0=o[:, n, :], scalar=rs[:, 3, n:n + 1],
                                                             in1=w.sub_gain[:], op0=ALU.mult, op1=ALU.mult)
                    ins.then_inc(o_ready, 1)
                for n in range(4):
                    dve.wait_ge(turned, n + 1)
                    t, half = n // 2, n % 2
                    nc.vector.tensor_copy(w.oT[:, 4 * half:4 * half + 4, t * P:(t + 1) * P],
                                          core.ps[:, n, :].rearrange("p (h q) -> p h q", q=P)).then_inc(taken, 1)

            @block.scalar
            def _(act):
                act.wait_ge(var_ready, 1)
                nc.scalar.activation(rs[:, 2, :], rs[:, 1, :], ACT.Sqrt).then_inc(root_ready, 1)

            @block.tensor
            def _(pe):
                for n in range(4):
                    pe.wait_ge(o_ready, n // 2 + 1)
                    for i in range(4):
                        mm = nc.tensor.transpose(core.ps[:, n, i * P:(i + 1) * P], sq[:, 4 * n + i, :], core.c("ident"))
                    mm.then_inc(turned, 1)


class OddBuffers:
    def __init__(self, nc, stack):
        def sb(name, shape):
            return stack.enter_context(nc.sbuf_tensor(name, shape, F32))

        self.q = sb("q1", [P, 2, D])
        self.k, self.v = sb("k1", [P, TILES, D]), sb("v1", [P, TILES, D])
        self.qT, self.kT = sb("qT1", [P, KD, LAT]), sb("kT1", [P, KD, CTX + LAT])
        self.o = sb("o1", [P, 2, DIFF_HEADS, 2 * HEAD])
        self.oT = sb("oT1", [P, KD, LAT])
        self.sub_gain = sb("sub_gain", [P, 2 * HEAD])
        self.neg_lam = sb("neg_lam", [P, 1])


def layer_odd(core, a):
    with ExitStack() as stack:
        w = OddBuffers(core.nc, stack)
        norm_transpose(core, 1, 0, [0, 1])
        project_odd(core, a, w)
        rope_odd(core, a, w)
        attend_odd(core, w)
        norm_heads(core, w)
        project_out(core, a, 1, "diff_w_out", w, [2, 3], lambda t: slice((t - 2) * P, (t - 1) * P))


def finish(core, a, out):
    nc = core.nc
    with Stage(nc, "final") as st:
        xn = st.sb("xn", [P, 2, D])
        gain = st.sb("gain", [P, D])
        ss, rs = st.sb("ss", [P, 2]), st.sb("rs", [P, 3, 2])
        sq_ready, var_ready, root_ready = st.sem("sq"), st.sem("var"), st.sem("root")
        row_ready, own, gain_in, done, stored = (st.sem(n) for n in ("row", "own", "gain_in", "done", "stored"))
        on_act, on_dve = rms_rows(core, [2, 3], xn, ss, rs, sq_ready, root_ready, var_ready)
        with nc.Block() as block:
            @block.sync
            def _(sp):
                sp.dma_start(gain[:], a["final_norm"].rearrange("(o d) -> o d", o=1).to_broadcast([P, D])).then_inc(gain_in, 16)
                for i in range(2):
                    sp.wait_ge(done, i + 1)
                    sp.dma_start(out[0, i * P:(i + 1) * P, :], xn[:, i, :]).then_inc(stored, 16)
                sp.wait_ge(stored, 32)

            @block.scalar
            def _(act):
                on_act(act)

            @block.vector
            def _(dve):
                link = Chain(dve, own)
                on_dve(dve, link, row_ready)
                dve.wait_ge(gain_in, 16)
                for i in range(2):
                    dve.wait_ge(row_ready, i + 1)
                    nc.vector.tensor_tensor(xn[:, i, :], xn[:, i, :], gain[:], ALU.mult).then_inc(done, 1)


def backbone(nc, a, out):
    with ExitStack() as ctx:
        core = Core(nc, ctx)
        modulation(core, a)
        layer_even(core, a)
        moe(core, a, 0, list(range(TILES)))
        layer_odd(core, a)
        moe(core, a, 1, [2, 3])
        finish(core, a, out)


_INS = ["x", "c", "ctx", "c_ctx", "ada_w", "ada_b", "norm_mix", "norm_ffn", "ab_w_in", "ab_w_out", "na_rpb",
        "gqa_q_gain", "gqa_k_gain", "diff_w_in", "diff_w_out", "diff_lq1", "diff_lk1", "diff_lq2", "diff_lk2",
        "diff_sub_gain", "router_w", "router_bias", "expert_w_gate", "expert_w_up", "expert_w_down",
        "shared_w_gate", "shared_w_up", "shared_w_down", "final_norm"]
_OUT = (1, LAT, D)


def kernel(**inputs):
    import concourse.bacc as _bacc
    from concourse.bass_utils import run_bass_kernel_spmd as _run

    nc = _bacc.Bacc("TRN2", target_bir_lowering=False, num_devices=1)
    arrays, args = {}, {}
    for name in _INS + ["consts"]:
        v = constants() if name == "consts" else np.ascontiguousarray(inputs[name])
        arrays[f"in_{name}_dram"] = v
        args[name] = nc.dram_tensor(f"in_{name}_dram", v.shape, mybir.dt.from_np(v.dtype), kind="ExternalInput").ap()
    out = nc.dram_tensor("out_0_dram", _OUT, F32, kind="ExternalOutput").ap()
    backbone(nc, args, out)
    r = _run(nc, [arrays], core_ids=[0])
    return r.results[0]["out_0_dram"]
```

```python
from contextlib import ExitStack

import numpy as np

import concourse.bass as bass
from concourse import mybir

F32 = mybir.dt.float32
BF16 = mybir.dt.bfloat16
I32 = mybir.dt.int32
ALU = mybir.AluOpType
ACT = mybir.ActivationFunctionType
AX = mybir.AxisListType.X

P = 128
D = 1024
KD = D // P
CTX = 256
LAT = 256
GRID_W = 64
WIN_COLS = 16
WIN_ROWS = 8
HEAD = 64
NA_HEADS = 8
GQA_HEADS = 8
GQA_KV = 2
HEADS = NA_HEADS + GQA_HEADS
DIFF_HEADS = 8
EPS = 1e-6
SCALE = HEAD ** -0.5
E = 64
TOP_K = 8
F = D // 4
KF = F // P
ROUTED_SCALE = 2.5
LAM_INIT = 0.8 - 0.6 * float(np.exp(-0.3))
STREAMS = 2
TILES = (CTX + LAT) // P
SLOTS = 128
BIG = 16384
MASKED = -1e30
NA_ROWS = LAT // GRID_W
REL = NA_ROWS + 2
ROPE = HEAD // 2

CONST = {}
_at = 0
for _name, _n in (("ident", P), ("flip", P), ("before", P), ("ones", P), ("iota", 512), ("pick", 2),
                  ("na_mask", GRID_W), ("cos", 2 * ROPE), ("sin", 2 * ROPE), ("tok_hi", TILES),
                  ("dest_hi", TILES), ("tok_lo", 1), ("dest_lo", 1)):
    CONST[_name] = (_at, _at + _n)
    _at += _n
CONST_W = _at


def constants():
    c = np.zeros((P, CONST_W), np.float32)

    def put(name, a):
        c[:, CONST[name][0]:CONST[name][1]] = a

    p = np.arange(P)
    put("ident", np.eye(P))
    flip = np.zeros((P, P))
    for half in range(2):
        for i in range(GRID_W):
            flip[half * GRID_W + i, half * GRID_W + GRID_W - 1 - i] = 1.0
    put("flip", flip)
    put("before", p[:, None] < p[None, :])
    put("ones", np.ones((P, P)))
    put("iota", np.tile(np.arange(512), (P, 1)))
    pick = np.zeros((P, 2))
    for g in range(4):
        pick[32 * g, 0] = pick[32 * g + 1, 1] = 1.0
    put("pick", pick)
    col = GRID_W - 1 - p % GRID_W
    start = np.clip(col - WIN_COLS // 2, 0, GRID_W - WIN_COLS)
    key = np.arange(GRID_W)
    inside = (key[None] >= start[:, None]) & (key[None] < start[:, None] + WIN_COLS)
    put("na_mask", np.where(inside, 0.0, MASKED))
    t = np.arange(LAT)
    pairs = HEAD // 4
    freq = (np.float32(10000.0) ** (-np.arange(pairs, dtype=np.float32) / np.float32(pairs))).astype(np.float32)
    row, column = (t // GRID_W).astype(np.float32), (t % GRID_W).astype(np.float32)
    angle = np.concatenate([row[:, None] * freq, column[:, None] * freq], axis=-1).astype(np.float32)
    put("cos", np.cos(angle).reshape(2, P, ROPE).transpose(1, 0, 2).reshape(P, -1))
    put("sin", np.sin(angle).reshape(2, P, ROPE).transpose(1, 0, 2).reshape(P, -1))
    put("tok_hi", np.tile(P * np.arange(TILES) - BIG, (P, 1)))
    put("dest_hi", np.tile(TOP_K * P * np.arange(TILES) - BIG, (P, 1)))
    put("tok_lo", p[:, None])
    put("dest_lo", TOP_K * p[:, None])
    return c


class Stage:

    def __init__(self, nc, name):
        self.nc, self.name, self.sems, self.stack = nc, name, [], ExitStack()

    def __enter__(self):
        return self

    def sb(self, name, shape, dt=F32):
        return self.stack.enter_context(self.nc.sbuf_tensor(f"{self.name}_{name}", shape, dt))

    def sem(self, name):
        s = self.stack.enter_context(self.nc.semaphore(f"{self.name}_{name}"))
        self.sems.append(s)
        return s

    def pool_sem(self, name):
        return self.nc.alloc_semaphore(f"{self.name}_{name}")

    def __exit__(self, *a):
        if a[0] is None:
            with self.nc.Block() as block:
                @block.sync
                def _(sp):
                    for s in self.sems:
                        sp.sem_clear(s)
        self.stack.close()


class Chain:

    def __init__(self, eng, sem):
        self.eng, self.sem, self.n = eng, sem, 0

    def __call__(self, ins):
        self.n += 1
        ins.then_inc(self.sem, 1)
        self.eng.wait_ge(self.sem, self.n)


BLOCK = 512
STREAM = 4


class Stream:

    def __init__(self, nc, wb, a):
        self.nc, self.wb, self.fed = nc, wb, 0
        self.loaded = [nc.alloc_semaphore(f"block_loaded{i}") for i in range(STREAM)]
        self.blocks, self.start, self.end = [], {}, {}
        ada = a["ada_w"].rearrange("l (p k) n -> l p k n", k=KD)
        for name, src in (("ada0", ada[0]), ("ab_w_in", a["ab_w_in"].rearrange("o (k p) n -> p (o k) n", p=P)),
                          ("ada1", ada[1]), ("ab_w_out", a["ab_w_out"].rearrange("o (k p) n -> p (o k) n", p=P)),
                          ("diff_w_in", a["diff_w_in"].rearrange("o (k p) n -> p (o k) n", p=P)),
                          ("diff_w_out", a["diff_w_out"].rearrange("o (k p) n -> p (o k) n", p=P))):
            self.start[name] = len(self.blocks)
            width = src.shape[-1]
            for c in range(0, width, BLOCK):
                self.blocks.append(src[:, :, c:min(c + BLOCK, width)])
            self.end[name] = len(self.blocks)

    def feed(self, sp, upto, first, used=None):
        for n in range(self.fed, upto):
            if n - STREAM >= first:
                sp.wait_ge(*used(n - STREAM - first))
            src = self.blocks[n]
            sp.dma_start(self.at(n)[:, :, 0:src.shape[-1]], src).then_inc(self.loaded[n % STREAM], 16)
        self.fed = max(self.fed, upto)

    def at(self, n):
        return self.wb[:, n % STREAM, :].rearrange("p (k n) -> p k n", n=BLOCK)

    def take(self, pe, n):
        pe.wait_ge(self.loaded[n % STREAM], 16 * (n // STREAM + 1))
        return self.at(n)


class Core:

    def __init__(self, nc, ctx, a):
        def sb(name, shape, dt=F32):
            return ctx.enter_context(nc.sbuf_tensor(name, shape, dt))

        self.nc = nc
        self.x = sb("x_res", [P, TILES, D])
        self.const = sb("const", [P, CONST_W])
        self.cols = sb("cols", [P, P])
        self.mod = sb("mod", [P, 2, 6 * KD, STREAMS])
        self.amp = sb("amp", [P, 2, 2, STREAMS, KD])
        self.hT = sb("hT", [P, KD, TILES * P])
        self.silu = sb("silu", [P, KD, 32])
        self.wb = sb("wb", [P, STREAM, KD * BLOCK])
        self.stream = Stream(nc, self.wb, a)
        self.ps = ctx.enter_context(nc.psum_tensor("ps", [P, 8, 512], F32))

    def c(self, name):
        return self.const[:, CONST[name][0]:CONST[name][1]]

    def gate_column(self, layer, which, stream, k):
        return self.mod[:, layer, (2 + 3 * which) * KD + k, stream:stream + 1]

    def shift_column(self, layer, which, stream, k):
        return self.mod[:, layer, 3 * which * KD + k, stream:stream + 1]


class Modulation:

    BLOCKS = 6 * D // BLOCK

    def __init__(self, core, st, layer, sum_banks, col_banks):
        self.core, self.layer, self.sum_banks, self.col_banks = core, layer, sum_banks, col_banks
        self.first = core.stream.start[f"ada{layer}"]
        self.part = st.sb("part", [P, 2, BLOCK])
        self.sums_ready, self.part_ready = st.sem("sums_ready"), st.sem("part_ready")
        self.colsum_ready, self.col_done = st.sem("colsum_ready"), st.sem("col_done")

    def used(self, n):
        return self.sums_ready, n + 1

    def pe_sums(self, pe, n):
        core, nc = self.core, self.core.nc
        w = core.stream.take(pe, self.first + n)
        if n >= len(self.sum_banks):
            pe.wait_ge(self.part_ready, n - len(self.sum_banks) + 1)
        bank = self.sum_banks[n % len(self.sum_banks)]
        for k in range(KD):
            g = 32 * (k % 4)
            mm = nc.tensor.matmul(core.ps[g:g + 32, bank, :], core.silu[:, k, :], w[:, k, :], start=k < 4,
                                  stop=k >= 4, skip_group_check=True, tile_position=(0, g))
        mm.then_inc(self.sums_ready, 1)

    def pe_columns(self, pe, n):
        core, nc = self.core, self.core.nc
        pe.wait_ge(self.part_ready, n + 1)
        if n >= len(self.col_banks):
            pe.wait_ge(self.col_done, n - len(self.col_banks) + 1)
        bank = self.col_banks[n % len(self.col_banks)]
        for j in range(4):
            mm = nc.tensor.matmul(core.ps[:, bank, 2 * j:2 * j + 2], self.part[:, n % 2, j * P:(j + 1) * P],
                                  core.c("pick"), start=True, stop=True)
        mm.then_inc(self.colsum_ready, 1)

    def dve_part(self, dve, n):
        dve.wait_ge(self.sums_ready, n + 1)
        if n >= 2:
            dve.wait_ge(self.colsum_ready, n - 1)
        bank = self.sum_banks[n % len(self.sum_banks)]
        self.core.nc.vector.tensor_copy(self.part[:, n % 2, :], self.core.ps[:, bank, :]).then_inc(self.part_ready, 1)

    def dve_take(self, dve, n):
        dve.wait_ge(self.colsum_ready, n + 1)
        out = self.core.mod[:, self.layer].rearrange("p j s -> p (j s)")[:, 8 * n:8 * n + 8]
        self.core.nc.vector.tensor_copy(out, self.core.ps[:, self.col_banks[n % len(self.col_banks)],
                                                          0:8]).then_inc(self.col_done, 1)

    def dve_finish(self, dve, link):
        core, nc, layer = self.core, self.core.nc, self.layer
        dve.wait_ge(self.col_done, self.BLOCKS)
        for s in range(STREAMS):
            m = core.mod[:, layer, :, s]
            link(nc.vector.tensor_tensor(m, m, core.cols[:, 6 * KD * layer:6 * KD * (layer + 1)], ALU.add))
        for which in range(2):
            gain = core.cols[:, 12 * KD + 16 * which + KD * layer:][:, 0:KD]
            for s in range(STREAMS):
                scale = core.mod[:, layer, (3 * which + 1) * KD:(3 * which + 2) * KD, s]
                link(nc.vector.scalar_tensor_tensor(out=core.amp[:, layer, which, s, :], in0=scale, scalar=1.0,
                                                    in1=gain, op0=ALU.add, op1=ALU.mult))


def modulation(core, a):
    nc = core.nc
    with Stage(nc, "adaln") as st:
        rows = st.sb("rows", [P, P])
        cond = st.sb("cond", [P, STREAMS, KD])
        tmp = st.sb("tmp", [P, 2, STREAMS * KD])
        const_in, rows_in, cond_in, x_in = (st.sem(n) for n in ("const_in", "rows_in", "cond_in", "x_in"))
        e_ready, silu_ready, rowsT, own = (st.sem(n) for n in ("e_ready", "silu_ready", "rowsT", "own"))
        m = Modulation(core, st, 0, [0, 1, 2, 3], [4, 5])
        with nc.Block() as block:
            @block.sync
            def _(sp):
                sp.dma_start(cond[:, 0, :], a["c_ctx"].rearrange("(p k) -> p k", k=KD)).then_inc(cond_in, 16)
                sp.dma_start(cond[:, 1, :], a["c"].rearrange("o (p k) -> (o p) k", k=KD)).then_inc(cond_in, 16)
                core.stream.feed(sp, 2, 0)
                sp.dma_start(core.const[:], a["consts"]).then_inc(const_in, 16)
                core.stream.feed(sp, STREAM, 0)
                nb = 2 * 6 * KD
                sp.dma_start(rows[0:nb, :], a["ada_b"].rearrange("l (j p) -> (l j) p", p=P)).then_inc(rows_in, 16)
                sp.dma_start(rows[nb:nb + 16, :], a["norm_mix"].rearrange("l (j p) -> (l j) p", p=P)).then_inc(rows_in, 16)
                sp.dma_start(rows[nb + 16:nb + 32, :], a["norm_ffn"].rearrange("l (j p) -> (l j) p", p=P)).then_inc(rows_in, 16)
                core.stream.feed(sp, m.BLOCKS, 0, m.used)
                sp.dma_start(core.x[:, 0:2], a["ctx"].rearrange("o (t p) d -> p (o t) d", p=P)).then_inc(x_in, 16)
                sp.dma_start(core.x[:, 2:4], a["x"].rearrange("o (t p) d -> p (o t) d", p=P)).then_inc(x_in, 16)
                core.stream.feed(sp, m.BLOCKS + STREAM, 0, m.used)
                sp.wait_ge(x_in, 32)

            @block.scalar
            def _(act):
                act.wait_ge(cond_in, 32)
                nc.scalar.activation(tmp[:, 0, :], cond[:].rearrange("p s k -> p (s k)"), ACT.Exp,
                                     scale=-1.0).then_inc(e_ready, 1)

            @block.tensor
            def _(pe):
                pe.wait_ge(silu_ready, 1)
                for n in range(m.BLOCKS):
                    m.pe_sums(pe, n)
                    if n == 0:
                        pe.wait_ge(const_in, 16)
                    if n >= 1:
                        m.pe_columns(pe, n - 1)
                m.pe_columns(pe, m.BLOCKS - 1)
                pe.wait_ge(rows_in, 48)
                nc.tensor.transpose(core.ps[:, 6, 0:P], rows[:], core.c("ident")).then_inc(rowsT, 1)

            @block.vector
            def _(dve):
                link = Chain(dve, own)
                link(nc.vector.memset(core.silu[:], 0.0))
                dve.wait_ge(e_ready, 1)
                link(nc.vector.tensor_scalar(tmp[:, 1, :], tmp[:, 0, :], 1.0, None, ALU.add))
                link(nc.vector.reciprocal(tmp[:, 0, :], tmp[:, 1, :]))
                nc.vector.tensor_tensor(core.silu[:, :, 0:STREAMS].rearrange("p k s -> p s k"), cond[:],
                                        tmp[:, 0, :].rearrange("p (s k) -> p s k", s=STREAMS),
                                        ALU.mult).then_inc(silu_ready, 1)
                for n in range(m.BLOCKS):
                    m.dve_part(dve, n)
                    if n >= 1:
                        m.dve_take(dve, n - 1)
                m.dve_take(dve, m.BLOCKS - 1)
                dve.wait_ge(rowsT, 1)
                link(nc.vector.tensor_copy(core.cols[:], core.ps[:, 6, 0:P]))
                m.dve_finish(dve, link)


def rms_rows(core, tiles, out, ss, rs, sq_ready, root_ready, var_ready):
    nc, n = core.nc, len(tiles)

    def on_act(act):
        for i, t in enumerate(tiles):
            ins = nc.scalar.activation(out[:, i, :], core.x[:, t, :], ACT.Square, accum_out=ss[:, i:i + 1])
        ins.then_inc(sq_ready, 1)
        act.wait_ge(var_ready, 1)
        nc.scalar.activation(rs[:, 1, 0:n], rs[:, 0, 0:n], ACT.Sqrt).then_inc(root_ready, 1)

    def on_dve(dve, link, row_ready):
        dve.wait_ge(sq_ready, 1)
        nc.vector.tensor_scalar(rs[:, 0, 0:n], ss[:, 0:n], 1.0 / D, EPS, ALU.mult, ALU.add).then_inc(var_ready, 1)
        dve.wait_ge(root_ready, 1)
        link(nc.vector.reciprocal(rs[:, 2, 0:n], rs[:, 1, 0:n]))
        for i, t in enumerate(tiles):
            nc.vector.tensor_scalar(out[:, i, :], core.x[:, t, :], rs[:, 2, i:i + 1], None,
                                    ALU.mult).then_inc(row_ready, 1)

    return on_act, on_dve


def norm_transpose(core, layer, which, streams, sync=None):
    nc = core.nc
    name = f"norm{layer}{which}"
    tiles = [2 * s + i for s in streams for i in range(2)]
    with Stage(nc, name) as st:
        xn = st.sb("xn", [P, len(tiles), D])
        ss, rs = st.sb("ss", [P, TILES]), st.sb("rs", [P, 3, TILES])
        sq_ready, var_ready, root_ready = st.sem("sq"), st.sem("var"), st.sem("root")
        row_ready, turned, taken = st.sem("row"), st.sem("turned"), [st.sem("taken_dve"), st.sem("taken_act")]
        own = st.sem("own")
        items = [(i, s, k) for i, s in enumerate(streams) for k in range(KD)]
        on_act, on_dve = rms_rows(core, tiles, xn, ss, rs, sq_ready, root_ready, var_ready)

        def scaled(n, engine):
            i, s, k = items[n]
            return (core.hT[:, k, s * CTX:s * CTX + CTX], core.ps[:, n % 8, 0:CTX],
                    core.amp[:, layer, which, s, k:k + 1], core.shift_column(layer, which, s, k))

        with nc.Block() as block:
            @block.sync
            def _(sp):
                if sync:
                    sync(sp)

            @block.scalar
            def _(act):
                on_act(act)
                for n in range(1, len(items), 2):
                    act.wait_ge(turned, n + 1)
                    out, src, amp, shift = scaled(n, act)
                    nc.scalar.activation(out, src, ACT.Identity, scale=amp, bias=shift).then_inc(taken[1], 1)

            @block.tensor
            def _(pe):
                for n, (i, s, k) in enumerate(items):
                    pe.wait_ge(row_ready, 2 * i + 2)
                    if n >= 8:
                        pe.wait_ge(taken[n % 2], (n - 8) // 2 + 1)
                    for j in range(2):
                        mm = nc.tensor.transpose(core.ps[:, n % 8, j * P:(j + 1) * P],
                                                 xn[:, 2 * i + j, k * P:(k + 1) * P], core.c("ident"))
                    mm.then_inc(turned, 1)

            @block.vector
            def _(dve):
                link = Chain(dve, own)
                on_dve(dve, link, row_ready)
                for n in range(0, len(items), 2):
                    dve.wait_ge(turned, n + 1)
                    out, src, amp, shift = scaled(n, dve)
                    nc.vector.tensor_scalar(out, src, amp, shift, ALU.mult, ALU.add).then_inc(taken[0], 1)




def project_even(core, a, w):
    nc = core.nc
    widths = [BLOCK] * 4 + [2 * GQA_KV * HEAD]
    rows = 2 * WIN_ROWS - 1
    first = core.stream.start["ab_w_in"]
    with Stage(nc, "proj0") as st:
        pad = st.sb("rpb_pad", [NA_HEADS * rows, P])
        rpb_sem, rpb_ready = st.pool_sem("rpb_sem"), st.sem("rpb_ready")
        summed, taken = st.sem("summed"), [st.sem("taken_dve"), st.sem("taken_act")]
        items = [(b, j) for b in range(len(widths)) for j in range(4)]

        def target(b, j):
            if b < 2:
                return (w.qaT, w.kaT)[b][:, j, :]
            return w.kvb[:, j, :] if b == 4 else (w.va, w.qb)[b - 2][:, j, :]

        with nc.Block() as block:
            @block.sync
            def _(sp):
                core.stream.feed(sp, core.stream.end["ab_w_in"] + STREAM, first, lambda b: (summed, 4 * b + 4))

            @block.gpsimd
            def _(pool):
                nc.gpsimd.memset(pad[:], 0.0).then_inc(rpb_ready, 1)
                pool.wait_ge(rpb_ready, 1)
                pool.dma_start(pad[:, GRID_W - WIN_COLS:GRID_W + WIN_COLS - 1],
                               a["na_rpb"].rearrange("o h r c -> (o h r) c")).then_inc(rpb_sem, 16)
                pool.wait_ge(rpb_sem, 16)
                pool.dma_start(w.rpb_rows, pad[:]).then_inc(rpb_sem, 16)
                pool.wait_ge(rpb_sem, 32)
                for half in range(2):
                    for h in range(NA_HEADS):
                        start = (h * rows + WIN_ROWS - 1 - 2 - half) * P
                        src = bass.AP(w.rpb_rows.tensor, start, [[1, GRID_W], [P, REL], [1, GRID_W]])
                        pool.dma_start(w.bias[half * GRID_W:(half + 1) * GRID_W, h], src).then_inc(rpb_sem, 16)
                pool.wait_ge(rpb_sem, 32 + 16 * 2 * NA_HEADS)
                m = core.c("na_mask").rearrange("p (o c) -> p o c", o=1).to_broadcast([P, NA_HEADS * REL, GRID_W])
                b = w.bias[:].rearrange("p h u c -> p (h u) c")
                nc.gpsimd.tensor_tensor(b, b, m, ALU.add).then_inc(rpb_ready, 1)

            @block.tensor
            def _(pe):
                for n, (b, j) in enumerate(items):
                    wb = core.stream.take(pe, first + b)
                    if n >= 8:
                        pe.wait_ge(taken[n % 2], (n - 8) // 2 + 1)
                    for k in range(KD):
                        if b < 2:
                            lhs, rhs = wb[:, k, j * P:(j + 1) * P], core.hT[:, k, :]
                        else:
                            lhs, rhs = core.hT[:, k, j * P:(j + 1) * P], wb[:, k, 0:widths[b]]
                        mm = nc.tensor.matmul(core.ps[:, n % 8, 0:widths[b]], lhs, rhs, start=k == 0,
                                              stop=k == KD - 1)
                    mm.then_inc(summed, 1)

            @block.vector
            def _(dve):
                for n in range(0, len(items), 2):
                    b, j = items[n]
                    dve.wait_ge(summed, n + 1)
                    nc.vector.tensor_scalar(target(b, j), core.ps[:, n % 8, 0:widths[b]], SCALE if b == 0 else 1.0,
                                            None, ALU.mult).then_inc(taken[0], 1)

            @block.scalar
            def _(act):
                for n in range(1, len(items), 2):
                    b, j = items[n]
                    act.wait_ge(summed, n + 1)
                    nc.scalar.activation(target(b, j), core.ps[:, n % 8, 0:widths[b]], ACT.Copy,
                                         scale=SCALE if b == 0 else 1.0).then_inc(taken[1], 1)


def rotate(nc, link, pairs, tmp, cos, sin):
    heads = pairs.shape[1]
    even, odd = pairs[:, :, :, 0], pairs[:, :, :, 1]
    t = [tmp[:, i, 0:heads * ROPE].rearrange("p (h r) -> p h r", h=heads) for i in range(4)]
    c = cos.rearrange("p (o r) -> p o r", o=1).to_broadcast([P, heads, ROPE])
    s = sin.rearrange("p (o r) -> p o r", o=1).to_broadcast([P, heads, ROPE])
    nc.vector.tensor_tensor(t[0], even, c, ALU.mult)
    nc.vector.tensor_tensor(t[1], odd, s, ALU.mult)
    nc.vector.tensor_tensor(t[2], even, s, ALU.mult)
    link(nc.vector.tensor_tensor(t[3], odd, c, ALU.mult))
    nc.vector.tensor_tensor(even, t[0], t[1], ALU.subtract)
    link(nc.vector.tensor_tensor(odd, t[2], t[3], ALU.add))


def qk_norm_rope(core, a, w):
    nc = core.nc
    with Stage(nc, "qknorm") as st:
        gain = st.sb("gain", [P, 2, HEAD])
        sq = st.sb("sq", [P, TILES, GQA_HEADS * HEAD])
        ss = st.sb("ss", [P, 4, TILES * GQA_HEADS])
        sk = st.sb("sk", [P, 4, TILES * GQA_KV])
        tmp = st.sb("tmp", [P, 4, GQA_HEADS * ROPE])
        kdup = st.sb("kdup", [P, TILES, GQA_KV, 2, HEAD])
        gains_in, own = st.sem("gains_in"), st.sem("own")
        var_ready, root_ready = st.sem("var_ready"), st.sem("root_ready")
        q_tile, k_ready = st.sem("q_tile"), st.sem("k_ready")
        turned, taken = st.sem("turned"), [st.sem("taken_dve"), st.sem("taken_act")]
        q = w.qb
        k = w.kvb[:, :, 0:GQA_KV * HEAD]
        items = [("q", c) for c in range(4)] + [("k", g) for g in range(GQA_KV)]
        with nc.Block() as block:
            @block.sync
            def _(sp):
                sp.dma_start(gain[:, 0, :], a["gqa_q_gain"].to_broadcast([P, HEAD])).then_inc(gains_in, 16)
                sp.dma_start(gain[:, 1, :], a["gqa_k_gain"].to_broadcast([P, HEAD])).then_inc(gains_in, 16)

            @block.scalar
            def _(act):
                act.wait_ge(var_ready, 1)
                nc.scalar.activation(ss[:, 2, :], ss[:, 1, :], ACT.Sqrt)
                nc.scalar.activation(sk[:, 2, :], sk[:, 1, :], ACT.Sqrt).then_inc(root_ready, 1)
                for n in range(1, len(items), 2):
                    act.wait_ge(turned, n + 1)
                    kind, c = items[n]
                    nc.scalar.copy((w.qbT if kind == "q" else w.kbT)[:, c, :], core.ps[:, n, :]).then_inc(taken[1], 1)

            @block.vector
            def _(dve):
                link = Chain(dve, own)
                nq, nk = GQA_HEADS * HEAD, GQA_KV * HEAD
                nc.vector.tensor_tensor(sq[:], q[:], q[:], ALU.mult)
                link(nc.vector.tensor_tensor(kdup[:].rearrange("p t g u d -> p t (g u d)")[:, :, 0:nk], k, k, ALU.mult))
                nc.vector.tensor_reduce(ss[:, 0, :], sq[:].rearrange("p t (h d) -> p (t h) d", d=HEAD), AX, ALU.add)
                link(nc.vector.tensor_reduce(sk[:, 0, :].rearrange("p (t g) -> p t g", t=TILES),
                                             kdup[:].rearrange("p t g u d -> p t (g u d)")[:, :, 0:nk]
                                             .rearrange("p t (g d) -> p t g d", d=HEAD), AX, ALU.add))
                nc.vector.tensor_scalar(ss[:, 1, :], ss[:, 0, :], 1.0 / HEAD, EPS, ALU.mult, ALU.add)
                nc.vector.tensor_scalar(sk[:, 1, :], sk[:, 0, :], 1.0 / HEAD, EPS, ALU.mult,
                                        ALU.add).then_inc(var_ready, 1)
                dve.wait_ge(gains_in, 32)
                link(nc.vector.tensor_scalar(gain[:, 0, :], gain[:, 0, :], SCALE, None, ALU.mult))
                dve.wait_ge(root_ready, 1)
                nc.vector.reciprocal(ss[:, 3, :], ss[:, 2, :])
                link(nc.vector.reciprocal(sk[:, 3, :], sk[:, 2, :]))
                for t in range(TILES):
                    qt = q[:, t, :].rearrange("p (h d) -> p h d", d=HEAD)
                    kt = k[:, t, :].rearrange("p (h d) -> p h d", d=HEAD)
                    for x, heads, r, g in ((qt, GQA_HEADS, ss, 0), (kt, GQA_KV, sk, 1)):
                        rb = r[:, 3, t * heads:(t + 1) * heads].rearrange("p (h o) -> p h o", o=1)
                        link(nc.vector.tensor_tensor(x, x, rb.to_broadcast([P, heads, HEAD]), ALU.mult))
                        gb = gain[:, g, :].rearrange("p (o d) -> p o d", o=1).to_broadcast([P, heads, HEAD])
                        link(nc.vector.tensor_tensor(x, x, gb, ALU.mult))
                        if t >= 2:
                            cos = core.c("cos")[:, (t - 2) * ROPE:(t - 1) * ROPE]
                            sin = core.c("sin")[:, (t - 2) * ROPE:(t - 1) * ROPE]
                            rotate(nc, link, x.rearrange("p h (r two) -> p h r two", two=2), tmp, cos, sin)
                    ins = nc.vector.tensor_copy(kdup[:, t], kt.rearrange("p g (o d) -> p g o d", o=1)
                                                .to_broadcast([P, GQA_KV, 2, HEAD]))
                    link(ins)
                nc.vector.engine_nop().then_inc(q_tile, 1)
                for n in range(0, len(items), 2):
                    dve.wait_ge(turned, n + 1)
                    kind, c = items[n]
                    nc.vector.tensor_copy((w.qbT if kind == "q" else w.kbT)[:, c, :], core.ps[:, n, :]).then_inc(taken[0], 1)

            @block.tensor
            def _(pe):
                pe.wait_ge(q_tile, 1)
                for n, (kind, c) in enumerate(items):
                    for t in range(TILES):
                        src = q[:, t, c * P:(c + 1) * P] if kind == "q" else \
                            kdup[:, t, c].rearrange("p u d -> p (u d)")
                        mm = nc.tensor.transpose(core.ps[:, n, t * P:(t + 1) * P], src, core.c("ident"))
                    mm.then_inc(turned, 1)


def attend_even(core, w):
    nc = core.nc
    with Stage(nc, "attn0") as st:
        p = st.sb("p", [P, 4, 512])
        pn = st.sb("pn", [P, 4, 512])
        pT = st.sb("pT", [P, 4, 4, CTX])
        mx = st.sb("mx", [P, 4, 4])
        scored, max_ready, exp_ready, recip_ready = (
            st.sem(n) for n in ("scored", "max_ready", "exp_ready", "recip_ready"))
        norm_pool, norm_act = st.sem("norm_pool"), st.sem("norm_act")
        turned, pT_ready, summed, out_done = st.sem("turned"), st.sem("pT_ready"), st.sem("summed"), st.sem("out_done")
        own, m1_own = st.sem("own"), st.sem("m1_own")
        items = [(h, s, i) for h in range(HEADS) for s in range(STREAMS) for i in range(2)]
        m1 = Modulation(core, st, 1, [6], [7])
        ada_first = core.stream.start["ada1"]
        EVERY = 5

        def wait_normed(eng, n):
            if n % 3 == 2:
                eng.wait_ge(norm_act, n // 3 + 1)
            else:
                eng.wait_ge(norm_pool, n - (n + 1) // 3 + 1)

        def keys(s):
            return CTX if s == 0 else CTX + LAT

        def operands(h):
            base = HEAD * (h % 2)
            if h < NA_HEADS:
                return base, w.qaT[:, h // 2], w.kaT[:, h // 2]
            j = h - NA_HEADS
            return base, w.qbT[:, j // 2], w.kbT[:, j // (GQA_HEADS // GQA_KV)]

        def values(h, kt):
            if h < NA_HEADS:
                return w.va[:, kt, h * HEAD:(h + 1) * HEAD]
            g = (h - NA_HEADS) // (GQA_HEADS // GQA_KV)
            return w.kvb[:, kt, (GQA_KV + g) * HEAD:(GQA_KV + g + 1) * HEAD]

        with nc.Block() as block:
            @block.sync
            def _(sp):
                core.stream.feed(sp, core.stream.end["ab_w_out"], ada_first, m1.used)

            @block.tensor
            def _(pe):
                def score(n):
                    h, s, i = items[n]
                    t = 2 * s + i
                    base, qT, kT = operands(h)
                    if n >= 2:
                        pe.wait_ge(exp_ready, n - 1)
                    local = h < NA_HEADS and s == 1
                    mm = nc.tensor.matmul(core.ps[:, n % 2, 0:keys(s)], qT[base:base + HEAD, t * P:(t + 1) * P],
                                          kT[base:base + HEAD, 0:keys(s)], start=True, stop=not local,
                                          skip_group_check=True)
                    if local:
                        bias = w.bias[:, h, 2 - 2 * i:2 - 2 * i + NA_ROWS, :].rearrange("p u c -> p (u c)")
                        mm = nc.tensor.matmul(core.ps[:, n % 2, CTX:CTX + LAT], core.c("flip"), bias, start=False,
                                              stop=True, skip_group_check=True)
                    mm.then_inc(scored, 1)

                def turn(n):
                    h, s, i = items[n]
                    wait_normed(pe, n)
                    if n >= 2:
                        pe.wait_ge(pT_ready, n - 1)
                    for kt in range(keys(s) // P):
                        mm = nc.tensor.transpose(core.ps[:, 2 + n % 2, kt * P:(kt + 1) * P],
                                                 pn[:, n % 4, kt * P:(kt + 1) * P], core.c("ident"))
                    mm.then_inc(turned, 1)

                def weigh(m):
                    h, s, _ = items[2 * m]
                    base = HEAD * (h % 2)
                    pe.wait_ge(pT_ready, 2 * m + 2)
                    if m >= 2:
                        pe.wait_ge(out_done, m - 1)
                    for kt in range(keys(s) // P):
                        mm = nc.tensor.matmul(core.ps[base:base + HEAD, 4 + m % 2, 0:CTX], values(h, kt),
                                              pT[:, m % 4, kt, :], start=kt == 0, stop=kt == keys(s) // P - 1)
                    mm.then_inc(summed, 1)

                N = len(items)
                for n in range(N + 6):
                    if n < N:
                        score(n)
                    if 3 <= n < N + 3:
                        turn(n - 3)
                    if n >= 6 and n % 2 == 1:
                        weigh((n - 6) // 2)
                    if n % EVERY == 3 and n // EVERY < m1.BLOCKS:
                        m1.pe_sums(pe, n // EVERY)
                    if n >= EVERY and n % EVERY == 0 and n // EVERY - 1 < m1.BLOCKS:
                        m1.pe_columns(pe, n // EVERY - 1)
                weigh(N // 2 - 1) if (N + 5 - 6) // 2 < N // 2 - 1 else None

            @block.vector
            def _(dve):
                def take_max(n):
                    dve.wait_ge(scored, n + 1)
                    if n >= 4:
                        wait_normed(dve, n - 4)
                    nk = keys(items[n][1])
                    nc.vector.tensor_reduce(mx[:, n % 4, 0:1], core.ps[:, n % 2, 0:nk], AX, ALU.max).then_inc(own, 1)
                    dve.wait_ge(own, n + 1)
                    nc.vector.tensor_scalar(mx[:, n % 4, 1:2], mx[:, n % 4, 0:1], -1.0, None,
                                            ALU.mult).then_inc(max_ready, 1)

                def recip(n):
                    dve.wait_ge(exp_ready, n + 1)
                    nc.vector.reciprocal(mx[:, n % 4, 3:4], mx[:, n % 4, 2:3]).then_inc(recip_ready, 1)

                def take_turned(n):
                    nk = keys(items[n][1])
                    m = n // 2
                    dve.wait_ge(turned, n + 1)
                    if m >= 4:
                        dve.wait_ge(summed, m - 3)
                    nc.vector.tensor_copy(pT[:, m % 4, 0:nk // P, (n % 2) * P:(n % 2 + 1) * P],
                                          core.ps[:, 2 + n % 2, 0:nk].rearrange("p (k q) -> p k q", q=P)
                                          ).then_inc(pT_ready, 1)

                for n in range(len(items) + 3):
                    if n < len(items):
                        take_max(n)
                    if 1 <= n <= len(items):
                        recip(n - 1)
                    if n >= 3:
                        take_turned(n - 3)
                    if n % EVERY == 4 and n // EVERY < m1.BLOCKS:
                        m1.dve_part(dve, n // EVERY)
                    if n >= EVERY and n % EVERY == 1 and n // EVERY - 1 < m1.BLOCKS:
                        m1.dve_take(dve, n // EVERY - 1)
                m1.dve_finish(dve, Chain(dve, m1_own))

            @block.scalar
            def _(act):
                def take_out(m):
                    h, s, _ = items[2 * m]
                    base = HEAD * (h % 2)
                    act.wait_ge(summed, m + 1)
                    nc.scalar.copy(core.hT[base:base + HEAD, h // 2, s * CTX:(s + 1) * CTX],
                                   core.ps[base:base + HEAD, 4 + m % 2, 0:CTX]).then_inc(out_done, 1)

                def scale(n):
                    nk = keys(items[n][1])
                    act.wait_ge(recip_ready, n + 1)
                    if n >= 4:
                        act.wait_ge(turned, n - 3)
                    nc.scalar.activation(pn[:, n % 4, 0:nk], p[:, n % 4, 0:nk], ACT.Copy,
                                         scale=mx[:, n % 4, 3:4]).then_inc(norm_act, 1)

                N = len(items)
                for n in range(N):
                    nk = keys(items[n][1])
                    act.wait_ge(max_ready, n + 1)
                    nc.scalar.activation(p[:, n % 4, 0:nk], core.ps[:, n % 2, 0:nk], ACT.Exp, bias=mx[:, n % 4, 1:2],
                                         accum_out=mx[:, n % 4, 2:3]).then_inc(exp_ready, 1)
                    if n >= 2 and (n - 1) % 3 == 2:
                        scale(n - 1)
                    if n >= 9 and n % 2 == 1:
                        take_out((n - 9) // 2)
                for m in range((N - 1 - 9) // 2 + 1, N // 2):
                    take_out(m)

            @block.gpsimd
            def _(pool):
                for n in (n for n in range(len(items)) if n % 3 != 2):
                    nk = keys(items[n][1])
                    pool.wait_ge(recip_ready, n + 1)
                    if n >= 4:
                        pool.wait_ge(turned, n - 3)
                    nc.gpsimd.tensor_scalar(pn[:, n % 4, 0:nk], p[:, n % 4, 0:nk], mx[:, n % 4, 3:4], None,
                                            ALU.mult).then_inc(norm_pool, 1)


def project_out(core, a, layer, which_w, w, tiles, oT_at):
    nc = core.nc
    streams = sorted({t // 2 for t in tiles})
    with Stage(nc, f"out{layer}") as st:
        diag = st.sb("diag", [P, len(streams), KD, P])
        grow = st.sb("grow", [P, len(streams), D])
        prod = st.sb("prod", [P, 2, 512])
        diag_ready, spread, gates_ready = st.sem("diag_ready"), st.sem("spread"), st.sem("gates_ready")
        summed, added, own = st.sem("summed"), st.sem("added"), st.sem("own")
        first = core.stream.start[which_w]
        items = [(half, t) for half in range(2) for t in tiles]
        with nc.Block() as block:
            @block.tensor
            def _(pe):
                for i, s in enumerate(streams):
                    pe.wait_ge(diag_ready, i + 1)
                    for half in range(2):
                        for k in range(4):
                            mm = nc.tensor.matmul(core.ps[:, 6 + half, k * P:(k + 1) * P], core.c("ones"),
                                                  diag[:, i, 4 * half + k, :], start=True, stop=True)
                    mm.then_inc(spread, 1)
                    pe.wait_ge(gates_ready, i + 1)
                for n, (half, t) in enumerate(items):
                    wo = core.stream.take(pe, first + half)
                    if n >= 6:
                        pe.wait_ge(added, n - 5)
                    for k in range(KD):
                        mm = nc.tensor.matmul(core.ps[:, n % 6, :], core.hT[:, k, oT_at(t)], wo[:, k, :],
                                              start=k == 0, stop=k == KD - 1)
                    mm.then_inc(summed, 1)

            @block.vector
            def _(dve):
                for i, s in enumerate(streams):
                    for k in range(KD):
                        ins = nc.vector.tensor_scalar(diag[:, i, k, :], core.c("ident"),
                                                      core.gate_column(layer, 0, s, k), None, ALU.mult)
                    ins.then_inc(diag_ready, 1)
                for i, s in enumerate(streams):
                    dve.wait_ge(spread, i + 1)
                    nc.vector.tensor_copy(grow[:, i, :].rearrange("p (h c) -> p h c", h=2),
                                          core.ps[:, 6:8, :]).then_inc(gates_ready, 1)
                for n, (half, t) in enumerate(items):
                    dve.wait_ge(summed, n + 1)
                    dve.wait_ge(gates_ready, len(streams))
                    cols = slice(half * 512, (half + 1) * 512)
                    nc.vector.tensor_tensor(prod[:, n % 2, :], core.ps[:, n % 6, :],
                                            grow[:, streams.index(t // 2), cols], ALU.mult).then_inc(own, 1)
                    dve.wait_ge(own, n + 1)
                    nc.vector.tensor_tensor(core.x[:, t, cols], core.x[:, t, cols], prod[:, n % 2, :],
                                            ALU.add).then_inc(added, 1)


class EvenBuffers:

    def __init__(self, nc, stack):
        def sb(name, shape):
            return stack.enter_context(nc.sbuf_tensor(name, shape, F32))

        self.qaT, self.kaT = sb("qaT", [P, 4, 512]), sb("kaT", [P, 4, 512])
        self.va, self.qb = sb("va", [P, TILES, 512]), sb("qb", [P, TILES, 512])
        self.kvb = sb("kvb", [P, TILES, 2 * GQA_KV * HEAD])
        self.qbT, self.kbT = sb("qbT", [P, 4, 512]), sb("kbT", [P, GQA_KV, 512])
        self.bias = sb("na_bias", [P, NA_HEADS, REL, GRID_W])
        self.rpb_rows = nc.dram_tensor("rpb_rows", (NA_HEADS * (2 * WIN_ROWS - 1), P), F32, kind="Internal").ap()


def layer_even(core, a):
    with ExitStack() as stack:
        w = EvenBuffers(core.nc, stack)
        norm_transpose(core, 0, 0, [0, 1])
        project_even(core, a, w)
        qk_norm_rope(core, a, w)
        attend_even(core, w)
        project_out(core, a, 0, "ab_w_out", w, list(range(TILES)), lambda t: slice(t * P, (t + 1) * P))


def route(core, a, r, sw, layer, tiles):
    nc = core.nc
    NT, t0 = len(tiles), tiles[0]
    with Stage(nc, f"route{layer}") as st:
        hrow = st.sb("hrow", [P, NT, D])
        rw, wgu, wd, bias = sw.rw, sw.wgu, sw.wd, sw.bias
        score, picked, mask, gate = (st.sb(n, [P, NT, E]) for n in ("score", "picked", "mask", "gate"))
        work = st.sb("work", [P, NT, E])
        top = st.sb("top", [P, NT, 8])
        tot = st.sb("tot", [P, 2, NT])
        part = st.sb("part", [P, NT, E], BF16)
        cnt = st.sb("cnt", [P, 2])
        sg, hid = st.sb("sg", [P, 2, F]), st.sb("hid", [P, 2, F])
        hidT = st.sb("hidT", [P, 2, KF, P])
        rw_in, bias_in, wgu_in, wd_in = sw.rw_in, sw.bias_in, sw.wgu_in, sw.wd_in
        logits, e_ready, mask_ready, placed, counted = (
            st.sem(n) for n in ("logits", "e_ready", "mask_ready", "placed", "counted"))
        turned, taken, rows_out = st.sem("turned"), [st.sem("taken_dve"), st.sem("taken_act")], st.sem("rows_out")
        gu_ready, silu_ready, hid_ready = st.sem("gu_ready"), st.sem("silu_ready"), st.sem("hid_ready")
        hidT_turned, hidT_ready, down_ready = st.sem("hidT_turned"), st.sem("hidT_ready"), st.sem("down_ready")
        down_taken, own, parts_ready = st.sem("down_taken"), st.sem("own"), st.sem("parts_ready")
        gu_bank = lambda i: (4, 1)[i % 2]
        back = [(i, half) for i in range(NT) for half in range(2)]
        with nc.Block() as block:
            @block.sync
            def _(sp):
                r.load_first_experts(sp)
                for i in range(NT):
                    sp.wait_ge(taken[0], i + 1)
                    sp.wait_ge(taken[1], i + 1)
                    sp.dma_start(r.h_rows[i * P:(i + 1) * P, :], hrow[:, i, :]).then_inc(rows_out, 16)
                sp.wait_ge(rows_out, 16 * NT)

            @block.tensor
            def _(pe):
                def h(k, i):
                    return core.hT[:, k, (t0 + i) * P:(t0 + i + 1) * P]

                pe.wait_ge(rw_in, 16)
                for i in range(NT):
                    for k in range(KD):
                        mm = nc.tensor.matmul(core.ps[:, 0, i * E:(i + 1) * E], h(k, i), rw[:, k, :],
                                              start=k == 0, stop=k == KD - 1)
                mm.then_inc(logits, 1)
                for n, (i, half) in enumerate(back):
                    if n >= 2:
                        pe.wait_ge(taken[n % 2], (n - 2) // 2 + 1)
                    for k in range(4):
                        mm = nc.tensor.transpose(core.ps[:, 1 + n % 2, k * P:(k + 1) * P], h(4 * half + k, i),
                                                 core.c("ident"))
                    mm.then_inc(turned, 1)

                def gate_up(i):
                    pe.wait_ge(wgu_in, 32)
                    if i == 1:
                        pe.wait_ge(taken[0], NT)
                    if i >= 2:
                        pe.wait_ge(hid_ready, i - 1)
                    for k in range(KD):
                        mm = nc.tensor.matmul(core.ps[:, gu_bank(i), :], h(k, i), wgu[:, k].rearrange("p g f -> p (g f)"),
                                              start=k == 0, stop=k == KD - 1)
                    mm.then_inc(gu_ready, 1)

                def down(i):
                    pe.wait_ge(hid_ready, i + 1)
                    if i >= 1:
                        pe.wait_ge(hidT_ready, i)
                    for k in range(KF):
                        mm = nc.tensor.transpose(core.ps[:, 5, k * P:(k + 1) * P], hid[:, i % 2, k * P:(k + 1) * P],
                                                 core.c("ident"))
                    mm.then_inc(hidT_turned, 1)
                    pe.wait_ge(hidT_ready, i + 1)
                    pe.wait_ge(wd_in, 16)
                    if i >= 1:
                        pe.wait_ge(down_taken, i)
                    for half in range(2):
                        for k in range(KF):
                            mm = nc.tensor.matmul(core.ps[:, 6 + half, :], hidT[:, i % 2, k, :],
                                                  wd[:, k, half * 512:(half + 1) * 512], start=k == 0, stop=k == KF - 1)
                    mm.then_inc(down_ready, 1)

                gate_up(0)
                pe.wait_ge(mask_ready, 1)
                for i in range(NT):
                    for j in range(i + 1):
                        mm = nc.tensor.matmul(core.ps[:, 3, i * E:(i + 1) * E],
                                              core.c("before") if j == i else core.c("ones"), mask[:, j, :],
                                              start=j == 0, stop=j == i)
                mm.then_inc(placed, 1)
                for j in range(NT):
                    mm = nc.tensor.matmul(core.ps[:, 0, 0:E], core.c("ones"), mask[:, j, :], start=j == 0,
                                          stop=j == NT - 1)
                mm.then_inc(counted, 1)
                for i in range(1, NT):
                    gate_up(i)
                    down(i - 1)
                down(NT - 1)

            @block.scalar
            def _(act):
                act.wait_ge(logits, 1)
                nc.scalar.activation(score[:].rearrange("p t e -> p (t e)"), core.ps[:, 0, 0:NT * E], ACT.Exp,
                                     scale=-1.0).then_inc(e_ready, 1)
                for i in range(NT):
                    act.wait_ge(turned, 2 * i + 2)
                    nc.scalar.copy(hrow[:, i, 512:D], core.ps[:, 2, :]).then_inc(taken[1], 1)
                for i in range(NT):
                    act.wait_ge(gu_ready, i + 1)
                    if i >= 2:
                        act.wait_ge(hid_ready, i - 1)
                    nc.scalar.activation(sg[:, i % 2, :], core.ps[:, gu_bank(i), 0:F], ACT.Silu).then_inc(silu_ready, 1)

            @block.vector
            def _(dve):
                link = Chain(dve, own)
                dve.wait_ge(e_ready, 1)
                link(nc.vector.tensor_scalar(score[:], score[:], 1.0, None, ALU.add))
                link(nc.vector.reciprocal(score[:], score[:]))
                dve.wait_ge(bias_in, 16)
                link(nc.vector.tensor_tensor(picked[:], score[:], bias[:].rearrange("p (o e) -> p o e", o=1)
                                             .to_broadcast([P, NT, E]), ALU.add))
                for i in range(NT):
                    ins = nc.vector.max(top[:, i, :], picked[:, i, :])
                link(ins)
                for i in range(NT):
                    ins = nc.vector.match_replace(work[:, i, :], top[:, i, :], picked[:, i, :], MASKED)
                link(ins)
                nc.vector.tensor_tensor(mask[:], picked[:], work[:], ALU.not_equal).then_inc(mask_ready, 1)
                dve.wait_ge(mask_ready, 1)
                link(nc.vector.tensor_tensor(gate[:], score[:], mask[:], ALU.mult))
                link(nc.vector.tensor_reduce(tot[:, 0, :], gate[:], AX, ALU.add))
                link(nc.vector.reciprocal(tot[:, 1, :], tot[:, 0, :]))
                link(nc.vector.tensor_tensor(gate[:], gate[:], tot[:, 1, :].rearrange("p (t o) -> p t o", o=1)
                                             .to_broadcast([P, NT, E]), ALU.mult))
                link(nc.vector.tensor_scalar(gate[:], gate[:], ROUTED_SCALE, None, ALU.mult))
                for i in range(NT):
                    dve.wait_ge(turned, 2 * i + 1)
                    nc.vector.tensor_copy(hrow[:, i, 0:512], core.ps[:, 1, :]).then_inc(taken[0], 1)

                def hidden(i):
                    dve.wait_ge(silu_ready, i + 1)
                    nc.vector.tensor_tensor(hid[:, i % 2, :], sg[:, i % 2, :], core.ps[:, gu_bank(i), F:2 * F],
                                            ALU.mult).then_inc(hid_ready, 1)
                    dve.wait_ge(hidT_turned, i + 1)
                    nc.vector.tensor_copy(hidT[:, i % 2].rearrange("p k c -> p (k c)"),
                                          core.ps[:, 5, 0:F]).then_inc(hidT_ready, 1)
                    dve.wait_ge(down_ready, i + 1)
                    nc.vector.tensor_copy(r.shared[:, i, :].rearrange("p (h c) -> p h c", h=2),
                                          core.ps[:, 6:8, :]).then_inc(down_taken, 1)

                dve.wait_ge(placed, 1)
                pos = core.ps[:, 3, 0:NT * E].rearrange("p (t e) -> p t e", e=E)
                link(nc.vector.scalar_tensor_tensor(out=work[:], in0=pos, scalar=1.0, in1=mask[:], op0=ALU.add,
                                                    op1=ALU.mult))
                link(nc.vector.tensor_scalar(r.place[:], work[:], -1.0, None, ALU.add))
                dve.wait_ge(counted, 1)
                link(nc.vector.tensor_reduce(cnt[:, 0:1], core.ps[:, 0, 0:E], AX, ALU.max))
                link(nc.vector.tensor_copy(r.longest[:], cnt[:, 0:1]))
                for i in range(NT):
                    ins = nc.vector.tensor_tensor_scan(work[:, i, :], core.c("ones")[:, 0:E], mask[:, i, :], 0.0,
                                                       ALU.mult, ALU.add)
                link(ins)
                info = r.slot_info
                nc.vector.tensor_scalar(info[:, :, :, 2, 2], work[:], -1.0, None, ALU.add)
                link(nc.vector.tensor_copy(info[:, :, :, 0, 0], gate[:]))
                link(nc.vector.tensor_tensor(gate[:], gate[:], info[:, :, :, 0, 0], ALU.subtract))
                link(nc.vector.tensor_copy(info[:, :, :, 0, 1], gate[:]))
                link(nc.vector.tensor_tensor(gate[:], gate[:], info[:, :, :, 0, 1], ALU.subtract))
                link(nc.vector.tensor_copy(info[:, :, :, 0, 2], gate[:]))
                nc.vector.memset(info[:, :, :, 1, 2], 0.0)
                for i in range(NT):
                    for c, name in ((1, "tok"), (2, "dest")):
                        for s, v in ((0, core.c(name + "_hi")[:, i:i + 1]), (1, core.c(name + "_lo"))):
                            ins = nc.vector.tensor_copy(info[:, i, :, c, s], v.to_broadcast([P, E]))
                link(ins)
                for i in range(NT):
                    hidden(i)


class SharedWeights:

    def __init__(self, core, stack, a, layer):
        nc = core.nc

        def sb(name, shape):
            return stack.enter_context(nc.sbuf_tensor(f"{name}{layer}", shape, F32))

        self.a, self.layer = a, layer
        self.rw, self.bias = sb("rw", [P, KD, E]), sb("rbias", [P, E])
        self.wgu, self.wd = sb("sh_wgu", [P, KD, 2, F]), sb("sh_wd", [P, KF, D])
        self.rw_in, self.bias_in, self.wgu_in, self.wd_in = (
            nc.alloc_semaphore(f"{n}{layer}") for n in ("rw_in", "bias_in", "wgu_in", "wd_in"))

    def load(self, sp):
        a, layer = self.a, self.layer
        sp.dma_start(self.rw[:], a["router_w"][layer].rearrange("(k p) e -> p k e", p=P)).then_inc(self.rw_in, 16)
        sp.dma_start(self.bias[:], a["router_bias"][layer:layer + 1, :].to_broadcast([P, E])).then_inc(self.bias_in, 16)
        for i, name in enumerate(("shared_w_gate", "shared_w_up")):
            sp.dma_start(self.wgu[:, :, i, :], a[name][layer].rearrange("(k p) f -> p k f", p=P)).then_inc(self.wgu_in, 16)
        sp.dma_start(self.wd[:], a["shared_w_down"][layer].rearrange("(k p) d -> p k d", p=P)).then_inc(self.wd_in, 16)


class Routing:

    def __init__(self, core, stack, a, layer, NT):
        nc = core.nc

        def sb(name, shape, dt=F32):
            return stack.enter_context(nc.sbuf_tensor(f"{name}{layer}", shape, dt))

        self.place = sb("place", [P, NT, E])
        self.slot_info = sb("slot_info", [P, NT, E, 3, 3], BF16)
        self.shared = sb("shared", [P, NT, D])
        self.longest = sb("longest", [P, 1], I32)
        self.h_rows = nc.dram_tensor(f"h_rows{layer}", (NT * P, D), F32, kind="Internal").ap()
        self.wgu = core.wb[:].rearrange("p s (i n) -> p s i n", i=2)
        self.gu_in = [nc.alloc_semaphore(f"gu_in{layer}_{i}") for i in range(RING)]

        def grouped(t):
            return t[layer].rearrange("(g s) (p k) f -> s g p (k f)", s=GROUP, p=P)

        self.gate_src, self.up_src = grouped(a["expert_w_gate"]), grouped(a["expert_w_up"])
        self.down_src = grouped(a["expert_w_down"])
        self.y_rows = nc.dram_tensor(f"y_rows{layer}", (NT * P * TOP_K, D), F32, kind="Internal").ap()


    def load_first_experts(self, sp):
        for e in range(RING):
            for i, src in enumerate((self.gate_src, self.up_src)):
                sp.dma_start(self.wgu[:, e, i, :], src[e, 0]).then_inc(self.gu_in[e], 16)


RING = 4
GROUP = 8
GROUPS = E // GROUP


def experts(core, a, r, layer, tiles):
    nc = core.nc
    NT = len(tiles)
    T = NT * P
    with Stage(nc, f"moe{layer}") as st:
        wgu = r.wgu
        wd = st.sb("wd", [P, RING, KF * D])
        onehot = st.sb("onehot", [P, 2, NT, SLOTS], BF16)
        info = st.sb("info", [P, GROUP, 3])
        index = st.sb("index", [P, GROUP, 2], I32)
        xs = st.sb("xs", [P, RING, D])
        xT = st.sb("xT", [P, 2, KD, SLOTS])
        sg, hid = st.sb("sg", [P, 2, F]), st.sb("hid", [P, 2, F])
        hidT = st.sb("hidT", [P, 2, KF, SLOTS])
        y = st.sb("y", [P, 2, D])
        gu_in = r.gu_in
        d_in = [st.sem(f"d_in{i}") for i in range(RING)]
        gathered = [st.pool_sem(f"gathered{i}") for i in range(RING)]
        scattered = [st.pool_sem(f"scattered{i}") for i in range(2)]
        cleared, gathers, scatters = st.sem("cleared"), st.sem("gathers"), st.sem("scatters")
        hot_ready, info_sum, info_ready, index_ready = (
            st.sem(n) for n in ("hot_ready", "info_sum", "info_ready", "index_ready"))
        x_turned, xT_dve, xT_act = st.sem("x_turned"), st.sem("xT_dve"), st.sem("xT_act")
        gu_ready, silu_ready, hid_ready = st.sem("gu_ready"), st.sem("silu_ready"), st.sem("hid_ready")
        hid_turned, hidT_ready, down_ready = st.sem("hid_turned"), st.sem("hidT_ready"), st.sem("down_ready")
        y_dve, y_act = st.sem("y_dve"), st.sem("y_act")

        bounds = []

        def sp_step(sp, g, s, base, first):
            if not first:
                sp.wait_ge(down_ready, base + GROUP * g + s - RING + 1)
            def of(src):
                return src[s, g] if isinstance(g, int) else src[s, bass.ds(g, 1)].rearrange("o p n -> (o p) n")

            if not first:
                sp.dma_start(wgu[:, s % RING, 0, :], of(r.gate_src)).then_inc(gu_in[s % RING], 16)
                sp.dma_start(wgu[:, s % RING, 1, :], of(r.up_src)).then_inc(gu_in[s % RING], 16)
            sp.dma_start(wd[:, s % RING, :], of(r.down_src)).then_inc(d_in[s % RING], 16)

        def pool_gather(pool, g, s, base, first):
            n = base + GROUP * g + s
            if not first:
                pool.wait_ge(x_turned, n - RING + 1)
            pool.wait_ge(index_ready, n + 1)
            pool.sem_inc(gathers, 1)
            pool.indirect_dma_start(out=xs[:, s % RING, :], out_offset=None, in_=r.h_rows,
                                    in_offset=bass.IndirectOffsetOnAxis(ap=index[:, s, 0:1], axis=0),
                                    bounds_check=bounds[0], oob_is_err=False).then_inc(gathered[s % RING], 16)

        def pool_scatter(pool, g, s, base):
            n = base + GROUP * g + s
            pool.wait_ge(y_dve, n + 1)
            pool.wait_ge(y_act, n + 1)
            pool.sem_inc(scatters, 1)
            pool.indirect_dma_start(out=r.y_rows, out_offset=bass.IndirectOffsetOnAxis(ap=index[:, s, 1:2], axis=0),
                                    in_=y[:, s % 2, :], in_offset=None, bounds_check=bounds[1],
                                    oob_is_err=False).then_inc(scattered[s % 2], 16)

        def dve_hot(dve, g, s, base, block_at, first):
            n = base + GROUP * g + s
            if not first:
                dve.wait_ge(info_sum, n - 1)
            iota = core.c("iota")
            slots = iota[:, block_at * SLOTS:(block_at + 1) * SLOTS] if isinstance(block_at, int) else \
                iota[:, bass.ds(block_at * SLOTS, SLOTS)]
            e = GROUP * g + s
            for i in range(NT):
                where = r.place[:, i, e:e + 1] if isinstance(g, int) else r.place[:, i, bass.ds(e, 1)]
                ins = nc.vector.tensor_scalar(onehot[:, s % 2, i, :], slots, where, None, ALU.is_equal)
            ins.then_inc(hot_ready, 1)

        def pe_info(pe, g, s, base, first):
            n = base + GROUP * g + s
            pe.wait_ge(hot_ready, n + 1)
            if not first:
                pe.wait_ge(info_ready, n)
            flat = r.slot_info[:].rearrange("p t e c s -> p t (e c s)")
            for i in range(NT):
                at = 9 * (GROUP * g + s)
                rhs = flat[:, i, at:at + 9] if isinstance(g, int) else flat[:, i, bass.ds(at, 9)]
                mm = nc.tensor.matmul(core.ps[:, 7, 0:9], onehot[:, s % 2, i, :], rhs, start=i == 0, stop=i == NT - 1)
            mm.then_inc(info_sum, 1)

        def dve_info(dve, g, s, base, first):
            n = base + GROUP * g + s
            dve.wait_ge(info_sum, n + 1)
            if not first:
                dve.wait_ge(scattered[s % 2], 8 * (base + GROUP * g) + 16 * (s // 2) + 16 - 8 * GROUP)
            nc.vector.tensor_reduce(info[:, s, :], core.ps[:, 7, 0:9].rearrange("p (c s) -> p c s", s=3), AX,
                                    ALU.add).then_inc(info_ready, 1)
            dve.wait_ge(info_ready, n + 1)
            nc.vector.tensor_scalar(index[:, s, :], info[:, s, 1:3], float(BIG), None, ALU.add).then_inc(index_ready, 1)

        def pe_turn(pe, g, s, base, first):
            n = base + GROUP * g + s
            pe.wait_ge(gathered[s % RING], 4 * (base + GROUP * g) + 16 * (s // RING) + 16)
            if not first:
                pe.wait_ge(xT_dve, n)
                pe.wait_ge(xT_act, n)
            for k in range(KD):
                mm = nc.tensor.transpose(core.ps[:, 4 + k // 4, (k % 4) * P:(k % 4 + 1) * P],
                                         xs[:, s % RING, k:D:KD], core.c("ident"))
            mm.then_inc(x_turned, 1)

        def take_x(eng, bank, g, s, base, first):
            n = base + GROUP * g + s
            eng.wait_ge(x_turned, n + 1)
            if not first:
                eng.wait_ge(gu_ready, n - 1)
            out = xT[:, s % 2, 4 * bank:4 * bank + 4, :].rearrange("p k c -> p (k c)")
            if bank == 0:
                nc.vector.tensor_copy(out, core.ps[:, 4, :]).then_inc(xT_dve, 1)
            else:
                nc.scalar.copy(out, core.ps[:, 5, :]).then_inc(xT_act, 1)

        def pe_gate_up(pe, g, s, base, first):
            n = base + GROUP * g + s
            pe.wait_ge(gu_in[s % RING], 8 * (base + GROUP * g) + 32 * (s // RING) + 32)
            pe.wait_ge(xT_dve, n + 1)
            pe.wait_ge(xT_act, n + 1)
            if not first:
                pe.wait_ge(hid_ready, n - 1)
            w = wgu[:, s % RING].rearrange("p i (k f) -> p k i f", f=F)
            for k in range(KD):
                mm = nc.tensor.matmul(core.ps[:, s % 2, :], xT[:, s % 2, k, :], w[:, k], start=k == 0,
                                      stop=k == KD - 1)
            mm.then_inc(gu_ready, 1)

        def act_silu(act, g, s, base, first):
            n = base + GROUP * g + s
            act.wait_ge(gu_ready, n + 1)
            if not first:
                act.wait_ge(hid_ready, n - 1)
            nc.scalar.activation(sg[:, s % 2, :], core.ps[:, s % 2, 0:F], ACT.Silu).then_inc(silu_ready, 1)

        def dve_hidden(dve, g, s, base, first):
            n = base + GROUP * g + s
            dve.wait_ge(silu_ready, n + 1)
            if not first:
                dve.wait_ge(hid_turned, n - 1)
            nc.vector.tensor_tensor(hid[:, s % 2, :], sg[:, s % 2, :], core.ps[:, s % 2, F:2 * F],
                                    ALU.mult).then_inc(hid_ready, 1)

        def pe_turn_hidden(pe, g, s, base, first):
            n = base + GROUP * g + s
            pe.wait_ge(hid_ready, n + 1)
            if not first:
                pe.wait_ge(hidT_ready, n)
            for k in range(KF):
                mm = nc.tensor.transpose(core.ps[:, 6, k * P:(k + 1) * P], hid[:, s % 2, k:F:KF], core.c("ident"))
            mm.then_inc(hid_turned, 1)

        def dve_take_hidden(dve, g, s, base, first):
            n = base + GROUP * g + s
            dve.wait_ge(hid_turned, n + 1)
            if not first:
                dve.wait_ge(down_ready, n - 1)
            nc.vector.tensor_copy(hidT[:, s % 2].rearrange("p k c -> p (k c)"), core.ps[:, 6, 0:F]).then_inc(hidT_ready, 1)

        def pe_down(pe, g, s, base, first):
            n = base + GROUP * g + s
            pe.wait_ge(hidT_ready, n + 1)
            pe.wait_ge(d_in[s % RING], 4 * (base + GROUP * g) + 16 * (s // RING) + 16)
            if not first:
                pe.wait_ge(y_dve, n)
                pe.wait_ge(y_act, n)
            for half in range(2):
                for k in range(KF):
                    mm = nc.tensor.matmul(core.ps[:, 2 + half, :], hidT[:, s % 2, k, :],
                                          wd[:, s % RING, k * D + half * 512:k * D + half * 512 + 512], start=k == 0,
                                          stop=k == KF - 1)
            mm.then_inc(down_ready, 1)

        def take_y(eng, half, g, s, base, first):
            n = base + GROUP * g + s
            eng.wait_ge(down_ready, n + 1)
            if not first:
                eng.wait_ge(scattered[s % 2], 8 * (base + GROUP * g) + 16 * (s // 2))
            out, src, gate = y[:, s % 2, half * 512:(half + 1) * 512], core.ps[:, 2 + half, :], info[:, s, 0:1]
            if half == 0:
                nc.vector.tensor_scalar(out, src, gate, None, ALU.mult).then_inc(y_dve, 1)
            else:
                nc.scalar.activation(out, src, ACT.Copy, scale=gate).then_inc(y_act, 1)

        def at(g, s, ahead):
            return g + (s + ahead) // GROUP, (s + ahead) % GROUP

        def run(eng, step):
            for s in range(GROUP):
                step(0, s, s)
            with eng.Fori(1, GROUPS - 1) as g:
                for s in range(GROUP):
                    step(g, s, None)
            for s in range(GROUP):
                step(GROUPS - 1, s, E - GROUP + s)

        def inside(e, ahead):
            return e is None or 0 <= e + ahead < E

        def early(e, ahead, ring, base_is_zero):
            return base_is_zero and e is not None and e + ahead < ring

        def sp_pass(sp, base, z):
            def step(g, s, e):
                sp_step(sp, g, s, base, early(e, 0, RING, z))
            run(sp, step)

        def pool_pass(pool, base, z):
            for e in range(2):
                pool_gather(pool, 0, e, base, early(e, 0, RING, z))

            def step(g, s, e):
                if inside(e, 2):
                    pool_gather(pool, *at(g, s, 2), base, early(e, 2, RING, z))
                if inside(e, -2):
                    pool_scatter(pool, *at(g, s, -2), base)
            run(pool, step)
            for s in range(GROUP - 2, GROUP):
                pool_scatter(pool, GROUPS - 1, s, base)

        def dve_pass(dve, base, z, blk):
            def hot(e, g, s):
                dve_hot(dve, g, s, base, blk, early(e, 0, 2, z))

            def slots(e, g, s):
                dve_info(dve, g, s, base, early(e, 0, GROUP, z))

            for e in range(2):
                hot(e, 0, e)
                slots(e, 0, e)
            hot(2, 0, 2)
            take_x(dve, 0, 0, 0, base, z)

            def step(g, s, e):
                up = (lambda k: None) if e is None else (lambda k: e + k)
                if inside(e, 2):
                    slots(up(2), *at(g, s, 2))
                if inside(e, 3):
                    hot(up(3), *at(g, s, 3))
                if inside(e, 1):
                    take_x(dve, 0, *at(g, s, 1), base, early(e, 1, 2, z))
                dve_hidden(dve, g, s, base, early(e, 0, 2, z))
                if inside(e, -1):
                    take_y(dve, 0, *at(g, s, -1), base, early(e, -1, 2, z))
                dve_take_hidden(dve, g, s, base, early(e, 0, 2, z))
            run(dve, step)
            take_y(dve, 0, GROUPS - 1, GROUP - 1, base, False)

        def act_pass(act, base, z):
            take_x(act, 1, 0, 0, base, z)

            def step(g, s, e):
                if inside(e, 1):
                    take_x(act, 1, *at(g, s, 1), base, early(e, 1, 2, z))
                act_silu(act, g, s, base, early(e, 0, 2, z))
                if inside(e, -1):
                    take_y(act, 1, *at(g, s, -1), base, early(e, -1, 2, z))
            run(act, step)
            take_y(act, 1, GROUPS - 1, GROUP - 1, base, False)

        def pe_pass(pe, base, z):
            for e in range(2):
                pe_info(pe, 0, e, base, early(e, 0, 1, z))
            pe_turn(pe, 0, 0, base, z)

            def step(g, s, e):
                if inside(e, 2):
                    pe_info(pe, *at(g, s, 2), base, early(e, 2, 1, z))
                if inside(e, 1):
                    pe_turn(pe, *at(g, s, 1), base, early(e, 1, 1, z))
                pe_gate_up(pe, g, s, base, early(e, 0, 2, z))
                if inside(e, -1):
                    pe_down(pe, *at(g, s, -1), base, early(e, -1, 1, z))
                pe_turn_hidden(pe, g, s, base, early(e, 0, 1, z))
            run(pe, step)
            pe_down(pe, GROUPS - 1, GROUP - 1, base, False)

        def further(eng, body):
            longest = eng.value_load(r.longest[0:1, 0:1], min_val=0, max_val=T)
            with eng.If(longest > SLOTS):
                with eng.Fori(1, T // SLOTS) as b:
                    body(b * E, b)

        with nc.Block() as block:
            @block.sync
            def _(sp):
                sp_pass(sp, 0, True)
                further(sp, lambda base, b: sp_pass(sp, base, False))

            @block.gpsimd
            def _(pool):
                last_row, last_out = pool.to_reg(T - 1), pool.to_reg(T * TOP_K - 1)
                bounds[:] = [last_row, last_out]
                pool.wait_ge(cleared, 1)
                pool_pass(pool, 0, True)
                further(pool, lambda base, b: pool_pass(pool, base, False))
                for i in range(2):
                    pool.wait_ge(scattered[i], 16 * (E // 2))

            @block.scalar
            def _(act):
                act_pass(act, 0, True)
                further(act, lambda base, b: act_pass(act, base, False))

            @block.vector
            def _(dve):
                nc.vector.memset(xs[:], 0.0).then_inc(cleared, 1)
                dve_pass(dve, 0, True, 0)
                further(dve, lambda base, b: dve_pass(dve, base, False, b))

            @block.tensor
            def _(pe):
                pe_pass(pe, 0, True)
                further(pe, lambda base, b: pe_pass(pe, base, False))


def combine(core, r, layer, tiles):
    nc = core.nc
    streams = sorted({t // 2 for t in tiles})
    with Stage(nc, f"combine{layer}") as st:
        yr = st.sb("yr", [P, 2, TOP_K, D])
        diag = st.sb("diag", [P, KD, P])
        grow = st.sb("grow", [P, len(streams), D])
        y_in = [st.sem("y_in0"), st.sem("y_in1")]
        diag_ready, spread, gates_ready = st.sem("diag_ready"), st.sem("spread"), st.sem("gates_ready")
        own, summed, pool_own, pool_summed = st.sem("own"), st.sem("summed"), st.sem("pool_own"), st.sem("pool_summed")
        y_view = r.y_rows.rearrange("(t p k) d -> t p k d", p=P, k=TOP_K)
        with nc.Block() as block:
            @block.sync
            def _(sp):
                for i in range(len(tiles)):
                    if i >= 2:
                        sp.wait_ge(summed, i - 1)
                    sp.dma_start(yr[:, i % 2], y_view[i]).then_inc(y_in[i % 2], 16)
                if layer == 0:
                    core.stream.feed(sp, core.stream.start["diff_w_in"] + STREAM, core.stream.start["diff_w_in"])

            @block.tensor
            def _(pe):
                for i in range(len(streams)):
                    pe.wait_ge(diag_ready, i + 1)
                    if i >= 1:
                        pe.wait_ge(gates_ready, i)
                    for k in range(KD):
                        mm = nc.tensor.matmul(core.ps[:, k // 4, (k % 4) * P:(k % 4 + 1) * P], core.c("ones"),
                                              diag[:, k, :], start=True, stop=True)
                    mm.then_inc(spread, 1)

            @block.gpsimd
            def _(pool):
                link = Chain(pool, pool_own)
                for i in range(len(tiles)):
                    pool.wait_ge(y_in[i % 2], 16 * (i // 2 + 1))
                    v = yr[:, i % 2]
                    link(nc.gpsimd.tensor_tensor(v[:, 0], v[:, 0], v[:, 1], ALU.add))
                    nc.gpsimd.tensor_tensor(v[:, 0], v[:, 0], v[:, 2], ALU.add).then_inc(pool_summed, 1)

            @block.vector
            def _(dve):
                link = Chain(dve, own)
                for i, s in enumerate(streams):
                    if i >= 1:
                        dve.wait_ge(spread, i)
                    for k in range(KD):
                        ins = nc.vector.tensor_scalar(diag[:, k, :], core.c("ident"), core.gate_column(layer, 1, s, k),
                                                      None, ALU.mult)
                    ins.then_inc(diag_ready, 1)
                    dve.wait_ge(spread, i + 1)
                    nc.vector.tensor_copy(grow[:, i, :].rearrange("p (h c) -> p h c", h=2),
                                          core.ps[:, 0:2, :]).then_inc(gates_ready, 1)
                for i, t in enumerate(tiles):
                    dve.wait_ge(y_in[i % 2], 16 * (i // 2 + 1))
                    v = yr[:, i % 2]
                    link(nc.vector.tensor_tensor(v[:, 4:6], v[:, 4:6], v[:, 6:8], ALU.add))
                    nc.vector.tensor_tensor(v[:, 3], v[:, 3], r.shared[:, i, :], ALU.add)
                    link(nc.vector.tensor_tensor(v[:, 4], v[:, 4], v[:, 5], ALU.add))
                    link(nc.vector.tensor_tensor(v[:, 3], v[:, 3], v[:, 4], ALU.add))
                    dve.wait_ge(pool_summed, i + 1)
                    link(nc.vector.tensor_tensor(v[:, 3], v[:, 3], v[:, 0], ALU.add))
                    if i == 0:
                        dve.wait_ge(gates_ready, len(streams))
                    link(nc.vector.tensor_tensor(v[:, 3], v[:, 3], grow[:, streams.index(t // 2), :], ALU.mult))
                    nc.vector.tensor_tensor(core.x[:, t, :], core.x[:, t, :], v[:, 3], ALU.add).then_inc(summed, 1)


def moe(core, a, layer, tiles):
    with ExitStack() as stack:
        r = Routing(core, stack, a, layer, len(tiles))
        with ExitStack() as inner:
            sw = SharedWeights(core, inner, a, layer)
            norm_transpose(core, layer, 1, sorted({t // 2 for t in tiles}), sw.load)
            route(core, a, r, sw, layer, tiles)
        experts(core, a, r, layer, tiles)
        combine(core, r, layer, tiles)


def project_odd(core, a, w):
    nc = core.nc
    COLS = BLOCK
    first = core.stream.start["diff_w_in"]
    with Stage(nc, "proj1") as st:
        summed, taken = st.sem("summed"), [st.sem("taken_dve"), st.sem("taken_act")]
        blocks = 3 * D // COLS
        items = [(b, t) for b in range(blocks) for t in (range(2, TILES) if b < 2 else range(TILES))]

        def target(b, t):
            cols = slice((b % 2) * COLS, (b % 2 + 1) * COLS)
            return w.q[:, t - 2, cols] if b < 2 else (w.k if b < 4 else w.v)[:, t, cols]

        with nc.Block() as block:
            @block.sync
            def _(sp):
                core.stream.feed(sp, core.stream.end["diff_w_out"], first,
                                 lambda b: (summed, sum(1 for x, _ in items if x <= b)))

            @block.tensor
            def _(pe):
                for n, (b, t) in enumerate(items):
                    wb = core.stream.take(pe, first + b)
                    if n >= 8:
                        pe.wait_ge(taken[n % 2], (n - 8) // 2 + 1)
                    for k in range(KD):
                        mm = nc.tensor.matmul(core.ps[:, n % 8, :], core.hT[:, k, t * P:(t + 1) * P],
                                              wb[:, k, :], start=k == 0, stop=k == KD - 1)
                    mm.then_inc(summed, 1)

            @block.vector
            def _(dve):
                for n in range(0, len(items), 2):
                    dve.wait_ge(summed, n + 1)
                    nc.vector.tensor_scalar(target(*items[n]), core.ps[:, n % 8, :],
                                            SCALE if items[n][0] < 2 else 1.0, None, ALU.mult).then_inc(taken[0], 1)

            @block.scalar
            def _(act):
                for n in range(1, len(items), 2):
                    act.wait_ge(summed, n + 1)
                    nc.scalar.activation(target(*items[n]), core.ps[:, n % 8, :], ACT.Copy,
                                         scale=SCALE if items[n][0] < 2 else 1.0).then_inc(taken[1], 1)


def rope_odd(core, a, w):
    nc = core.nc
    with Stage(nc, "rope1") as st:
        tmp = st.sb("tmp", [P, 4, 16 * ROPE])
        lam = st.sb("lam", [P, 4, HEAD])
        dots = st.sb("dots", [P, 4])
        lam_in, own, rotated = st.sem("lam_in"), st.sem("own"), st.sem("rotated")
        dots_ready, exps_ready = st.sem("dots_ready"), st.sem("exps_ready")
        turned, taken = st.sem("turned"), [st.sem("taken_dve"), st.sem("taken_act")]
        items = [("k", c, 0) for c in range(KD)] + [("k", c, 1) for c in range(KD)] + [("q", c, 1) for c in range(KD)]

        def target(kind, c, s):
            return w.kT[:, c, s * CTX:(s + 1) * CTX] if kind == "k" else w.qT[:, c, :]

        with nc.Block() as block:
            @block.sync
            def _(sp):
                for i, name in enumerate(("diff_lq1", "diff_lk1", "diff_lq2", "diff_lk2")):
                    sp.dma_start(lam[:, i, :], a[name].to_broadcast([P, HEAD])).then_inc(lam_in, 16)
                sp.dma_start(w.sub_gain[:], a["diff_sub_gain"].to_broadcast([P, 2 * HEAD])).then_inc(lam_in, 16)

            @block.tensor
            def _(pe):
                for n, (kind, c, s) in enumerate(items):
                    if n == KD:
                        pe.wait_ge(rotated, 2)
                    if n == 2 * KD:
                        pe.wait_ge(rotated, 4)
                    if n >= 8:
                        pe.wait_ge(taken[n % 2], (n - 8) // 2 + 1)
                    for j in range(2):
                        src = w.k[:, 2 * s + j] if kind == "k" else w.q[:, j]
                        mm = nc.tensor.transpose(core.ps[:, n % 8, j * P:(j + 1) * P], src[:, c * P:(c + 1) * P],
                                                 core.c("ident"))
                    mm.then_inc(turned, 1)

            @block.scalar
            def _(act):
                act.wait_ge(dots_ready, 1)
                nc.scalar.activation(dots[:, 2:4], dots[:, 0:2], ACT.Exp).then_inc(exps_ready, 1)
                for n in range(1, len(items), 2):
                    act.wait_ge(turned, n + 1)
                    nc.scalar.copy(target(*items[n]), core.ps[:, n % 8, 0:CTX]).then_inc(taken[1], 1)

            @block.vector
            def _(dve):
                link = Chain(dve, own)

                def take(n):
                    dve.wait_ge(turned, n + 1)
                    nc.vector.tensor_copy(target(*items[n]), core.ps[:, n % 8, 0:CTX]).then_inc(taken[0], 1)

                for x in (w.k[:, 2:4], w.q):
                    for t in range(2):
                        cos = core.c("cos")[:, t * ROPE:(t + 1) * ROPE]
                        sin = core.c("sin")[:, t * ROPE:(t + 1) * ROPE]
                        rotate(nc, link, x[:, t, :].rearrange("p (h r two) -> p h r two", r=ROPE, two=2), tmp, cos, sin)
                        nc.vector.engine_nop().then_inc(rotated, 1)
                        for n in range(0, KD, 2):
                            if x is not w.q and t == 0:
                                take(n)
                dve.wait_ge(lam_in, 16 * 5)
                for i in range(2):
                    link(nc.vector.tensor_tensor(lam[:, 2 * i, :], lam[:, 2 * i, :], lam[:, 2 * i + 1, :], ALU.mult))
                    ins = nc.vector.tensor_reduce(dots[:, i:i + 1], lam[:, 2 * i, :], AX, ALU.add)
                ins.then_inc(dots_ready, 1)
                link(nc.vector.tensor_scalar(w.sub_gain[:], w.sub_gain[:], 1.0 - LAM_INIT, None, ALU.mult))
                dve.wait_ge(exps_ready, 1)
                link(nc.vector.tensor_tensor(dots[:, 0:1], dots[:, 3:4], dots[:, 2:3], ALU.subtract))
                link(nc.vector.tensor_scalar(w.neg_lam[:], dots[:, 0:1], -LAM_INIT, None, ALU.add))
                for n in range(KD, len(items), 2):
                    take(n)


def attend_odd(core, w):
    nc = core.nc
    KEYS = CTX + LAT
    with Stage(nc, "attn1") as st:
        p = st.sb("p", [P, 4, 2, KEYS])
        pd = st.sb("pd", [P, 2, KEYS])
        pT = st.sb("pT", [P, 2, 4, P])
        mx = st.sb("mx", [P, 4, 2, 2])
        sm = st.sb("sm", [P, 4, 4])
        sc = lambda n: (0, 6)[n % 2]
        names = ("scored", "max_own", "max_ready", "exp_ready", "recip_ready", "scaled", "mixed", "turned",
                 "pT_ready", "summed", "o_taken")
        (scored, max_own, max_ready, exp_ready, recip_ready, scaled, mixed, turned, pT_ready, summed,
         o_taken) = (st.sem(n) for n in names)
        items = [(h, t) for h in range(DIFF_HEADS) for t in range(2)]
        N = len(items)
        with nc.Block() as block:
            @block.tensor
            def _(pe):
                def score(n):
                    h, t = items[n]
                    if n >= 2:
                        pe.wait_ge(exp_ready, n - 1)
                    for c in range(2):
                        base = HEAD * c
                        mm = nc.tensor.matmul(core.ps[:, sc(n) + c, :], w.qT[base:base + HEAD, h, t * P:(t + 1) * P],
                                              w.kT[base:base + HEAD, h, :], start=True, stop=True)
                    mm.then_inc(scored, 1)

                def turn(n):
                    pe.wait_ge(mixed, n + 1)
                    if n >= 2:
                        pe.wait_ge(pT_ready, n - 1)
                    for kt in range(4):
                        mm = nc.tensor.transpose(core.ps[:, 2 + n % 2, kt * P:(kt + 1) * P],
                                                 pd[:, n % 2, kt * P:(kt + 1) * P], core.c("ident"))
                    mm.then_inc(turned, 1)

                def weigh(n):
                    h, t = items[n]
                    pe.wait_ge(pT_ready, n + 1)
                    if n >= 2:
                        pe.wait_ge(o_taken, n - 1)
                    for kt in range(4):
                        mm = nc.tensor.matmul(core.ps[:, 4 + n % 2, 0:P], pT[:, n % 2, kt, :],
                                              w.v[:, kt, h * P:(h + 1) * P], start=kt == 0, stop=kt == 3)
                    mm.then_inc(summed, 1)

                for n in range(N + 4):
                    if n < N:
                        score(n)
                    if 3 <= n < N + 3:
                        turn(n - 3)
                    if 4 <= n:
                        weigh(n - 4)

            @block.scalar
            def _(act):
                def exps(n):
                    if n >= 4:
                        act.wait_ge(mixed, n - 3)
                    act.wait_ge(max_ready, n + 1)
                    for c in range(2):
                        ins = nc.scalar.activation(p[:, n % 4, c, :], core.ps[:, sc(n) + c, :], ACT.Exp,
                                                   bias=mx[:, n % 4, 1, c:c + 1], accum_out=sm[:, n % 4, c:c + 1])
                    ins.then_inc(exp_ready, 1)

                def take_turned(n):
                    act.wait_ge(turned, n + 1)
                    if n >= 2:
                        act.wait_ge(summed, n - 1)
                    nc.scalar.copy(pT[:, n % 2].rearrange("p k q -> p (k q)"), core.ps[:, 2 + n % 2, :]).then_inc(pT_ready, 1)

                for n in range(N + 3):
                    if n < N:
                        exps(n)
                    if n >= 3:
                        take_turned(n - 3)

            @block.gpsimd
            def _(pool):
                for n in range(N):
                    pool.wait_ge(recip_ready, n + 1)
                    nc.gpsimd.tensor_scalar(p[:, n % 4, 1, :], p[:, n % 4, 1, :], sm[:, n % 4, 3:4], w.neg_lam[:, 0:1],
                                            ALU.mult, ALU.mult).then_inc(scaled, 1)

            @block.vector
            def _(dve):
                def take_max(n):
                    dve.wait_ge(scored, n + 1)
                    if n >= 4:
                        dve.wait_ge(exp_ready, n - 3)
                    nc.vector.tensor_reduce(mx[:, n % 4, 0, :], core.ps[:, sc(n):sc(n) + 2, :], AX, ALU.max).then_inc(max_own, 1)
                    dve.wait_ge(max_own, n + 1)
                    nc.vector.tensor_scalar(mx[:, n % 4, 1, :], mx[:, n % 4, 0, :], -1.0, None, ALU.mult).then_inc(max_ready, 1)

                def recip(n):
                    dve.wait_ge(exp_ready, n + 1)
                    nc.vector.reciprocal(sm[:, n % 4, 2:4], sm[:, n % 4, 0:2]).then_inc(recip_ready, 1)

                def mix(n):
                    dve.wait_ge(scaled, n + 1)
                    if n >= 2:
                        dve.wait_ge(turned, n - 1)
                    nc.vector.scalar_tensor_tensor(out=pd[:, n % 2, :], in0=p[:, n % 4, 0, :], scalar=sm[:, n % 4, 2:3],
                                                   in1=p[:, n % 4, 1, :], op0=ALU.mult, op1=ALU.add).then_inc(mixed, 1)

                def take_out(n):
                    h, t = items[n]
                    dve.wait_ge(summed, n + 1)
                    nc.vector.tensor_copy(w.o[:, t, h, :], core.ps[:, 4 + n % 2, 0:P]).then_inc(o_taken, 1)

                for n in range(N + 5):
                    if n < N:
                        take_max(n)
                    if 1 <= n < N + 1:
                        recip(n - 1)
                    if 2 <= n < N + 2:
                        mix(n - 2)
                    if 5 <= n:
                        take_out(n - 5)


def norm_heads(core, w):
    nc = core.nc
    H = DIFF_HEADS
    with Stage(nc, "subnorm") as st:
        sq = st.sb("sq", [P, 2 * H, 2 * HEAD])
        rs = st.sb("rs", [P, 4, 2 * H])
        own, var_ready, root_ready, o_ready, turned, taken = (
            st.sem(n) for n in ("own", "var_ready", "root_ready", "o_ready", "turned", "taken"))
        o = w.o[:].rearrange("p t h d -> p (t h) d")
        with nc.Block() as block:
            @block.vector
            def _(dve):
                link = Chain(dve, own)
                link(nc.vector.tensor_tensor(sq[:], o, o, ALU.mult))
                link(nc.vector.tensor_reduce(rs[:, 0, :], sq[:], AX, ALU.add))
                nc.vector.tensor_scalar(rs[:, 1, :], rs[:, 0, :], 1.0 / P, EPS, ALU.mult, ALU.add).then_inc(var_ready, 1)
                dve.wait_ge(root_ready, 1)
                link(nc.vector.reciprocal(rs[:, 3, :], rs[:, 2, :]))
                for t in range(2):
                    for h in range(H):
                        n = t * H + h
                        ins = nc.vector.scalar_tensor_tensor(out=sq[:, n, :], in0=o[:, n, :], scalar=rs[:, 3, n:n + 1],
                                                             in1=w.sub_gain[:], op0=ALU.mult, op1=ALU.mult)
                    ins.then_inc(o_ready, 1)
                for n in range(4):
                    dve.wait_ge(turned, n + 1)
                    t, half = n // 2, n % 2
                    nc.vector.tensor_copy(core.hT[:, 4 * half:4 * half + 4, t * P:(t + 1) * P],
                                          core.ps[:, n, :].rearrange("p (h q) -> p h q", q=P)).then_inc(taken, 1)

            @block.scalar
            def _(act):
                act.wait_ge(var_ready, 1)
                nc.scalar.activation(rs[:, 2, :], rs[:, 1, :], ACT.Sqrt).then_inc(root_ready, 1)

            @block.tensor
            def _(pe):
                for n in range(4):
                    pe.wait_ge(o_ready, n // 2 + 1)
                    for i in range(4):
                        mm = nc.tensor.transpose(core.ps[:, n, i * P:(i + 1) * P], sq[:, 4 * n + i, :], core.c("ident"))
                    mm.then_inc(turned, 1)


class OddBuffers:
    def __init__(self, nc, stack):
        def sb(name, shape):
            return stack.enter_context(nc.sbuf_tensor(name, shape, F32))

        self.q = sb("q1", [P, 2, D])
        self.k, self.v = sb("k1", [P, TILES, D]), sb("v1", [P, TILES, D])
        self.qT, self.kT = sb("qT1", [P, KD, LAT]), sb("kT1", [P, KD, CTX + LAT])
        self.o = sb("o1", [P, 2, DIFF_HEADS, 2 * HEAD])
        self.sub_gain = sb("sub_gain", [P, 2 * HEAD])
        self.neg_lam = sb("neg_lam", [P, 1])


def layer_odd(core, a):
    with ExitStack() as stack:
        w = OddBuffers(core.nc, stack)
        norm_transpose(core, 1, 0, [0, 1])
        project_odd(core, a, w)
        rope_odd(core, a, w)
        attend_odd(core, w)
        norm_heads(core, w)
        project_out(core, a, 1, "diff_w_out", w, [2, 3], lambda t: slice((t - 2) * P, (t - 1) * P))


def finish(core, a, out):
    nc = core.nc
    with Stage(nc, "final") as st:
        xn = st.sb("xn", [P, 2, D])
        gain = st.sb("gain", [P, D])
        ss, rs = st.sb("ss", [P, 2]), st.sb("rs", [P, 3, 2])
        sq_ready, var_ready, root_ready = st.sem("sq"), st.sem("var"), st.sem("root")
        row_ready, own, gain_in, done, stored = (st.sem(n) for n in ("row", "own", "gain_in", "done", "stored"))
        on_act, on_dve = rms_rows(core, [2, 3], xn, ss, rs, sq_ready, root_ready, var_ready)
        with nc.Block() as block:
            @block.sync
            def _(sp):
                sp.dma_start(gain[:], a["final_norm"].rearrange("(o d) -> o d", o=1).to_broadcast([P, D])).then_inc(gain_in, 16)
                for i in range(2):
                    sp.wait_ge(done, i + 1)
                    sp.dma_start(out[0, i * P:(i + 1) * P, :], xn[:, i, :]).then_inc(stored, 16)
                sp.wait_ge(stored, 32)

            @block.scalar
            def _(act):
                on_act(act)

            @block.vector
            def _(dve):
                link = Chain(dve, own)
                on_dve(dve, link, row_ready)
                dve.wait_ge(gain_in, 16)
                for i in range(2):
                    dve.wait_ge(row_ready, i + 1)
                    nc.vector.tensor_tensor(xn[:, i, :], xn[:, i, :], gain[:], ALU.mult).then_inc(done, 1)


def backbone(nc, a, out):
    with ExitStack() as ctx:
        core = Core(nc, ctx, a)
        modulation(core, a)
        layer_even(core, a)
        moe(core, a, 0, list(range(TILES)))
        layer_odd(core, a)
        moe(core, a, 1, [2, 3])
        finish(core, a, out)


_INS = ["x", "c", "ctx", "c_ctx", "ada_w", "ada_b", "norm_mix", "norm_ffn", "ab_w_in", "ab_w_out", "na_rpb",
        "gqa_q_gain", "gqa_k_gain", "diff_w_in", "diff_w_out", "diff_lq1", "diff_lk1", "diff_lq2", "diff_lk2",
        "diff_sub_gain", "router_w", "router_bias", "expert_w_gate", "expert_w_up", "expert_w_down",
        "shared_w_gate", "shared_w_up", "shared_w_down", "final_norm"]
_OUT = (1, LAT, D)


def kernel(**inputs):
    import concourse.bacc as _bacc
    from concourse.bass_utils import run_bass_kernel_spmd as _run

    nc = _bacc.Bacc("TRN2", target_bir_lowering=False, num_devices=1)
    arrays, args = {}, {}
    for name in _INS + ["consts"]:
        v = constants() if name == "consts" else np.ascontiguousarray(inputs[name])
        arrays[f"in_{name}_dram"] = v
        args[name] = nc.dram_tensor(f"in_{name}_dram", v.shape, mybir.dt.from_np(v.dtype), kind="ExternalInput").ap()
    out = nc.dram_tensor("out_0_dram", _OUT, F32, kind="ExternalOutput").ap()
    backbone(nc, args, out)
    r = _run(nc, [arrays], core_ids=[0])
    return r.results[0]["out_0_dram"]
```

```python
from contextlib import ExitStack

import numpy as np

import concourse.bass as bass
from concourse import mybir

F32 = mybir.dt.float32
BF16 = mybir.dt.bfloat16
I32 = mybir.dt.int32
ALU = mybir.AluOpType
ACT = mybir.ActivationFunctionType
AX = mybir.AxisListType.X

P = 128
D = 1024
KD = D // P
CTX = 256
LAT = 256
GRID_W = 64
WIN_COLS = 16
WIN_ROWS = 8
HEAD = 64
NA_HEADS = 8
GQA_HEADS = 8
GQA_KV = 2
HEADS = NA_HEADS + GQA_HEADS
DIFF_HEADS = 8
EPS = 1e-6
SCALE = HEAD ** -0.5
E = 64
TOP_K = 8
F = D // 4
KF = F // P
ROUTED_SCALE = 2.5
LAM_INIT = 0.8 - 0.6 * float(np.exp(-0.3))
STREAMS = 2
TILES = (CTX + LAT) // P
SLOTS = 128
BIG = 16384
MASKED = -1e30
NA_ROWS = LAT // GRID_W
REL = NA_ROWS + 2
ROPE = HEAD // 2

CONST = {}
_at = 0
for _name, _n in (("ident", P), ("flip", P), ("before", P), ("ones", P), ("iota", 512), ("pick", 2),
                  ("na_mask", GRID_W), ("cos", 2 * ROPE), ("sin", 2 * ROPE), ("tok_hi", TILES),
                  ("dest_hi", TILES), ("tok_lo", 1), ("dest_lo", 1)):
    CONST[_name] = (_at, _at + _n)
    _at += _n
CONST_W = _at


def constants():
    c = np.zeros((P, CONST_W), np.float32)

    def put(name, a):
        c[:, CONST[name][0]:CONST[name][1]] = a

    p = np.arange(P)
    put("ident", np.eye(P))
    flip = np.zeros((P, P))
    for half in range(2):
        for i in range(GRID_W):
            flip[half * GRID_W + i, half * GRID_W + GRID_W - 1 - i] = 1.0
    put("flip", flip)
    put("before", p[:, None] < p[None, :])
    put("ones", np.ones((P, P)))
    put("iota", np.tile(np.arange(512), (P, 1)))
    pick = np.zeros((P, 2))
    for g in range(4):
        pick[32 * g, 0] = pick[32 * g + 1, 1] = 1.0
    put("pick", pick)
    col = GRID_W - 1 - p % GRID_W
    start = np.clip(col - WIN_COLS // 2, 0, GRID_W - WIN_COLS)
    key = np.arange(GRID_W)
    inside = (key[None] >= start[:, None]) & (key[None] < start[:, None] + WIN_COLS)
    put("na_mask", np.where(inside, 0.0, MASKED))
    t = np.arange(LAT)
    pairs = HEAD // 4
    freq = (np.float32(10000.0) ** (-np.arange(pairs, dtype=np.float32) / np.float32(pairs))).astype(np.float32)
    row, column = (t // GRID_W).astype(np.float32), (t % GRID_W).astype(np.float32)
    angle = np.concatenate([row[:, None] * freq, column[:, None] * freq], axis=-1).astype(np.float32)
    put("cos", np.cos(angle).reshape(2, P, ROPE).transpose(1, 0, 2).reshape(P, -1))
    put("sin", np.sin(angle).reshape(2, P, ROPE).transpose(1, 0, 2).reshape(P, -1))
    put("tok_hi", np.tile(P * np.arange(TILES) - BIG, (P, 1)))
    put("dest_hi", np.tile(TOP_K * P * np.arange(TILES) - BIG, (P, 1)))
    put("tok_lo", p[:, None])
    put("dest_lo", TOP_K * p[:, None])
    return c


class Stage:

    def __init__(self, nc, name):
        self.nc, self.name, self.sems, self.stack = nc, name, [], ExitStack()

    def __enter__(self):
        return self

    def sb(self, name, shape, dt=F32):
        return self.stack.enter_context(self.nc.sbuf_tensor(f"{self.name}_{name}", shape, dt))

    def sem(self, name):
        s = self.stack.enter_context(self.nc.semaphore(f"{self.name}_{name}"))
        self.sems.append(s)
        return s

    def pool_sem(self, name):
        return self.nc.alloc_semaphore(f"{self.name}_{name}")

    def __exit__(self, *a):
        if a[0] is None:
            with self.nc.Block() as block:
                @block.sync
                def _(sp):
                    for s in self.sems:
                        sp.sem_clear(s)
        self.stack.close()


class Chain:

    def __init__(self, eng, sem):
        self.eng, self.sem, self.n = eng, sem, 0

    def __call__(self, ins):
        self.n += 1
        ins.then_inc(self.sem, 1)
        self.eng.wait_ge(self.sem, self.n)


BLOCK = 512
STREAM = 4
AB_FIRST = 3


class Stream:

    def __init__(self, nc, wb, a):
        self.nc, self.wb, self.fed = nc, wb, 0
        self.loaded = [nc.alloc_semaphore(f"block_loaded{i}") for i in range(STREAM)]
        self.blocks, self.start, self.end = [], {}, {}
        ada = a["ada_w"].rearrange("l (p k) n -> l p k n", k=KD)
        for name, src in (("ada_first", ada[0][:, :, 0:2 * D]), ("ab_w_in", a["ab_w_in"][:, :, AB_FIRST * BLOCK:].rearrange("o (k p) n -> p (o k) n", p=P)),
                          ("ab_w_in_rest", a["ab_w_in"][:, :, 0:AB_FIRST * BLOCK].rearrange("o (k p) n -> p (o k) n", p=P)),
                          ("ada_rest", ada[0][:, :, 2 * D:]), ("ada1", ada[1]), ("ab_w_out", a["ab_w_out"].rearrange("o (k p) n -> p (o k) n", p=P)),
                          ("diff_w_kv", a["diff_w_in"][:, :, D:].rearrange("o (k p) n -> p (o k) n", p=P)),
                          ("diff_w_q", a["diff_w_in"][:, :, 0:D].rearrange("o (k p) n -> p (o k) n", p=P)),
                          ("diff_w_out", a["diff_w_out"].rearrange("o (k p) n -> p (o k) n", p=P))):
            self.start[name] = len(self.blocks)
            width = src.shape[-1]
            for c in range(0, width, BLOCK):
                self.blocks.append(src[:, :, c:min(c + BLOCK, width)])
            self.end[name] = len(self.blocks)

    def feed(self, sp, upto, first, used=None):
        for n in range(self.fed, upto):
            if n - STREAM >= first:
                sp.wait_ge(*used(n - STREAM - first))
            src = self.blocks[n]
            sp.dma_start(self.at(n)[:, :, 0:src.shape[-1]], src).then_inc(self.loaded[n % STREAM], 16)
        self.fed = max(self.fed, upto)

    def at(self, n):
        return self.wb[:, n % STREAM, :].rearrange("p (k n) -> p k n", n=BLOCK)

    def take(self, pe, n):
        pe.wait_ge(self.loaded[n % STREAM], 16 * (n // STREAM + 1))
        return self.at(n)


class Core:

    def __init__(self, nc, ctx, a):
        def sb(name, shape, dt=F32):
            return ctx.enter_context(nc.sbuf_tensor(name, shape, dt))

        self.nc = nc
        self.x = sb("x_res", [P, TILES, D])
        self.const = sb("const", [P, CONST_W])
        self.cols = sb("cols", [P, P])
        self.mod = sb("mod", [P, 2, 6 * KD, STREAMS])
        self.amp = sb("amp", [P, 2, 2, STREAMS, KD])
        self.hT = sb("hT", [P, KD, TILES * P])
        self.silu = sb("silu", [P, KD, 32])
        self.wb = sb("wb", [P, STREAM, KD * BLOCK])
        self.pool = sb("pool", [P, 5, 2 * D])
        self.stream = Stream(nc, self.wb, a)
        self.ps = ctx.enter_context(nc.psum_tensor("ps", [P, 8, 512], F32))
        self.xn = self.piece(0, 2)

    def c(self, name):
        return self.const[:, CONST[name][0]:CONST[name][1]]

    def piece(self, i, n=1):
        flat = self.pool[:, i:i + n].rearrange("p i c -> p (i c)")
        return flat.rearrange("p (t c) -> p t c", c=512 if n == 1 else D)

    def gate_column(self, layer, which, stream, k):
        return self.mod[:, layer, (2 + 3 * which) * KD + k, stream:stream + 1]

    def shift_column(self, layer, which, stream, k):
        return self.mod[:, layer, 3 * which * KD + k, stream:stream + 1]


class Modulation:

    def __init__(self, core, st, jobs, first, sum_banks, col_banks):
        self.core, self.jobs, self.first = core, jobs, first
        self.sum_banks, self.col_banks = sum_banks, col_banks
        self.part = st.sb("part", [P, 2, BLOCK])
        self.sums_ready, self.part_ready = st.sem("sums_ready"), st.sem("part_ready")
        self.colsum_ready, self.col_done = st.sem("colsum_ready"), st.sem("col_done")

    def used(self, n):
        return self.sums_ready, n + 1

    def pe_sums(self, pe, n):
        core, nc = self.core, self.core.nc
        w = core.stream.take(pe, self.first + n)
        if n >= len(self.sum_banks):
            pe.wait_ge(self.part_ready, n - len(self.sum_banks) + 1)
        bank = self.sum_banks[n % len(self.sum_banks)]
        for k in range(KD):
            g = 32 * (k % 4)
            mm = nc.tensor.matmul(core.ps[g:g + 32, bank, :], core.silu[:, k, :], w[:, k, :], start=k < 4,
                                  stop=k >= 4, skip_group_check=True, tile_position=(0, g))
        mm.then_inc(self.sums_ready, 1)

    def pe_columns(self, pe, n):
        core, nc = self.core, self.core.nc
        pe.wait_ge(self.part_ready, n + 1)
        if n >= len(self.col_banks):
            pe.wait_ge(self.col_done, n - len(self.col_banks) + 1)
        bank = self.col_banks[n % len(self.col_banks)]
        for j in range(4):
            mm = nc.tensor.matmul(core.ps[:, bank, 2 * j:2 * j + 2], self.part[:, n % 2, j * P:(j + 1) * P],
                                  core.c("pick"), start=True, stop=True)
        mm.then_inc(self.colsum_ready, 1)

    def dve_part(self, dve, n):
        dve.wait_ge(self.sums_ready, n + 1)
        if n >= 2:
            dve.wait_ge(self.colsum_ready, n - 1)
        bank = self.sum_banks[n % len(self.sum_banks)]
        self.core.nc.vector.tensor_copy(self.part[:, n % 2, :], self.core.ps[:, bank, :]).then_inc(self.part_ready, 1)

    def dve_take(self, dve, n):
        dve.wait_ge(self.colsum_ready, n + 1)
        layer, block = self.jobs[n]
        out = self.core.mod[:, layer].rearrange("p j s -> p (j s)")[:, 8 * block:8 * block + 8]
        self.core.nc.vector.tensor_copy(out, self.core.ps[:, self.col_banks[n % len(self.col_banks)],
                                                          0:8]).then_inc(self.col_done, 1)

    def dve_finish(self, dve, link):
        core, nc = self.core, self.core.nc
        dve.wait_ge(self.col_done, len(self.jobs))
        per = BLOCK // P
        for layer in sorted({l for l, _ in self.jobs}):
            mine = [b for l, b in self.jobs if l == layer]
            lo, hi = per * min(mine), per * (max(mine) + 1)
            for s in range(STREAMS):
                m = core.mod[:, layer, lo:hi, s]
                link(nc.vector.tensor_tensor(m, m, core.cols[:, 6 * KD * layer + lo:6 * KD * layer + hi], ALU.add))
            for which in range(2):
                at = (3 * which + 1) * KD
                if not lo <= at < hi:
                    continue
                gain = core.cols[:, 12 * KD + 16 * which + KD * layer:][:, 0:KD]
                for s in range(STREAMS):
                    link(nc.vector.scalar_tensor_tensor(out=core.amp[:, layer, which, s, :],
                                                        in0=core.mod[:, layer, at:at + KD, s], scalar=1.0,
                                                        in1=gain, op0=ALU.add, op1=ALU.mult))


class RowNorm:

    def __init__(self, core, st, tiles):
        self.core, self.tiles = core, tiles
        self.ss, self.rs = st.sb("ss", [P, TILES]), st.sb("rs", [P, 3, TILES])
        self.sq_ready, self.var_ready, self.root_ready = st.sem("sq"), st.sem("var"), st.sem("root")
        self.row_ready, self.inverse = st.sem("row"), st.sem("inverse")

    def act_square(self, act, i):
        self.core.nc.scalar.activation(self.core.xn[:, i, :], self.core.x[:, self.tiles[i], :], ACT.Square,
                                       accum_out=self.ss[:, i:i + 1]).then_inc(self.sq_ready, 1)

    def act_root(self, act, i):
        act.wait_ge(self.var_ready, i + 1)
        self.core.nc.scalar.activation(self.rs[:, 1, i:i + 1], self.rs[:, 0, i:i + 1],
                                       ACT.Sqrt).then_inc(self.root_ready, 1)

    def dve_rows(self, dve, i):
        nc, rs = self.core.nc, self.rs
        dve.wait_ge(self.sq_ready, i + 1)
        nc.vector.tensor_scalar(rs[:, 0, i:i + 1], self.ss[:, i:i + 1], 1.0 / D, EPS, ALU.mult,
                                ALU.add).then_inc(self.var_ready, 1)
        dve.wait_ge(self.root_ready, i + 1)
        nc.vector.reciprocal(rs[:, 2, i:i + 1], rs[:, 1, i:i + 1]).then_inc(self.inverse, 1)
        dve.wait_ge(self.inverse, i + 1)
        nc.vector.tensor_scalar(self.core.xn[:, i, :], self.core.x[:, self.tiles[i], :], rs[:, 2, i:i + 1], None,
                                ALU.mult).then_inc(self.row_ready, 1)


MOD_BLOCKS = 6 * D // BLOCK
MOD_FIRST = 2 * D // BLOCK


def modulation(core, a):
    nc = core.nc
    with Stage(nc, "adaln") as st:
        rows = st.sb("rows", [P, P])
        cond = st.sb("cond", [P, STREAMS, KD])
        tmp = st.sb("tmp", [P, 2, STREAMS * KD])
        const_in, rows_in, cond_in = (st.sem(n) for n in ("const_in", "rows_in", "cond_in"))
        x_in = [st.sem(f"x_in{s}") for s in range(STREAMS)]
        norm = RowNorm(core, st, list(range(TILES)))
        e_ready, silu_ready, rowsT, own = (st.sem(n) for n in ("e_ready", "silu_ready", "rowsT", "own"))
        m = Modulation(core, st, [(0, b) for b in range(MOD_FIRST)], 0, [0, 1, 2, 3], [4, 5])
        with nc.Block() as block:
            @block.sync
            def _(sp):
                sp.dma_start(cond[:, 0, :], a["c_ctx"].rearrange("(p k) -> p k", k=KD)).then_inc(cond_in, 16)
                sp.dma_start(cond[:, 1, :], a["c"].rearrange("o (p k) -> (o p) k", k=KD)).then_inc(cond_in, 16)
                core.stream.feed(sp, 2, 0)
                sp.dma_start(core.const[:], a["consts"]).then_inc(const_in, 16)
                sp.dma_start(core.x[:, 0:2], a["ctx"].rearrange("o (t p) d -> p (o t) d", p=P)).then_inc(x_in[0], 16)
                core.stream.feed(sp, 3, 0)
                sp.dma_start(core.x[:, 2:4], a["x"].rearrange("o (t p) d -> p (o t) d", p=P)).then_inc(x_in[1], 16)
                nb = 2 * 6 * KD
                sp.dma_start(rows[0:nb, :], a["ada_b"].rearrange("l (j p) -> (l j) p", p=P)).then_inc(rows_in, 16)
                sp.dma_start(rows[nb:nb + 16, :], a["norm_mix"].rearrange("l (j p) -> (l j) p", p=P)).then_inc(rows_in, 16)
                sp.dma_start(rows[nb + 16:nb + 32, :], a["norm_ffn"].rearrange("l (j p) -> (l j) p", p=P)).then_inc(rows_in, 16)
                core.stream.feed(sp, MOD_FIRST, 0, m.used)
                core.stream.feed(sp, MOD_FIRST + STREAM, 0, m.used)

            @block.scalar
            def _(act):
                act.wait_ge(cond_in, 32)
                nc.scalar.activation(tmp[:, 0, :], cond[:].rearrange("p s k -> p (s k)"), ACT.Exp,
                                     scale=-1.0).then_inc(e_ready, 1)
                for i in range(TILES):
                    act.wait_ge(x_in[i // 2], 16)
                    norm.act_square(act, i)
                    norm.act_root(act, i)

            @block.tensor
            def _(pe):
                pe.wait_ge(silu_ready, 1)
                for n in range(MOD_FIRST):
                    m.pe_sums(pe, n)
                    if n == 0:
                        pe.wait_ge(const_in, 16)
                    if n >= 1:
                        m.pe_columns(pe, n - 1)
                m.pe_columns(pe, MOD_FIRST - 1)
                pe.wait_ge(rows_in, 48)
                nc.tensor.transpose(core.ps[:, 6, 0:P], rows[:], core.c("ident")).then_inc(rowsT, 1)

            @block.vector
            def _(dve):
                link = Chain(dve, own)
                link(nc.vector.memset(core.silu[:], 0.0))
                dve.wait_ge(e_ready, 1)
                link(nc.vector.tensor_scalar(tmp[:, 1, :], tmp[:, 0, :], 1.0, None, ALU.add))
                link(nc.vector.reciprocal(tmp[:, 0, :], tmp[:, 1, :]))
                nc.vector.tensor_tensor(core.silu[:, :, 0:STREAMS].rearrange("p k s -> p s k"), cond[:],
                                        tmp[:, 0, :].rearrange("p (s k) -> p s k", s=STREAMS),
                                        ALU.mult).then_inc(silu_ready, 1)
                for n in range(MOD_FIRST):
                    m.dve_part(dve, n)
                    if n >= 1:
                        m.dve_take(dve, n - 1)
                    for i in ([n] if n < MOD_FIRST - 2 else range(n, TILES) if n == MOD_FIRST - 2 else []):
                        norm.dve_rows(dve, i)
                m.dve_take(dve, MOD_FIRST - 1)
                dve.wait_ge(rowsT, 1)
                link(nc.vector.tensor_copy(core.cols[:], core.ps[:, 6, 0:P]))
                m.dve_finish(dve, link)


def norm_transpose(core, layer, which, streams, sync=None):
    nc = core.nc
    name = f"norm{layer}{which}"
    with Stage(nc, name) as st:
        xn = core.xn
        turned, taken = st.sem("turned"), [st.sem("taken_dve"), st.sem("taken_act")]
        items = [(i, s, k) for i, s in enumerate(streams) for k in range(KD)]

        def scaled(n):
            i, s, k = items[n]
            return (core.hT[:, k, s * CTX:s * CTX + CTX], core.ps[:, n % 8, 0:CTX],
                    core.amp[:, layer, which, s, k:k + 1], core.shift_column(layer, which, s, k))

        with nc.Block() as block:
            @block.sync
            def _(sp):
                if sync:
                    sync(sp)

            @block.scalar
            def _(act):
                for n in range(1, len(items), 2):
                    act.wait_ge(turned, n + 1)
                    out, src, amp, shift = scaled(n)
                    nc.scalar.activation(out, src, ACT.Identity, scale=amp, bias=shift).then_inc(taken[1], 1)

            @block.tensor
            def _(pe):
                for n, (i, s, k) in enumerate(items):
                    if n >= 8:
                        pe.wait_ge(taken[n % 2], (n - 8) // 2 + 1)
                    for j in range(2):
                        mm = nc.tensor.transpose(core.ps[:, n % 8, j * P:(j + 1) * P],
                                                 xn[:, 2 * i + j, k * P:(k + 1) * P], core.c("ident"))
                    mm.then_inc(turned, 1)

            @block.vector
            def _(dve):
                for n in range(0, len(items), 2):
                    dve.wait_ge(turned, n + 1)
                    out, src, amp, shift = scaled(n)
                    nc.vector.tensor_scalar(out, src, amp, shift, ALU.mult, ALU.add).then_inc(taken[0], 1)




def rotate(nc, link, pairs, tmp, cos, sin):
    heads = pairs.shape[1]
    even, odd = pairs[:, :, :, 0], pairs[:, :, :, 1]
    t = [tmp[:, i, 0:heads * ROPE].rearrange("p (h r) -> p h r", h=heads) for i in range(4)]
    c = cos.rearrange("p (o r) -> p o r", o=1).to_broadcast([P, heads, ROPE])
    s = sin.rearrange("p (o r) -> p o r", o=1).to_broadcast([P, heads, ROPE])
    nc.vector.tensor_tensor(t[0], even, c, ALU.mult)
    nc.vector.tensor_tensor(t[1], odd, s, ALU.mult)
    nc.vector.tensor_tensor(t[2], even, s, ALU.mult)
    link(nc.vector.tensor_tensor(t[3], odd, c, ALU.mult))
    nc.vector.tensor_tensor(even, t[0], t[1], ALU.subtract)
    link(nc.vector.tensor_tensor(odd, t[2], t[3], ALU.add))


class QKNorm:

    ITEMS = [("q", c) for c in range(4)] + [("k", g) for g in range(GQA_KV)]

    def __init__(self, core, st, a, w):
        self.core, self.a, self.w = core, a, w
        self.gain = st.sb("gain", [P, 2, HEAD])
        self.sq = st.sb("sq", [P, TILES, GQA_HEADS * HEAD])
        self.ss = st.sb("ss", [P, 4, TILES * GQA_HEADS])
        self.sk = st.sb("sk", [P, 4, TILES * GQA_KV])
        self.tmp = st.sb("tmp", [P, 4, GQA_HEADS * ROPE])
        self.kdup = st.sb("kdup", [P, TILES, GQA_KV, 2, HEAD])
        self.gains_in, self.own = st.sem("gains_in"), st.sem("own")
        self.var_ready, self.root_ready = st.sem("var_ready"), st.sem("root_ready")
        self.qk_ready, self.turned = st.sem("qk_ready"), st.sem("turned")
        self.taken = [st.sem("taken_dve"), st.sem("taken_act")]

    def load(self, sp):
        sp.dma_start(self.gain[:, 0, :], self.a["gqa_q_gain"].to_broadcast([P, HEAD])).then_inc(self.gains_in, 16)
        sp.dma_start(self.gain[:, 1, :], self.a["gqa_k_gain"].to_broadcast([P, HEAD])).then_inc(self.gains_in, 16)

    def act_root(self, act):
        nc = self.core.nc
        act.wait_ge(self.var_ready, 1)
        nc.scalar.activation(self.ss[:, 2, :], self.ss[:, 1, :], ACT.Sqrt)
        nc.scalar.activation(self.sk[:, 2, :], self.sk[:, 1, :], ACT.Sqrt).then_inc(self.root_ready, 1)

    def place(self, n):
        kind, c = self.ITEMS[n]
        return (self.w.qbT if kind == "q" else self.w.kbT)[:, c, :], self.core.ps[:, n, :]

    def act_take(self, act):
        for n in range(1, len(self.ITEMS), 2):
            act.wait_ge(self.turned, n + 1)
            self.core.nc.scalar.copy(*self.place(n)).then_inc(self.taken[1], 1)

    def dve_take(self, dve):
        for n in range(0, len(self.ITEMS), 2):
            dve.wait_ge(self.turned, n + 1)
            self.core.nc.vector.tensor_copy(*self.place(n)).then_inc(self.taken[0], 1)

    def dve_norm(self, dve):
        core, nc = self.core, self.core.nc
        gain, sq, ss, sk, tmp, kdup = self.gain, self.sq, self.ss, self.sk, self.tmp, self.kdup
        q, k = self.w.qb, self.w.kvb[:, :, 0:GQA_KV * HEAD]
        link = Chain(dve, self.own)
        nk = GQA_KV * HEAD
        ksq = kdup[:].rearrange("p t g u d -> p t (g u d)")[:, :, 0:nk]
        nc.vector.tensor_tensor(sq[:], q[:], q[:], ALU.mult)
        link(nc.vector.tensor_tensor(ksq, k, k, ALU.mult))
        nc.vector.tensor_reduce(ss[:, 0, :], sq[:].rearrange("p t (h d) -> p (t h) d", d=HEAD), AX, ALU.add)
        link(nc.vector.tensor_reduce(sk[:, 0, :].rearrange("p (t g) -> p t g", t=TILES),
                                     ksq.rearrange("p t (g d) -> p t g d", d=HEAD), AX, ALU.add))
        nc.vector.tensor_scalar(ss[:, 1, :], ss[:, 0, :], 1.0 / HEAD, EPS, ALU.mult, ALU.add)
        nc.vector.tensor_scalar(sk[:, 1, :], sk[:, 0, :], 1.0 / HEAD, EPS, ALU.mult, ALU.add).then_inc(self.var_ready, 1)
        dve.wait_ge(self.gains_in, 32)
        link(nc.vector.tensor_scalar(gain[:, 0, :], gain[:, 0, :], SCALE, None, ALU.mult))
        dve.wait_ge(self.root_ready, 1)
        nc.vector.reciprocal(ss[:, 3, :], ss[:, 2, :])
        link(nc.vector.reciprocal(sk[:, 3, :], sk[:, 2, :]))
        for t in range(TILES):
            qt = q[:, t, :].rearrange("p (h d) -> p h d", d=HEAD)
            kt = k[:, t, :].rearrange("p (h d) -> p h d", d=HEAD)
            for x, heads, r, g in ((qt, GQA_HEADS, ss, 0), (kt, GQA_KV, sk, 1)):
                rb = r[:, 3, t * heads:(t + 1) * heads].rearrange("p (h o) -> p h o", o=1)
                link(nc.vector.tensor_tensor(x, x, rb.to_broadcast([P, heads, HEAD]), ALU.mult))
                gb = gain[:, g, :].rearrange("p (o d) -> p o d", o=1).to_broadcast([P, heads, HEAD])
                link(nc.vector.tensor_tensor(x, x, gb, ALU.mult))
                if t >= 2:
                    cos = core.c("cos")[:, (t - 2) * ROPE:(t - 1) * ROPE]
                    sin = core.c("sin")[:, (t - 2) * ROPE:(t - 1) * ROPE]
                    rotate(nc, link, x.rearrange("p h (r two) -> p h r two", two=2), tmp, cos, sin)
            ins = nc.vector.tensor_copy(kdup[:, t], kt.rearrange("p g (o d) -> p g o d", o=1)
                                        .to_broadcast([P, GQA_KV, 2, HEAD]))
            if t < TILES - 1:
                link(ins)
        ins.then_inc(self.qk_ready, 1)

    def pe_turn(self, pe):
        nc = self.core.nc
        pe.wait_ge(self.qk_ready, 1)
        for n, (kind, c) in enumerate(self.ITEMS):
            for t in range(TILES):
                src = self.w.qb[:, t, c * P:(c + 1) * P] if kind == "q" else \
                    self.kdup[:, t, c].rearrange("p u d -> p (u d)")
                mm = nc.tensor.transpose(self.core.ps[:, n, t * P:(t + 1) * P], src, self.core.c("ident"))
            mm.then_inc(self.turned, 1)


def project_even(core, a, w):
    nc = core.nc
    widths = [BLOCK] * 4 + [2 * GQA_KV * HEAD]
    rows = 2 * WIN_ROWS - 1
    first = core.stream.start["ab_w_in"]
    with Stage(nc, "proj0") as st:
        pad = st.sb("rpb_pad", [NA_HEADS * rows, P])
        rpb_sem, rpb_ready = st.pool_sem("rpb_sem"), st.sem("rpb_ready")
        summed, taken = st.sem("summed"), st.sem("taken")
        blocks = [3, 4, 0, 1, 2]
        items = [(b, j) for b in blocks for j in range(4)]
        qk = QKNorm(core, st, a, w)

        def target(b, j):
            if b < 2:
                return (w.qaT, w.kaT)[b][:, j, :]
            return w.kvb[:, j, :] if b == 4 else (w.va, w.qb)[b - 2][:, j, :]

        with nc.Block() as block:
            @block.sync
            def _(sp):
                qk.load(sp)
                core.stream.feed(sp, core.stream.end["ab_w_in_rest"] + STREAM, first, lambda b: (summed, 4 * b + 4))

            @block.gpsimd
            def _(pool):
                nc.gpsimd.memset(pad[:], 0.0).then_inc(rpb_ready, 1)
                pool.wait_ge(rpb_ready, 1)
                pool.dma_start(pad[:, GRID_W - WIN_COLS:GRID_W + WIN_COLS - 1],
                               a["na_rpb"].rearrange("o h r c -> (o h r) c")).then_inc(rpb_sem, 16)
                pool.wait_ge(rpb_sem, 16)
                pool.dma_start(w.rpb_rows, pad[:]).then_inc(rpb_sem, 16)
                pool.wait_ge(rpb_sem, 32)
                for half in range(2):
                    for h in range(NA_HEADS):
                        start = (h * rows + WIN_ROWS - 1 - 2 - half) * P
                        src = bass.AP(w.rpb_rows.tensor, start, [[1, GRID_W], [P, REL], [1, GRID_W]])
                        pool.dma_start(w.bias[half * GRID_W:(half + 1) * GRID_W, h], src).then_inc(rpb_sem, 16)
                pool.wait_ge(rpb_sem, 32 + 16 * 2 * NA_HEADS)
                m = core.c("na_mask").rearrange("p (o c) -> p o c", o=1).to_broadcast([P, NA_HEADS * REL, GRID_W])
                b = w.bias[:].rearrange("p h u c -> p (h u) c")
                nc.gpsimd.tensor_tensor(b, b, m, ALU.add).then_inc(rpb_ready, 1)

            @block.tensor
            def _(pe):
                for n, (b, j) in enumerate(items):
                    wb = core.stream.take(pe, first + blocks.index(b))
                    if n >= 8:
                        pe.wait_ge(taken, n - 7)
                    for k in range(KD):
                        if b < 2:
                            lhs, rhs = wb[:, k, j * P:(j + 1) * P], core.hT[:, k, :]
                        else:
                            lhs, rhs = core.hT[:, k, j * P:(j + 1) * P], wb[:, k, 0:widths[b]]
                        mm = nc.tensor.matmul(core.ps[:, n % 8, 0:widths[b]], lhs, rhs, start=k == 0,
                                              stop=k == KD - 1)
                    mm.then_inc(summed, 1)
                pe.wait_ge(taken, len(items))
                qk.pe_turn(pe)

            @block.vector
            def _(dve):
                dve.wait_ge(taken, 8)
                qk.dve_norm(dve)
                qk.dve_take(dve)

            @block.scalar
            def _(act):
                for n, (b, j) in enumerate(items):
                    if n == 8:
                        qk.act_root(act)
                    act.wait_ge(summed, n + 1)
                    nc.scalar.activation(target(b, j), core.ps[:, n % 8, 0:widths[b]], ACT.Copy,
                                         scale=SCALE if b == 0 else 1.0).then_inc(taken, 1)
                qk.act_take(act)


def attend_even(core, w):
    nc = core.nc
    with Stage(nc, "attn0") as st:
        p = st.sb("p", [P, 4, 512])
        pn = st.sb("pn", [P, 4, 512])
        pT = st.sb("pT", [P, 4, 4, CTX])
        mx = st.sb("mx", [P, 4, 4])
        scored, max_ready, exp_ready, recip_ready = (
            st.sem(n) for n in ("scored", "max_ready", "exp_ready", "recip_ready"))
        norm_pool, norm_act = st.sem("norm_pool"), st.sem("norm_act")
        turned, pT_ready, summed, out_done = st.sem("turned"), st.sem("pT_ready"), st.sem("summed"), st.sem("out_done")
        own, rest_own = st.sem("own"), st.sem("rest_own")
        items = [(h, s, i) for h in range(HEADS) for s in range(STREAMS) for i in range(2)]
        rest = Modulation(core, st, [(0, b) for b in range(MOD_FIRST, MOD_BLOCKS)] + [(1, b) for b in range(MOD_BLOCKS)],
                        core.stream.start["ada_rest"], [6], [7])
        EVERY = 3

        def wait_normed(eng, n):
            if n % 3 == 2:
                eng.wait_ge(norm_act, n // 3 + 1)
            else:
                eng.wait_ge(norm_pool, n - (n + 1) // 3 + 1)

        def keys(s):
            return CTX if s == 0 else CTX + LAT

        def operands(h):
            base = HEAD * (h % 2)
            if h < NA_HEADS:
                return base, w.qaT[:, h // 2], w.kaT[:, h // 2]
            j = h - NA_HEADS
            return base, w.qbT[:, j // 2], w.kbT[:, j // (GQA_HEADS // GQA_KV)]

        def values(h, kt):
            if h < NA_HEADS:
                return w.va[:, kt, h * HEAD:(h + 1) * HEAD]
            g = (h - NA_HEADS) // (GQA_HEADS // GQA_KV)
            return w.kvb[:, kt, (GQA_KV + g) * HEAD:(GQA_KV + g + 1) * HEAD]

        with nc.Block() as block:
            @block.sync
            def _(sp):
                core.stream.feed(sp, core.stream.end["ab_w_out"], rest.first, rest.used)

            @block.tensor
            def _(pe):
                def score(n):
                    h, s, i = items[n]
                    t = 2 * s + i
                    base, qT, kT = operands(h)
                    if n >= 2:
                        pe.wait_ge(exp_ready, n - 1)
                    local = h < NA_HEADS and s == 1
                    mm = nc.tensor.matmul(core.ps[:, n % 2, 0:keys(s)], qT[base:base + HEAD, t * P:(t + 1) * P],
                                          kT[base:base + HEAD, 0:keys(s)], start=True, stop=not local,
                                          skip_group_check=True)
                    if local:
                        bias = w.bias[:, h, 2 - 2 * i:2 - 2 * i + NA_ROWS, :].rearrange("p u c -> p (u c)")
                        mm = nc.tensor.matmul(core.ps[:, n % 2, CTX:CTX + LAT], core.c("flip"), bias, start=False,
                                              stop=True, skip_group_check=True)
                    mm.then_inc(scored, 1)

                def turn(n):
                    h, s, i = items[n]
                    wait_normed(pe, n)
                    if n >= 2:
                        pe.wait_ge(pT_ready, n - 1)
                    for kt in range(keys(s) // P):
                        mm = nc.tensor.transpose(core.ps[:, 2 + n % 2, kt * P:(kt + 1) * P],
                                                 pn[:, n % 4, kt * P:(kt + 1) * P], core.c("ident"))
                    mm.then_inc(turned, 1)

                def weigh(m):
                    h, s, _ = items[2 * m]
                    base = HEAD * (h % 2)
                    pe.wait_ge(pT_ready, 2 * m + 2)
                    if m >= 2:
                        pe.wait_ge(out_done, m - 1)
                    for kt in range(keys(s) // P):
                        mm = nc.tensor.matmul(core.ps[base:base + HEAD, 4 + m % 2, 0:CTX], values(h, kt),
                                              pT[:, m % 4, kt, :], start=kt == 0, stop=kt == keys(s) // P - 1)
                    mm.then_inc(summed, 1)

                N = len(items)
                for n in range(N + 6):
                    if n < N:
                        score(n)
                    if 4 <= n < N + 4:
                        turn(n - 4)
                    if n >= 6 and n % 2 == 1:
                        weigh((n - 6) // 2)
                    if n % EVERY == 1 and n // EVERY < len(rest.jobs):
                        rest.pe_sums(pe, n // EVERY)
                    if n >= EVERY and n % EVERY == 0 and n // EVERY - 1 < len(rest.jobs):
                        rest.pe_columns(pe, n // EVERY - 1)

            @block.vector
            def _(dve):
                def take_max(n):
                    dve.wait_ge(scored, n + 1)
                    if n >= 4:
                        wait_normed(dve, n - 4)
                    nk = keys(items[n][1])
                    nc.vector.tensor_reduce(mx[:, n % 4, 0:1], core.ps[:, n % 2, 0:nk], AX, ALU.max).then_inc(own, 1)
                    dve.wait_ge(own, n + 1)
                    nc.vector.tensor_scalar(mx[:, n % 4, 1:2], mx[:, n % 4, 0:1], -1.0, None,
                                            ALU.mult).then_inc(max_ready, 1)

                def recip(n):
                    dve.wait_ge(exp_ready, n + 1)
                    nc.vector.reciprocal(mx[:, n % 4, 3:4], mx[:, n % 4, 2:3]).then_inc(recip_ready, 1)

                def take_turned(n):
                    nk = keys(items[n][1])
                    m = n // 2
                    dve.wait_ge(turned, n + 1)
                    if m >= 4:
                        dve.wait_ge(summed, m - 3)
                    nc.vector.tensor_copy(pT[:, m % 4, 0:nk // P, (n % 2) * P:(n % 2 + 1) * P],
                                          core.ps[:, 2 + n % 2, 0:nk].rearrange("p (k q) -> p k q", q=P)
                                          ).then_inc(pT_ready, 1)

                for n in range(len(items) + 4):
                    if n < len(items):
                        take_max(n)
                    if 1 <= n <= len(items):
                        recip(n - 1)
                    if n >= 4:
                        take_turned(n - 4)
                    if n % EVERY == 2 and n // EVERY < len(rest.jobs):
                        rest.dve_part(dve, n // EVERY)
                    if n >= EVERY and n % EVERY == 1 and n // EVERY - 1 < len(rest.jobs):
                        rest.dve_take(dve, n // EVERY - 1)
                rest.dve_finish(dve, Chain(dve, rest_own))

            @block.scalar
            def _(act):
                def take_out(m):
                    h, s, _ = items[2 * m]
                    base = HEAD * (h % 2)
                    act.wait_ge(summed, m + 1)
                    nc.scalar.copy(core.hT[base:base + HEAD, h // 2, s * CTX:(s + 1) * CTX],
                                   core.ps[base:base + HEAD, 4 + m % 2, 0:CTX]).then_inc(out_done, 1)

                def scale(n):
                    nk = keys(items[n][1])
                    act.wait_ge(recip_ready, n + 1)
                    if n >= 4:
                        act.wait_ge(turned, n - 3)
                    nc.scalar.activation(pn[:, n % 4, 0:nk], p[:, n % 4, 0:nk], ACT.Copy,
                                         scale=mx[:, n % 4, 3:4]).then_inc(norm_act, 1)

                N = len(items)
                for n in range(N):
                    nk = keys(items[n][1])
                    act.wait_ge(max_ready, n + 1)
                    nc.scalar.activation(p[:, n % 4, 0:nk], core.ps[:, n % 2, 0:nk], ACT.Exp, bias=mx[:, n % 4, 1:2],
                                         accum_out=mx[:, n % 4, 2:3]).then_inc(exp_ready, 1)
                    if n >= 2 and (n - 1) % 3 == 2:
                        scale(n - 1)
                    if n >= 9 and n % 2 == 1:
                        take_out((n - 9) // 2)
                for m in range((N - 1 - 9) // 2 + 1, N // 2):
                    take_out(m)

            @block.gpsimd
            def _(pool):
                for n in (n for n in range(len(items)) if n % 3 != 2):
                    nk = keys(items[n][1])
                    pool.wait_ge(recip_ready, n + 1)
                    if n >= 4:
                        pool.wait_ge(turned, n - 3)
                    nc.gpsimd.tensor_scalar(pn[:, n % 4, 0:nk], p[:, n % 4, 0:nk], mx[:, n % 4, 3:4], None,
                                            ALU.mult).then_inc(norm_pool, 1)


def project_out(core, layer, which_w, tiles, oT_at):
    nc = core.nc
    streams = sorted({t // 2 for t in tiles})
    with Stage(nc, f"out{layer}") as st:
        diag = st.sb("diag", [P, len(streams), KD, P])
        grow = st.sb("grow", [P, len(streams), D])
        prod = st.sb("prod", [P, 2, 512])
        diag_ready, spread, gates_ready = st.sem("diag_ready"), st.sem("spread"), st.sem("gates_ready")
        summed, added, own = st.sem("summed"), st.sem("added"), st.sem("own")
        first = core.stream.start[which_w]
        items = [(t, half) for t in tiles for half in range(2)]
        norm = RowNorm(core, st, tiles)
        with nc.Block() as block:
            @block.tensor
            def _(pe):
                def spread_gates(i):
                    pe.wait_ge(diag_ready, i + 1)
                    if i >= 1:
                        pe.wait_ge(gates_ready, i)
                    for half in range(2):
                        for k in range(4):
                            mm = nc.tensor.matmul(core.ps[:, 6 + half, k * P:(k + 1) * P], core.c("ones"),
                                                  diag[:, i, 4 * half + k, :], start=True, stop=True)
                    mm.then_inc(spread, 1)

                for n, (t, half) in enumerate(items):
                    wo = core.stream.take(pe, first + half)
                    if n >= 6:
                        pe.wait_ge(added, n - 5)
                    for k in range(KD):
                        mm = nc.tensor.matmul(core.ps[:, n % 6, :], core.hT[:, k, oT_at(t)], wo[:, k, :],
                                              start=k == 0, stop=k == KD - 1)
                    mm.then_inc(summed, 1)
                    if n < len(streams):
                        spread_gates(n)

            @block.vector
            def _(dve):
                for i, s in enumerate(streams):
                    for k in range(KD):
                        ins = nc.vector.tensor_scalar(diag[:, i, k, :], core.c("ident"),
                                                      core.gate_column(layer, 0, s, k), None, ALU.mult)
                    ins.then_inc(diag_ready, 1)
                for i, s in enumerate(streams):
                    dve.wait_ge(spread, i + 1)
                    nc.vector.tensor_copy(grow[:, i, :].rearrange("p (h c) -> p h c", h=2),
                                          core.ps[:, 6:8, :]).then_inc(gates_ready, 1)
                for n, (t, half) in enumerate(items):
                    dve.wait_ge(summed, n + 1)
                    dve.wait_ge(gates_ready, len(streams))
                    cols = slice(half * 512, (half + 1) * 512)
                    nc.vector.tensor_tensor(prod[:, n % 2, :], core.ps[:, n % 6, :],
                                            grow[:, streams.index(t // 2), cols], ALU.mult).then_inc(own, 1)
                    dve.wait_ge(own, n + 1)
                    nc.vector.tensor_tensor(core.x[:, t, cols], core.x[:, t, cols], prod[:, n % 2, :],
                                            ALU.add).then_inc(added, 1)
                    if half == 0 and n >= 2:
                        norm.dve_rows(dve, n // 2 - 1)
                norm.dve_rows(dve, len(tiles) - 1)

            @block.scalar
            def _(act):
                for i in range(len(tiles)):
                    act.wait_ge(added, 2 * i + 2)
                    norm.act_square(act, i)
                    norm.act_root(act, i)


class EvenBuffers:

    def __init__(self, core, stack):
        nc = core.nc

        def sb(name, shape):
            return stack.enter_context(nc.sbuf_tensor(name, shape, F32))

        self.qaT, self.kaT, self.va, self.qb, self.qbT = (core.piece(i) for i in range(5))
        self.kvb = sb("kvb", [P, TILES, 2 * GQA_KV * HEAD])
        self.kbT = sb("kbT", [P, GQA_KV, 512])
        self.bias = sb("na_bias", [P, NA_HEADS, REL, GRID_W])
        self.rpb_rows = nc.dram_tensor("rpb_rows", (NA_HEADS * (2 * WIN_ROWS - 1), P), F32, kind="Internal").ap()


def layer_even(core, a):
    with ExitStack() as stack:
        w = EvenBuffers(core, stack)
        norm_transpose(core, 0, 0, [0, 1])
        project_even(core, a, w)
        attend_even(core, w)
        project_out(core, 0, "ab_w_out", list(range(TILES)), lambda t: slice(t * P, (t + 1) * P))


def later_tiles(NT):
    return NT // 2


def route(core, r, sw, layer, tiles):
    nc = core.nc
    NT, t0 = len(tiles), tiles[0]
    NS = NT - later_tiles(NT)
    with Stage(nc, f"route{layer}") as st:
        hrow = core.piece(2, 2)
        rw, wgu, wd, bias = sw.rw, sw.wgu, sw.wd, sw.bias
        score, picked, mask, gate = (st.sb(n, [P, NT, E]) for n in ("score", "picked", "mask", "gate"))
        work = st.sb("work", [P, NT, E])
        top = st.sb("top", [P, NT, 8])
        tot = st.sb("tot", [P, 2, NT])
        cnt = st.sb("cnt", [P, 2])
        sg, hid = st.sb("sg", [P, 2, F]), st.sb("hid", [P, 2, F])
        hidT = st.sb("hidT", [P, 2, KF, P])
        rw_in, bias_in, wgu_in, wd_in = sw.rw_in, sw.bias_in, sw.wgu_in, sw.wd_in
        logits, e_ready, mask_ready, placed, counted = (
            st.sem(n) for n in ("logits", "e_ready", "mask_ready", "placed", "counted"))
        turned, taken, rows_out = st.sem("turned"), [st.sem("taken_dve"), st.sem("taken_act")], st.sem("rows_out")
        gu_ready, silu_ready, hid_ready = st.sem("gu_ready"), st.sem("silu_ready"), st.sem("hid_ready")
        hidT_turned, hidT_ready, down_ready = st.sem("hidT_turned"), st.sem("hidT_ready"), st.sem("down_ready")
        down_taken, own = st.sem("down_taken"), st.sem("own")
        gu_bank = lambda i: (4, 1)[i % 2]
        back = [(i, half) for i in range(NT) for half in range(2)]
        with nc.Block() as block:
            @block.sync
            def _(sp):
                r.load_first_experts(sp)
                for i in range(NT):
                    sp.wait_ge(taken[0], i + 1)
                    sp.wait_ge(taken[1], i + 1)
                    sp.dma_start(r.h_rows[i * P:(i + 1) * P, :], hrow[:, i, :]).then_inc(rows_out, 16)
                sp.wait_ge(rows_out, 16 * NT)

            @block.tensor
            def _(pe):
                def h(k, i):
                    return core.hT[:, k, (t0 + i) * P:(t0 + i + 1) * P]

                pe.wait_ge(rw_in, 16)
                for i in range(NT):
                    for k in range(KD):
                        mm = nc.tensor.matmul(core.ps[:, 0, i * E:(i + 1) * E], h(k, i), rw[:, k, :],
                                              start=k == 0, stop=k == KD - 1)
                mm.then_inc(logits, 1)
                def gate_up(i):
                    pe.wait_ge(wgu_in, 32)
                    if i == 1:
                        pe.wait_ge(taken[0], NT)
                    if i >= 2:
                        pe.wait_ge(hid_ready, i - 1)
                    for k in range(KD):
                        mm = nc.tensor.matmul(core.ps[:, gu_bank(i), :], h(k, i), wgu[:, k].rearrange("p g f -> p (g f)"),
                                              start=k == 0, stop=k == KD - 1)
                    mm.then_inc(gu_ready, 1)

                def down(i):
                    pe.wait_ge(hid_ready, i + 1)
                    if i >= 1:
                        pe.wait_ge(hidT_ready, i)
                    for k in range(KF):
                        mm = nc.tensor.transpose(core.ps[:, 5, k * P:(k + 1) * P], hid[:, i % 2, k * P:(k + 1) * P],
                                                 core.c("ident"))
                    mm.then_inc(hidT_turned, 1)
                    pe.wait_ge(hidT_ready, i + 1)
                    pe.wait_ge(wd_in, 16)
                    if i >= 1:
                        pe.wait_ge(down_taken, i)
                    for half in range(2):
                        for k in range(KF):
                            mm = nc.tensor.matmul(core.ps[:, 6 + half, :], hidT[:, i % 2, k, :],
                                                  wd[:, k, half * 512:(half + 1) * 512], start=k == 0, stop=k == KF - 1)
                    mm.then_inc(down_ready, 1)

                gate_up(0)
                pe.wait_ge(mask_ready, 1)
                for i in range(NT):
                    for j in range(i + 1):
                        mm = nc.tensor.matmul(core.ps[:, 3, i * E:(i + 1) * E],
                                              core.c("before") if j == i else core.c("ones"), mask[:, j, :],
                                              start=j == 0, stop=j == i)
                mm.then_inc(placed, 1)
                for j in range(NT):
                    mm = nc.tensor.matmul(core.ps[:, 0, 0:E], core.c("ones"), mask[:, j, :], start=j == 0,
                                          stop=j == NT - 1)
                mm.then_inc(counted, 1)
                for n, (i, half) in enumerate(back):
                    if n >= 2:
                        pe.wait_ge(taken[n % 2], (n - 2) // 2 + 1)
                    for k in range(4):
                        mm = nc.tensor.transpose(core.ps[:, 1 + n % 2, k * P:(k + 1) * P], h(4 * half + k, i),
                                                 core.c("ident"))
                    mm.then_inc(turned, 1)

                for i in range(1, NS):
                    gate_up(i)
                    down(i - 1)
                down(NS - 1)

            @block.scalar
            def _(act):
                act.wait_ge(logits, 1)
                nc.scalar.activation(score[:].rearrange("p t e -> p (t e)"), core.ps[:, 0, 0:NT * E], ACT.Exp,
                                     scale=-1.0).then_inc(e_ready, 1)
                for i in range(NT):
                    act.wait_ge(turned, 2 * i + 2)
                    nc.scalar.copy(hrow[:, i, 512:D], core.ps[:, 2, :]).then_inc(taken[1], 1)
                for i in range(NS):
                    act.wait_ge(gu_ready, i + 1)
                    if i >= 2:
                        act.wait_ge(hid_ready, i - 1)
                    nc.scalar.activation(sg[:, i % 2, :], core.ps[:, gu_bank(i), 0:F], ACT.Silu).then_inc(silu_ready, 1)

            @block.vector
            def _(dve):
                link = Chain(dve, own)
                dve.wait_ge(e_ready, 1)
                link(nc.vector.tensor_scalar(score[:], score[:], 1.0, None, ALU.add))
                link(nc.vector.reciprocal(score[:], score[:]))
                dve.wait_ge(bias_in, 16)
                link(nc.vector.tensor_tensor(picked[:], score[:], bias[:].rearrange("p (o e) -> p o e", o=1)
                                             .to_broadcast([P, NT, E]), ALU.add))
                for i in range(NT):
                    ins = nc.vector.max(top[:, i, :], picked[:, i, :])
                link(ins)
                for i in range(NT):
                    ins = nc.vector.match_replace(work[:, i, :], top[:, i, :], picked[:, i, :], MASKED)
                link(ins)
                nc.vector.tensor_tensor(mask[:], picked[:], work[:], ALU.not_equal).then_inc(mask_ready, 1)
                dve.wait_ge(mask_ready, 1)
                link(nc.vector.tensor_tensor(gate[:], score[:], mask[:], ALU.mult))
                link(nc.vector.tensor_reduce(tot[:, 0, :], gate[:], AX, ALU.add))
                link(nc.vector.reciprocal(tot[:, 1, :], tot[:, 0, :]))
                link(nc.vector.tensor_tensor(gate[:], gate[:], tot[:, 1, :].rearrange("p (t o) -> p t o", o=1)
                                             .to_broadcast([P, NT, E]), ALU.mult))
                link(nc.vector.tensor_scalar(gate[:], gate[:], ROUTED_SCALE, None, ALU.mult))
                for i in range(NT):
                    dve.wait_ge(turned, 2 * i + 1)
                    nc.vector.tensor_copy(hrow[:, i, 0:512], core.ps[:, 1, :]).then_inc(taken[0], 1)

                def hidden(i):
                    dve.wait_ge(silu_ready, i + 1)
                    nc.vector.tensor_tensor(hid[:, i % 2, :], sg[:, i % 2, :], core.ps[:, gu_bank(i), F:2 * F],
                                            ALU.mult).then_inc(hid_ready, 1)
                    dve.wait_ge(hidT_turned, i + 1)
                    nc.vector.tensor_copy(hidT[:, i % 2].rearrange("p k c -> p (k c)"),
                                          core.ps[:, 5, 0:F]).then_inc(hidT_ready, 1)
                    dve.wait_ge(down_ready, i + 1)
                    nc.vector.tensor_copy(r.shared[:, i, :].rearrange("p (h c) -> p h c", h=2),
                                          core.ps[:, 6:8, :]).then_inc(down_taken, 1)

                dve.wait_ge(placed, 1)
                pos = core.ps[:, 3, 0:NT * E].rearrange("p (t e) -> p t e", e=E)
                link(nc.vector.scalar_tensor_tensor(out=work[:], in0=pos, scalar=1.0, in1=mask[:], op0=ALU.add,
                                                    op1=ALU.mult))
                link(nc.vector.tensor_scalar(r.place[:], work[:], -1.0, None, ALU.add))
                dve.wait_ge(counted, 1)
                link(nc.vector.tensor_reduce(cnt[:, 0:1], core.ps[:, 0, 0:E], AX, ALU.max))
                link(nc.vector.tensor_copy(r.longest[:], cnt[:, 0:1]))
                for i in range(NT):
                    ins = nc.vector.tensor_tensor_scan(work[:, i, :], core.c("ones")[:, 0:E], mask[:, i, :], 0.0,
                                                       ALU.mult, ALU.add)
                link(ins)
                info = r.slot_info
                nc.vector.tensor_scalar(info[:, :, :, 2, 2], work[:], -1.0, None, ALU.add)
                link(nc.vector.tensor_copy(info[:, :, :, 0, 0], gate[:]))
                link(nc.vector.tensor_tensor(gate[:], gate[:], info[:, :, :, 0, 0], ALU.subtract))
                link(nc.vector.tensor_copy(info[:, :, :, 0, 1], gate[:]))
                link(nc.vector.tensor_tensor(gate[:], gate[:], info[:, :, :, 0, 1], ALU.subtract))
                link(nc.vector.tensor_copy(info[:, :, :, 0, 2], gate[:]))
                nc.vector.memset(info[:, :, :, 1, 2], 0.0)
                for i in range(NT):
                    for c, name in ((1, "tok"), (2, "dest")):
                        for s, v in ((0, core.c(name + "_hi")[:, i:i + 1]), (1, core.c(name + "_lo"))):
                            ins = nc.vector.tensor_copy(info[:, i, :, c, s], v.to_broadcast([P, E]))
                link(ins)
                for i in range(NS):
                    hidden(i)


class SharedWeights:

    def __init__(self, core, stack, a, layer):
        nc = core.nc

        def sb(name, shape):
            return stack.enter_context(nc.sbuf_tensor(f"{name}{layer}", shape, F32))

        self.a, self.layer = a, layer
        self.rw, self.bias = sb("rw", [P, KD, E]), sb("rbias", [P, E])
        self.wgu, self.wd = sb("sh_wgu", [P, KD, 2, F]), sb("sh_wd", [P, KF, D])
        self.rw_in, self.bias_in, self.wgu_in, self.wd_in = (
            nc.alloc_semaphore(f"{n}{layer}") for n in ("rw_in", "bias_in", "wgu_in", "wd_in"))

    def load(self, sp):
        a, layer = self.a, self.layer
        sp.dma_start(self.rw[:], a["router_w"][layer].rearrange("(k p) e -> p k e", p=P)).then_inc(self.rw_in, 16)
        sp.dma_start(self.bias[:], a["router_bias"][layer:layer + 1, :].to_broadcast([P, E])).then_inc(self.bias_in, 16)
        for i, name in enumerate(("shared_w_gate", "shared_w_up")):
            sp.dma_start(self.wgu[:, :, i, :], a[name][layer].rearrange("(k p) f -> p k f", p=P)).then_inc(self.wgu_in, 16)
        sp.dma_start(self.wd[:], a["shared_w_down"][layer].rearrange("(k p) d -> p k d", p=P)).then_inc(self.wd_in, 16)


class Routing:

    def __init__(self, core, stack, a, layer, NT):
        nc = core.nc

        def sb(name, shape, dt=F32):
            return stack.enter_context(nc.sbuf_tensor(f"{name}{layer}", shape, dt))

        self.place = sb("place", [P, NT, E])
        self.slot_info = sb("slot_info", [P, NT, E, 3, 3], BF16)
        self.shared = sb("shared", [P, NT, D])
        self.longest = sb("longest", [P, 1], I32)
        self.h_rows = nc.dram_tensor(f"h_rows{layer}", (NT * P, D), F32, kind="Internal").ap()
        self.wgu = core.wb[:].rearrange("p s (i n) -> p s i n", i=2)
        self.gu_in = [nc.alloc_semaphore(f"gu_in{layer}_{i}") for i in range(RING)]

        def grouped(t):
            return t[layer].rearrange("(g s) (p k) f -> s g p (k f)", s=GROUP, p=P)

        self.gate_src, self.up_src = grouped(a["expert_w_gate"]), grouped(a["expert_w_up"])
        self.down_src = grouped(a["expert_w_down"])
        self.y_rows = nc.dram_tensor(f"y_rows{layer}", (NT * P * TOP_K, D), F32, kind="Internal").ap()


    def load_first_experts(self, sp):
        for e in range(RING):
            for i, src in enumerate((self.gate_src, self.up_src)):
                sp.dma_start(self.wgu[:, e, i, :], src[e, 0]).then_inc(self.gu_in[e], 16)


RING = 4
GROUP = 8
GROUPS = E // GROUP


def experts(core, r, sw, layer, tiles):
    nc = core.nc
    NT = len(tiles)
    T = NT * P
    with Stage(nc, f"moe{layer}") as st:
        wgu = r.wgu
        wd = core.pool[:, 0:2, :]
        wd_more = core.hT[:].rearrange("p (r k) t -> p r (k t)", r=RING // 2)
        onehot = st.sb("onehot", [P, 2, NT, SLOTS], BF16)
        info = st.sb("info", [P, GROUP, 3])
        index = st.sb("index", [P, GROUP, 2], I32)
        xs = core.piece(2, 2)
        xT = core.pool[:, 4, :].rearrange("p (i k c) -> p i k c", i=2, k=KD)
        sg, hid = st.sb("sg", [P, 2, F]), st.sb("hid", [P, 2, F])
        hidT = st.sb("hidT", [P, 2, KF, SLOTS])
        y = st.sb("y", [P, 2, D])
        gu_in = r.gu_in
        d_in = [st.sem(f"d_in{i}") for i in range(RING)]
        gathered = [st.pool_sem(f"gathered{i}") for i in range(RING)]
        scattered = [st.pool_sem(f"scattered{i}") for i in range(2)]
        cleared, gathers, scatters = st.sem("cleared"), st.sem("gathers"), st.sem("scatters")
        hot_ready, info_sum, info_ready, index_ready = (
            st.sem(n) for n in ("hot_ready", "info_sum", "info_ready", "index_ready"))
        x_turned, xT_dve, xT_act = st.sem("x_turned"), st.sem("xT_dve"), st.sem("xT_act")
        gu_ready, silu_ready, hid_ready = st.sem("gu_ready"), st.sem("silu_ready"), st.sem("hid_ready")
        hid_turned, hidT_ready, down_ready = st.sem("hid_turned"), st.sem("hidT_ready"), st.sem("down_ready")
        y_dve, y_act = st.sem("y_dve"), st.sem("y_act")
        sh_gu, sh_silu, sh_hid, sh_turned, sh_hidT, sh_down, sh_taken = (
            st.sem(n) for n in ("sh_gu", "sh_silu", "sh_hid", "sh_turned", "sh_hidT", "sh_down", "sh_taken"))
        LATER = later_tiles(NT)
        later = list(range(NT - LATER, NT))

        def wd_at(s):
            i, half = s % RING, RING // 2
            return wd[:, i, :] if i < half else wd_more[:, i - half, :]

        bounds = []

        def sp_step(sp, g, s, base, first):
            def of(src):
                return src[s, g] if isinstance(g, int) else src[s, bass.ds(g, 1)].rearrange("o p n -> (o p) n")

            if not first:
                sp.wait_ge(gu_ready, base + GROUP * g + s - RING + 1)
                sp.dma_start(wgu[:, s % RING, 0, :], of(r.gate_src)).then_inc(gu_in[s % RING], 16)
                sp.dma_start(wgu[:, s % RING, 1, :], of(r.up_src)).then_inc(gu_in[s % RING], 16)
                sp.wait_ge(down_ready, base + GROUP * g + s - RING + 1)
            if first and s == RING // 2:
                sp.wait_ge(sh_gu, LATER)
            sp.dma_start(wd_at(s), of(r.down_src)).then_inc(d_in[s % RING], 16)

        def pool_gather(pool, g, s, base, first):
            n = base + GROUP * g + s
            if not first:
                pool.wait_ge(x_turned, n - RING + 1)
            pool.wait_ge(index_ready, n + 1)
            pool.sem_inc(gathers, 1)
            pool.indirect_dma_start(out=xs[:, s % RING, :], out_offset=None, in_=r.h_rows,
                                    in_offset=bass.IndirectOffsetOnAxis(ap=index[:, s, 0:1], axis=0),
                                    bounds_check=bounds[0], oob_is_err=False).then_inc(gathered[s % RING], 16)

        def pool_scatter(pool, g, s, base):
            n = base + GROUP * g + s
            pool.wait_ge(y_dve, n + 1)
            pool.wait_ge(y_act, n + 1)
            pool.sem_inc(scatters, 1)
            pool.indirect_dma_start(out=r.y_rows, out_offset=bass.IndirectOffsetOnAxis(ap=index[:, s, 1:2], axis=0),
                                    in_=y[:, s % 2, :], in_offset=None, bounds_check=bounds[1],
                                    oob_is_err=False).then_inc(scattered[s % 2], 16)

        def dve_hot(dve, g, s, base, block_at, first):
            n = base + GROUP * g + s
            if not first:
                dve.wait_ge(info_sum, n - 1)
            iota = core.c("iota")
            slots = iota[:, block_at * SLOTS:(block_at + 1) * SLOTS] if isinstance(block_at, int) else \
                iota[:, bass.ds(block_at * SLOTS, SLOTS)]
            e = GROUP * g + s
            for i in range(NT):
                where = r.place[:, i, e:e + 1] if isinstance(g, int) else r.place[:, i, bass.ds(e, 1)]
                ins = nc.vector.tensor_scalar(onehot[:, s % 2, i, :], slots, where, None, ALU.is_equal)
            ins.then_inc(hot_ready, 1)

        def pe_info(pe, g, s, base, first):
            n = base + GROUP * g + s
            pe.wait_ge(hot_ready, n + 1)
            if not first:
                pe.wait_ge(info_ready, n)
            flat = r.slot_info[:].rearrange("p t e c s -> p t (e c s)")
            for i in range(NT):
                at = 9 * (GROUP * g + s)
                rhs = flat[:, i, at:at + 9] if isinstance(g, int) else flat[:, i, bass.ds(at, 9)]
                mm = nc.tensor.matmul(core.ps[:, 7, 0:9], onehot[:, s % 2, i, :], rhs, start=i == 0, stop=i == NT - 1)
            mm.then_inc(info_sum, 1)

        def dve_info(dve, g, s, base, first):
            n = base + GROUP * g + s
            dve.wait_ge(info_sum, n + 1)
            if not first:
                dve.wait_ge(scattered[s % 2], 8 * (base + GROUP * g) + 16 * (s // 2) + 16 - 8 * GROUP)
            nc.vector.tensor_reduce(info[:, s, :], core.ps[:, 7, 0:9].rearrange("p (c s) -> p c s", s=3), AX,
                                    ALU.add).then_inc(info_ready, 1)
            dve.wait_ge(info_ready, n + 1)
            nc.vector.tensor_scalar(index[:, s, :], info[:, s, 1:3], float(BIG), None, ALU.add).then_inc(index_ready, 1)

        def pe_turn(pe, g, s, base, first):
            n = base + GROUP * g + s
            pe.wait_ge(gathered[s % RING], 4 * (base + GROUP * g) + 16 * (s // RING) + 16)
            if not first:
                pe.wait_ge(xT_dve, n)
                pe.wait_ge(xT_act, n)
            for k in range(KD):
                mm = nc.tensor.transpose(core.ps[:, 4 + k // 4, (k % 4) * P:(k % 4 + 1) * P],
                                         xs[:, s % RING, k:D:KD], core.c("ident"))
            mm.then_inc(x_turned, 1)

        def take_x(eng, bank, g, s, base, first):
            n = base + GROUP * g + s
            eng.wait_ge(x_turned, n + 1)
            if not first:
                eng.wait_ge(gu_ready, n - 1)
            out = xT[:, s % 2, 4 * bank:4 * bank + 4, :].rearrange("p k c -> p (k c)")
            if bank == 0:
                nc.vector.tensor_copy(out, core.ps[:, 4, :]).then_inc(xT_dve, 1)
            else:
                nc.scalar.copy(out, core.ps[:, 5, :]).then_inc(xT_act, 1)

        def pe_gate_up(pe, g, s, base, first):
            n = base + GROUP * g + s
            pe.wait_ge(gu_in[s % RING], 8 * (base + GROUP * g) + 32 * (s // RING) + 32)
            pe.wait_ge(xT_dve, n + 1)
            pe.wait_ge(xT_act, n + 1)
            if not first:
                pe.wait_ge(hid_ready, n - 1)
            w = wgu[:, s % RING].rearrange("p i (k f) -> p k i f", f=F)
            for k in range(KD):
                mm = nc.tensor.matmul(core.ps[:, s % 2, :], xT[:, s % 2, k, :], w[:, k], start=k == 0,
                                      stop=k == KD - 1)
            mm.then_inc(gu_ready, 1)

        def act_silu(act, g, s, base, first):
            n = base + GROUP * g + s
            act.wait_ge(gu_ready, n + 1)
            if not first:
                act.wait_ge(hid_ready, n - 1)
            nc.scalar.activation(sg[:, s % 2, :], core.ps[:, s % 2, 0:F], ACT.Silu).then_inc(silu_ready, 1)

        def dve_hidden(dve, g, s, base, first):
            n = base + GROUP * g + s
            dve.wait_ge(silu_ready, n + 1)
            if not first:
                dve.wait_ge(hid_turned, n - 1)
            nc.vector.tensor_tensor(hid[:, s % 2, :], sg[:, s % 2, :], core.ps[:, s % 2, F:2 * F],
                                    ALU.mult).then_inc(hid_ready, 1)

        def pe_turn_hidden(pe, g, s, base, first):
            n = base + GROUP * g + s
            pe.wait_ge(hid_ready, n + 1)
            if not first:
                pe.wait_ge(hidT_ready, n)
            for k in range(KF):
                mm = nc.tensor.transpose(core.ps[:, 6, k * P:(k + 1) * P], hid[:, s % 2, k:F:KF], core.c("ident"))
            mm.then_inc(hid_turned, 1)

        def dve_take_hidden(dve, g, s, base, first):
            n = base + GROUP * g + s
            dve.wait_ge(hid_turned, n + 1)
            if not first:
                dve.wait_ge(down_ready, n - 1)
            nc.vector.tensor_copy(hidT[:, s % 2].rearrange("p k c -> p (k c)"), core.ps[:, 6, 0:F]).then_inc(hidT_ready, 1)

        def pe_down(pe, g, s, base, first):
            n = base + GROUP * g + s
            pe.wait_ge(hidT_ready, n + 1)
            pe.wait_ge(d_in[s % RING], 4 * (base + GROUP * g) + 16 * (s // RING) + 16)
            if not first:
                pe.wait_ge(y_dve, n)
                pe.wait_ge(y_act, n)
            else:
                pe.wait_ge(sh_taken, LATER)
            for half in range(2):
                for k in range(KF):
                    mm = nc.tensor.matmul(core.ps[:, 2 + half, :], hidT[:, s % 2, k, :],
                                          wd_at(s)[:, k * D + half * 512:k * D + half * 512 + 512], start=k == 0,
                                          stop=k == KF - 1)
            mm.then_inc(down_ready, 1)

        def take_y(eng, half, g, s, base, first):
            n = base + GROUP * g + s
            eng.wait_ge(down_ready, n + 1)
            if not first:
                eng.wait_ge(scattered[s % 2], 8 * (base + GROUP * g) + 16 * (s // 2))
            out, src, gate = y[:, s % 2, half * 512:(half + 1) * 512], core.ps[:, 2 + half, :], info[:, s, 0:1]
            if half == 0:
                nc.vector.tensor_scalar(out, src, gate, None, ALU.mult).then_inc(y_dve, 1)
            else:
                nc.scalar.activation(out, src, ACT.Copy, scale=gate).then_inc(y_act, 1)

        def pe_shared_gate_up(pe, j):
            i = tiles[0] + later[j]
            for k in range(KD):
                mm = nc.tensor.matmul(core.ps[:, j, :], core.hT[:, k, i * P:(i + 1) * P],
                                      sw.wgu[:, k].rearrange("p g f -> p (g f)"), start=k == 0, stop=k == KD - 1)
            mm.then_inc(sh_gu, 1)

        def pe_shared_down(pe, j):
            pe.wait_ge(sh_hid, j + 1)
            for k in range(KF):
                mm = nc.tensor.transpose(core.ps[:, 6, k * P:(k + 1) * P], hid[:, j, k * P:(k + 1) * P], core.c("ident"))
            mm.then_inc(sh_turned, 1)
            pe.wait_ge(sh_hidT, j + 1)
            if j >= 1:
                pe.wait_ge(sh_taken, j)
            for half in range(2):
                for k in range(KF):
                    mm = nc.tensor.matmul(core.ps[:, 2 + half, :], hidT[:, j, k, :],
                                          sw.wd[:, k, half * 512:(half + 1) * 512], start=k == 0, stop=k == KF - 1)
            mm.then_inc(sh_down, 1)

        def act_shared_silu(act, j):
            act.wait_ge(sh_gu, j + 1)
            nc.scalar.activation(sg[:, j, :], core.ps[:, j, 0:F], ACT.Silu).then_inc(sh_silu, 1)

        def dve_shared_hidden(dve, j):
            dve.wait_ge(sh_silu, j + 1)
            nc.vector.tensor_tensor(hid[:, j, :], sg[:, j, :], core.ps[:, j, F:2 * F], ALU.mult).then_inc(sh_hid, 1)

        def dve_shared_take(dve, j):
            dve.wait_ge(sh_turned, j + 1)
            nc.vector.tensor_copy(hidT[:, j].rearrange("p k c -> p (k c)"), core.ps[:, 6, 0:F]).then_inc(sh_hidT, 1)
            dve.wait_ge(sh_down, j + 1)
            nc.vector.tensor_copy(r.shared[:, later[j], :].rearrange("p (h c) -> p h c", h=2),
                                  core.ps[:, 2:4, :]).then_inc(sh_taken, 1)

        def at(g, s, ahead):
            return g + (s + ahead) // GROUP, (s + ahead) % GROUP

        def run(eng, step):
            for s in range(GROUP):
                step(0, s, s)
            with eng.Fori(1, GROUPS - 1) as g:
                for s in range(GROUP):
                    step(g, s, None)
            for s in range(GROUP):
                step(GROUPS - 1, s, E - GROUP + s)

        def inside(e, ahead):
            return e is None or 0 <= e + ahead < E

        def early(e, ahead, ring, base_is_zero):
            return base_is_zero and e is not None and e + ahead < ring

        def sp_pass(sp, base, z):
            def step(g, s, e):
                sp_step(sp, g, s, base, early(e, 0, RING, z))
            run(sp, step)

        def pool_pass(pool, base, z):
            for e in range(2):
                pool_gather(pool, 0, e, base, early(e, 0, RING, z))

            def step(g, s, e):
                if inside(e, 2):
                    pool_gather(pool, *at(g, s, 2), base, early(e, 2, RING, z))
                if inside(e, -2):
                    pool_scatter(pool, *at(g, s, -2), base)
            run(pool, step)
            for s in range(GROUP - 2, GROUP):
                pool_scatter(pool, GROUPS - 1, s, base)

        def dve_pass(dve, base, z, blk):
            def hot(e, g, s):
                dve_hot(dve, g, s, base, blk, early(e, 0, 2, z))

            def slots(e, g, s):
                dve_info(dve, g, s, base, early(e, 0, GROUP, z))

            for e in range(2):
                hot(e, 0, e)
                slots(e, 0, e)
            hot(2, 0, 2)
            for j in range(LATER if z else 0):
                dve_shared_hidden(dve, j)
            take_x(dve, 0, 0, 0, base, z)
            for j in range(LATER if z else 0):
                dve_shared_take(dve, j)

            def step(g, s, e):
                up = (lambda k: None) if e is None else (lambda k: e + k)
                if inside(e, 2):
                    slots(up(2), *at(g, s, 2))
                if inside(e, 3):
                    hot(up(3), *at(g, s, 3))
                if inside(e, 1):
                    take_x(dve, 0, *at(g, s, 1), base, early(e, 1, 2, z))
                dve_hidden(dve, g, s, base, early(e, 0, 2, z))
                if inside(e, -1):
                    take_y(dve, 0, *at(g, s, -1), base, early(e, -1, 2, z))
                dve_take_hidden(dve, g, s, base, early(e, 0, 2, z))
            run(dve, step)
            take_y(dve, 0, GROUPS - 1, GROUP - 1, base, False)

        def act_pass(act, base, z):
            for j in range(LATER if z else 0):
                act_shared_silu(act, j)
            take_x(act, 1, 0, 0, base, z)

            def step(g, s, e):
                if inside(e, 1):
                    take_x(act, 1, *at(g, s, 1), base, early(e, 1, 2, z))
                act_silu(act, g, s, base, early(e, 0, 2, z))
                if inside(e, -1):
                    take_y(act, 1, *at(g, s, -1), base, early(e, -1, 2, z))
            run(act, step)
            take_y(act, 1, GROUPS - 1, GROUP - 1, base, False)

        def pe_pass(pe, base, z):
            for e in range(2):
                pe_info(pe, 0, e, base, early(e, 0, 1, z))
            for j in range(LATER if z else 0):
                pe_shared_gate_up(pe, j)
            pe_turn(pe, 0, 0, base, z)
            for j in range(LATER if z else 0):
                pe_shared_down(pe, j)

            def step(g, s, e):
                if inside(e, 2):
                    pe_info(pe, *at(g, s, 2), base, early(e, 2, 1, z))
                if inside(e, 1):
                    pe_turn(pe, *at(g, s, 1), base, early(e, 1, 1, z))
                pe_gate_up(pe, g, s, base, early(e, 0, 2, z))
                if inside(e, -1):
                    pe_down(pe, *at(g, s, -1), base, early(e, -1, 1, z))
                pe_turn_hidden(pe, g, s, base, early(e, 0, 1, z))
            run(pe, step)
            pe_down(pe, GROUPS - 1, GROUP - 1, base, False)

        def further(eng, body):
            longest = eng.value_load(r.longest[0:1, 0:1], min_val=0, max_val=T)
            with eng.If(longest > SLOTS):
                with eng.Fori(1, T // SLOTS) as b:
                    body(b * E, b)

        with nc.Block() as block:
            @block.sync
            def _(sp):
                sp_pass(sp, 0, True)
                further(sp, lambda base, b: sp_pass(sp, base, False))

            @block.gpsimd
            def _(pool):
                last_row, last_out = pool.to_reg(T - 1), pool.to_reg(T * TOP_K - 1)
                bounds[:] = [last_row, last_out]
                nc.gpsimd.memset(xs[:], 0.0).then_inc(cleared, 1)
                pool.wait_ge(cleared, 1)
                pool_pass(pool, 0, True)
                further(pool, lambda base, b: pool_pass(pool, base, False))
                for i in range(2):
                    pool.wait_ge(scattered[i], 16 * (E // 2))

            @block.scalar
            def _(act):
                act_pass(act, 0, True)
                further(act, lambda base, b: act_pass(act, base, False))

            @block.vector
            def _(dve):
                dve_pass(dve, 0, True, 0)
                further(dve, lambda base, b: dve_pass(dve, base, False, b))

            @block.tensor
            def _(pe):
                pe_pass(pe, 0, True)
                further(pe, lambda base, b: pe_pass(pe, base, False))


def combine(core, r, layer, tiles):
    nc = core.nc
    streams = sorted({t // 2 for t in tiles})
    with Stage(nc, f"combine{layer}") as st:
        yr = core.wb[:].rearrange("p (i s) (k d) -> p i (s k) d", i=2, d=D)
        diag = st.sb("diag", [P, KD, P])
        grow = st.sb("grow", [P, len(streams), D])
        norm = RowNorm(core, st, tiles)
        y_in = [st.sem("y_in0"), st.sem("y_in1")]
        diag_ready, spread, gates_ready = st.sem("diag_ready"), st.sem("spread"), st.sem("gates_ready")
        own, summed, pool_own, pool_summed = st.sem("own"), st.sem("summed"), st.sem("pool_own"), st.sem("pool_summed")
        y_view = r.y_rows.rearrange("(t p k) d -> t p k d", p=P, k=TOP_K)
        with nc.Block() as block:
            @block.sync
            def _(sp):
                for i in range(len(tiles)):
                    if i >= 2:
                        sp.wait_ge(summed, i - 1)
                    sp.dma_start(yr[:, i % 2], y_view[i]).then_inc(y_in[i % 2], 16)

            @block.tensor
            def _(pe):
                for i in range(len(streams)):
                    pe.wait_ge(diag_ready, i + 1)
                    if i >= 1:
                        pe.wait_ge(gates_ready, i)
                    for k in range(KD):
                        mm = nc.tensor.matmul(core.ps[:, k // 4, (k % 4) * P:(k % 4 + 1) * P], core.c("ones"),
                                              diag[:, k, :], start=True, stop=True)
                    mm.then_inc(spread, 1)

            @block.gpsimd
            def _(pool):
                link = Chain(pool, pool_own)
                for i in range(len(tiles)):
                    pool.wait_ge(y_in[i % 2], 16 * (i // 2 + 1))
                    v = yr[:, i % 2]
                    link(nc.gpsimd.tensor_tensor(v[:, 0], v[:, 0], v[:, 1], ALU.add))
                    nc.gpsimd.tensor_tensor(v[:, 0], v[:, 0], v[:, 2], ALU.add).then_inc(pool_summed, 1)

            @block.vector
            def _(dve):
                link = Chain(dve, own)
                for i, s in enumerate(streams):
                    if i >= 1:
                        dve.wait_ge(spread, i)
                    for k in range(KD):
                        ins = nc.vector.tensor_scalar(diag[:, k, :], core.c("ident"), core.gate_column(layer, 1, s, k),
                                                      None, ALU.mult)
                    ins.then_inc(diag_ready, 1)
                    dve.wait_ge(spread, i + 1)
                    nc.vector.tensor_copy(grow[:, i, :].rearrange("p (h c) -> p h c", h=2),
                                          core.ps[:, 0:2, :]).then_inc(gates_ready, 1)
                for i, t in enumerate(tiles):
                    dve.wait_ge(y_in[i % 2], 16 * (i // 2 + 1))
                    v = yr[:, i % 2]
                    link(nc.vector.tensor_tensor(v[:, 4:6], v[:, 4:6], v[:, 6:8], ALU.add))
                    nc.vector.tensor_tensor(v[:, 3], v[:, 3], r.shared[:, i, :], ALU.add)
                    link(nc.vector.tensor_tensor(v[:, 4], v[:, 4], v[:, 5], ALU.add))
                    link(nc.vector.tensor_tensor(v[:, 3], v[:, 3], v[:, 4], ALU.add))
                    dve.wait_ge(pool_summed, i + 1)
                    link(nc.vector.tensor_tensor(v[:, 3], v[:, 3], v[:, 0], ALU.add))
                    if i == 0:
                        dve.wait_ge(gates_ready, len(streams))
                    link(nc.vector.tensor_tensor(v[:, 3], v[:, 3], grow[:, streams.index(t // 2), :], ALU.mult))
                    nc.vector.tensor_tensor(core.x[:, t, :], core.x[:, t, :], v[:, 3], ALU.add).then_inc(summed, 1)
                    norm.dve_rows(dve, i)

            @block.scalar
            def _(act):
                for i in range(len(tiles)):
                    act.wait_ge(summed, i + 1)
                    norm.act_square(act, i)
                    norm.act_root(act, i)


def moe(core, a, layer, tiles, r):
    with ExitStack() as stack:
        sw = SharedWeights(core, stack, a, layer)
        norm_transpose(core, layer, 1, sorted({t // 2 for t in tiles}), sw.load)
        route(core, r, sw, layer, tiles)
        experts(core, r, sw, layer, tiles)


def combine_project(core, r, w):
    nc = core.nc
    COLS = BLOCK
    HALF = TOP_K // 2
    first = core.stream.start["diff_w_kv"]
    kv = 2 * D // COLS
    with Stage(nc, "mix1") as st:
        yr = st.sb("yr", [P, 2, HALF, D])
        diag = core.pool[:, 4, 0:D].rearrange("p (k c) -> p k c", k=KD)
        grow = st.sb("grow", [P, STREAMS, D])
        ss, rs = st.sb("ss", [P, TILES]), st.sb("rs", [P, 3, TILES])
        y_in = [st.sem("y_in0"), st.sem("y_in1")]
        y_used, x_ready, own = st.sem("y_used"), st.sem("x_ready"), st.sem("own")
        diag_ready, spread, gates_ready = st.sem("diag_ready"), st.sem("spread"), st.sem("gates_ready")
        sq_ready, var_ready, root_ready, row_ready = (st.sem(n) for n in ("sq", "var", "root", "row"))
        turned, h_dve, h_act = st.sem("turned"), st.sem("h_dve"), st.sem("h_act")
        summed, kv_taken, q_taken = st.sem("summed"), st.sem("kv_taken"), st.sem("q_taken")
        y_view = r.y_rows.rearrange("(t p k) d -> t p k d", p=P, k=TOP_K)
        items = [(t, b) for t in range(TILES) for b in range(kv)] + [(t, kv + b) for t in (2, 3) for b in range(2)]
        xn = r.shared

        def h_part(t, k):
            return core.hT[:, k, t * P:(t + 1) * P], core.ps[:, 6 + k // 4, (k % 4) * P:(k % 4 + 1) * P], \
                core.amp[:, 1, 0, t // 2, k:k + 1], core.shift_column(1, 0, t // 2, k)

        def last_use(b):
            return max(n for n, (_, x) in enumerate(items) if x == b) + 1

        with nc.Block() as block:
            @block.sync
            def _(sp):
                def rows(n):
                    if n >= 2:
                        sp.wait_ge(y_used, n - 1)
                    sp.dma_start(yr[:, n % 2], y_view[n // 2][:, HALF * (n % 2):HALF * (n % 2 + 1), :]).then_inc(y_in[n % 2], 16)

                rows(0)
                rows(1)
                core.stream.feed(sp, first + 1, first)
                rows(2)
                core.stream.feed(sp, first + 2, first)
                rows(3)
                core.stream.feed(sp, first + kv, first)
                for n in range(4, 2 * TILES):
                    rows(n)
                core.stream.feed(sp, core.stream.end["diff_w_out"], first, lambda b: (summed, last_use(b)))

            @block.tensor
            def _(pe):
                def turn(t):
                    pe.wait_ge(row_ready, t + 1)
                    if t >= 1:
                        pe.wait_ge(h_dve, t)
                        pe.wait_ge(h_act, t)
                    for k in range(KD):
                        mm = nc.tensor.transpose(core.ps[:, 6 + k // 4, (k % 4) * P:(k % 4 + 1) * P],
                                                 xn[:, t, k * P:(k + 1) * P], core.c("ident"))
                        if k % 4 == 3:
                            mm.then_inc(turned, 1)

                for s in range(STREAMS):
                    pe.wait_ge(diag_ready, s + 1)
                    if s >= 1:
                        pe.wait_ge(gates_ready, s)
                    for k in range(KD):
                        mm = nc.tensor.matmul(core.ps[:, k // 4, (k % 4) * P:(k % 4 + 1) * P], core.c("ones"),
                                              diag[:, k, :], start=True, stop=True)
                    mm.then_inc(spread, 1)
                pe.wait_ge(gates_ready, STREAMS)
                turn(0)
                for n, (t, b) in enumerate(items):
                    if n < kv * TILES and b == 0:
                        pe.wait_ge(h_dve, t + 1)
                        pe.wait_ge(h_act, t + 1)
                    if n < kv * TILES and b == kv - 1 and t + 1 < TILES:
                        turn(t + 1)
                    wb = core.stream.take(pe, first + b)
                    if n >= 6:
                        pe.wait_ge(kv_taken, n - 5)
                    for k in range(KD):
                        mm = nc.tensor.matmul(core.ps[:, n % 6, :], core.hT[:, k, t * P:(t + 1) * P],
                                              wb[:, k, :], start=k == 0, stop=k == KD - 1)
                    mm.then_inc(summed, 1)

            @block.vector
            def _(dve):
                link = Chain(dve, own)
                for s in range(STREAMS):
                    if s >= 1:
                        dve.wait_ge(spread, s)
                    for k in range(KD):
                        ins = nc.vector.tensor_scalar(diag[:, k, :], core.c("ident"), core.gate_column(0, 1, s, k),
                                                      None, ALU.mult)
                    ins.then_inc(diag_ready, 1)
                    dve.wait_ge(spread, s + 1)
                    nc.vector.tensor_copy(grow[:, s, :].rearrange("p (h c) -> p h c", h=2),
                                          core.ps[:, 0:2, :]).then_inc(gates_ready, 1)
                dve.wait_ge(gates_ready, STREAMS)
                for t in range(TILES):
                    acc = r.shared[:, t, :]
                    for half in range(2):
                        dve.wait_ge(y_in[half], 16 * (t + 1))
                        v = yr[:, half]
                        link(nc.vector.tensor_tensor(v[:, 0:2], v[:, 0:2], v[:, 2:4], ALU.add))
                        link(nc.vector.tensor_tensor(acc, acc, v[:, 0], ALU.add))
                        nc.vector.tensor_tensor(acc, acc, v[:, 1], ALU.add).then_inc(y_used, 1)
                        dve.wait_ge(y_used, 2 * t + half + 1)
                    link(nc.vector.tensor_tensor(acc, acc, grow[:, t // 2, :], ALU.mult))
                    nc.vector.tensor_tensor(core.x[:, t, :], core.x[:, t, :], acc, ALU.add).then_inc(x_ready, 1)
                    dve.wait_ge(sq_ready, t + 1)
                    nc.vector.tensor_scalar(rs[:, 0, t:t + 1], ss[:, t:t + 1], 1.0 / D, EPS, ALU.mult,
                                            ALU.add).then_inc(var_ready, 1)
                    dve.wait_ge(root_ready, t + 1)
                    link(nc.vector.reciprocal(rs[:, 2, t:t + 1], rs[:, 1, t:t + 1]))
                    nc.vector.tensor_scalar(xn[:, t, :], core.x[:, t, :], rs[:, 2, t:t + 1], None,
                                            ALU.mult).then_inc(row_ready, 1)
                    dve.wait_ge(turned, 2 * t + 1)
                    for k in range(4):
                        out, src, amp, shift = h_part(t, k)
                        ins = nc.vector.tensor_scalar(out, src, amp, shift, ALU.mult, ALU.add)
                    ins.then_inc(h_dve, 1)
                tmp = yr[:, 0, 0:2, :].rearrange("p i (j c) -> p (i j) c", j=2)

                def turn_pairs(x, t):
                    cos = core.c("cos")[:, (t - 2) * ROPE:(t - 1) * ROPE]
                    sin = core.c("sin")[:, (t - 2) * ROPE:(t - 1) * ROPE]
                    rotate(nc, link, x.rearrange("p (h r two) -> p h r two", r=ROPE, two=2), tmp, cos, sin)

                for t in (2, 3):
                    dve.wait_ge(kv_taken, kv * t + 2)
                    turn_pairs(w.k[:, t, :], t)
                for n in range(kv * TILES, len(items)):
                    t, b = items[n]
                    dve.wait_ge(summed, n + 1)
                    nc.vector.tensor_scalar(w.q[:, t - 2, (b - kv) * COLS:(b - kv + 1) * COLS], core.ps[:, n % 6, :],
                                            SCALE, None, ALU.mult).then_inc(q_taken, 1)
                    if b == kv + 1:
                        dve.wait_ge(q_taken, n - kv * TILES + 1)
                        turn_pairs(w.q[:, t - 2, :], t)

            @block.scalar
            def _(act):
                def square(t):
                    act.wait_ge(x_ready, t + 1)
                    nc.scalar.activation(xn[:, t, :], core.x[:, t, :], ACT.Square,
                                         accum_out=ss[:, t:t + 1]).then_inc(sq_ready, 1)
                    act.wait_ge(var_ready, t + 1)
                    nc.scalar.activation(rs[:, 1, t:t + 1], rs[:, 0, t:t + 1], ACT.Sqrt).then_inc(root_ready, 1)

                def take_h(t):
                    act.wait_ge(turned, 2 * t + 2)
                    for k in range(4, KD):
                        out, src, amp, shift = h_part(t, k)
                        ins = nc.scalar.activation(out, src, ACT.Identity, scale=amp, bias=shift)
                    ins.then_inc(h_act, 1)

                square(0)
                take_h(0)
                for t in range(TILES):
                    for b in range(kv):
                        if t + 1 < TILES and b == 1:
                            square(t + 1)
                        if t + 1 < TILES and b == kv - 1:
                            take_h(t + 1)
                        n = kv * t + b
                        act.wait_ge(summed, n + 1)
                        out = (w.k, w.v)[b // 2][:, t, (b % 2) * COLS:(b % 2 + 1) * COLS]
                        nc.scalar.copy(out, core.ps[:, n % 6, :]).then_inc(kv_taken, 1)


def turn_odd(core, a, w):
    nc = core.nc
    with Stage(nc, "turn1") as st:
        lam = st.sb("lam", [P, 4, HEAD])
        dots = st.sb("dots", [P, 4])
        lam_in, own = st.sem("lam_in"), st.sem("own")
        dots_ready, exps_ready = st.sem("dots_ready"), st.sem("exps_ready")
        turned, taken = st.sem("turned"), [st.sem("taken_dve"), st.sem("taken_act")]
        items = [("k", c, 0) for c in range(KD)] + [("k", c, 1) for c in range(KD)] + [("q", c, 1) for c in range(KD)]

        def target(kind, c, s):
            return w.kT[:, c, s * CTX:(s + 1) * CTX] if kind == "k" else w.qT[:, c, :]

        with nc.Block() as block:
            @block.sync
            def _(sp):
                for i, name in enumerate(("diff_lq1", "diff_lk1", "diff_lq2", "diff_lk2")):
                    sp.dma_start(lam[:, i, :], a[name].to_broadcast([P, HEAD])).then_inc(lam_in, 16)
                sp.dma_start(w.sub_gain[:], a["diff_sub_gain"].to_broadcast([P, 2 * HEAD])).then_inc(lam_in, 16)

            @block.tensor
            def _(pe):
                for n, (kind, c, s) in enumerate(items):
                    if n >= 8:
                        pe.wait_ge(taken[n % 2], (n - 8) // 2 + 1)
                    for j in range(2):
                        src = w.k[:, 2 * s + j] if kind == "k" else w.q[:, j]
                        mm = nc.tensor.transpose(core.ps[:, n % 8, j * P:(j + 1) * P], src[:, c * P:(c + 1) * P],
                                                 core.c("ident"))
                    mm.then_inc(turned, 1)

            @block.scalar
            def _(act):
                for n in range(1, len(items), 2):
                    act.wait_ge(turned, n + 1)
                    nc.scalar.copy(target(*items[n]), core.ps[:, n % 8, 0:CTX]).then_inc(taken[1], 1)
                act.wait_ge(dots_ready, 1)
                nc.scalar.activation(dots[:, 2:4], dots[:, 0:2], ACT.Exp).then_inc(exps_ready, 1)

            @block.vector
            def _(dve):
                link = Chain(dve, own)

                def take(n):
                    dve.wait_ge(turned, n + 1)
                    nc.vector.tensor_copy(target(*items[n]), core.ps[:, n % 8, 0:CTX]).then_inc(taken[0], 1)

                for n in range(0, len(items), 2):
                    take(n)
                dve.wait_ge(lam_in, 16 * 5)
                for i in range(2):
                    link(nc.vector.tensor_tensor(lam[:, 2 * i, :], lam[:, 2 * i, :], lam[:, 2 * i + 1, :], ALU.mult))
                    ins = nc.vector.tensor_reduce(dots[:, i:i + 1], lam[:, 2 * i, :], AX, ALU.add)
                ins.then_inc(dots_ready, 1)
                link(nc.vector.tensor_scalar(w.sub_gain[:], w.sub_gain[:], 1.0 - LAM_INIT, None, ALU.mult))
                dve.wait_ge(exps_ready, 1)
                link(nc.vector.tensor_tensor(dots[:, 0:1], dots[:, 3:4], dots[:, 2:3], ALU.subtract))
                link(nc.vector.tensor_scalar(w.neg_lam[:], dots[:, 0:1], -LAM_INIT, None, ALU.add))


def attend_odd(core, w):
    nc = core.nc
    KEYS = CTX + LAT
    with Stage(nc, "attn1") as st:
        p = st.sb("p", [P, 4, 2, KEYS])
        pd = st.sb("pd", [P, 2, KEYS])
        pT = st.sb("pT", [P, 2, 4, P])
        mx = st.sb("mx", [P, 4, 2, 2])
        sm = st.sb("sm", [P, 4, 4])
        sq = st.sb("sq", [P, 2, P])
        o_squared = st.sem("o_squared")
        sc = lambda n: (0, 6)[n % 2]
        names = ("scored", "max_own", "max_ready", "exp_ready", "recip_ready", "scaled", "mixed", "turned",
                 "pT_ready", "summed", "o_taken")
        (scored, max_own, max_ready, exp_ready, recip_ready, scaled, mixed, turned, pT_ready, summed,
         o_taken) = (st.sem(n) for n in names)
        items = [(h, t) for h in range(DIFF_HEADS) for t in range(2)]
        N = len(items)
        with nc.Block() as block:
            @block.tensor
            def _(pe):
                def score(n):
                    h, t = items[n]
                    if n >= 2:
                        pe.wait_ge(exp_ready, n - 1)
                    for c in range(2):
                        base = HEAD * c
                        mm = nc.tensor.matmul(core.ps[:, sc(n) + c, :], w.qT[base:base + HEAD, h, t * P:(t + 1) * P],
                                              w.kT[base:base + HEAD, h, :], start=True, stop=True)
                    mm.then_inc(scored, 1)

                def turn(n):
                    pe.wait_ge(mixed, n + 1)
                    if n >= 2:
                        pe.wait_ge(pT_ready, n - 1)
                    for kt in range(4):
                        mm = nc.tensor.transpose(core.ps[:, 2 + n % 2, kt * P:(kt + 1) * P],
                                                 pd[:, n % 2, kt * P:(kt + 1) * P], core.c("ident"))
                    mm.then_inc(turned, 1)

                def weigh(n):
                    h, t = items[n]
                    pe.wait_ge(pT_ready, n + 1)
                    if n >= 2:
                        pe.wait_ge(o_taken, n - 1)
                    for kt in range(4):
                        mm = nc.tensor.matmul(core.ps[:, 4 + n % 2, 0:P], pT[:, n % 2, kt, :],
                                              w.v[:, kt, h * P:(h + 1) * P], start=kt == 0, stop=kt == 3)
                    mm.then_inc(summed, 1)

                for n in range(N + 4):
                    if n < N:
                        score(n)
                    if 3 <= n < N + 3:
                        turn(n - 3)
                    if 4 <= n:
                        weigh(n - 4)

            @block.scalar
            def _(act):
                def exps(n):
                    if n >= 4:
                        act.wait_ge(mixed, n - 3)
                    act.wait_ge(max_ready, n + 1)
                    for c in range(2):
                        ins = nc.scalar.activation(p[:, n % 4, c, :], core.ps[:, sc(n) + c, :], ACT.Exp,
                                                   bias=mx[:, n % 4, 1, c:c + 1], accum_out=sm[:, n % 4, c:c + 1])
                    ins.then_inc(exp_ready, 1)

                def take_turned(n):
                    act.wait_ge(turned, n + 1)
                    if n >= 2:
                        act.wait_ge(summed, n - 1)
                    nc.scalar.copy(pT[:, n % 2].rearrange("p k q -> p (k q)"), core.ps[:, 2 + n % 2, :]).then_inc(pT_ready, 1)

                def square_out(n):
                    act.wait_ge(o_taken, n + 1)
                    if n >= 2:
                        act.wait_ge(o_squared, n - 1)
                    h, t = items[n]
                    at = DIFF_HEADS * t + h
                    nc.scalar.activation(sq[:, n % 2, :], w.o[:, t, h, :], ACT.Square,
                                         accum_out=w.o_sq[:, at:at + 1]).then_inc(o_squared, 1)

                for n in range(N + 5):
                    if n < N:
                        exps(n)
                    if 3 <= n < N + 3:
                        take_turned(n - 3)
                    if 5 <= n:
                        square_out(n - 5)

            @block.gpsimd
            def _(pool):
                for n in range(N):
                    pool.wait_ge(recip_ready, n + 1)
                    nc.gpsimd.tensor_scalar(p[:, n % 4, 1, :], p[:, n % 4, 1, :], sm[:, n % 4, 3:4], w.neg_lam[:, 0:1],
                                            ALU.mult, ALU.mult).then_inc(scaled, 1)

            @block.vector
            def _(dve):
                def take_max(n):
                    dve.wait_ge(scored, n + 1)
                    if n >= 4:
                        dve.wait_ge(exp_ready, n - 3)
                    nc.vector.tensor_reduce(mx[:, n % 4, 0, :], core.ps[:, sc(n):sc(n) + 2, :], AX, ALU.max).then_inc(max_own, 1)
                    dve.wait_ge(max_own, n + 1)
                    nc.vector.tensor_scalar(mx[:, n % 4, 1, :], mx[:, n % 4, 0, :], -1.0, None, ALU.mult).then_inc(max_ready, 1)

                def recip(n):
                    dve.wait_ge(exp_ready, n + 1)
                    nc.vector.reciprocal(sm[:, n % 4, 2:4], sm[:, n % 4, 0:2]).then_inc(recip_ready, 1)

                def mix(n):
                    dve.wait_ge(scaled, n + 1)
                    if n >= 2:
                        dve.wait_ge(turned, n - 1)
                    nc.vector.scalar_tensor_tensor(out=pd[:, n % 2, :], in0=p[:, n % 4, 0, :], scalar=sm[:, n % 4, 2:3],
                                                   in1=p[:, n % 4, 1, :], op0=ALU.mult, op1=ALU.add).then_inc(mixed, 1)

                def take_out(n):
                    h, t = items[n]
                    dve.wait_ge(summed, n + 1)
                    nc.vector.tensor_copy(w.o[:, t, h, :], core.ps[:, 4 + n % 2, 0:P]).then_inc(o_taken, 1)

                for n in range(N + 5):
                    if n < N:
                        take_max(n)
                    if 1 <= n < N + 1:
                        recip(n - 1)
                    if 2 <= n < N + 2:
                        mix(n - 2)
                    if 5 <= n:
                        take_out(n - 5)


def norm_heads(core, w):
    nc = core.nc
    H = DIFF_HEADS
    with Stage(nc, "subnorm") as st:
        sq = st.sb("sq", [P, 2 * H, 2 * HEAD])
        rs = st.sb("rs", [P, 4, 2 * H])
        own, var_ready, root_ready, o_ready, turned, taken = (
            st.sem(n) for n in ("own", "var_ready", "root_ready", "o_ready", "turned", "taken"))
        o = w.o[:].rearrange("p t h d -> p (t h) d")
        with nc.Block() as block:
            @block.vector
            def _(dve):
                link = Chain(dve, own)
                nc.vector.tensor_scalar(rs[:, 1, :], w.o_sq[:], 1.0 / P, EPS, ALU.mult, ALU.add).then_inc(var_ready, 1)
                dve.wait_ge(root_ready, 1)
                link(nc.vector.reciprocal(rs[:, 3, :], rs[:, 2, :]))
                for t in range(2):
                    for h in range(H):
                        n = t * H + h
                        ins = nc.vector.scalar_tensor_tensor(out=sq[:, n, :], in0=o[:, n, :], scalar=rs[:, 3, n:n + 1],
                                                             in1=w.sub_gain[:], op0=ALU.mult, op1=ALU.mult)
                    ins.then_inc(o_ready, 1)
                for n in range(4):
                    dve.wait_ge(turned, n + 1)
                    t, half = n // 2, n % 2
                    nc.vector.tensor_copy(core.hT[:, 4 * half:4 * half + 4, t * P:(t + 1) * P],
                                          core.ps[:, n, :].rearrange("p (h q) -> p h q", q=P)).then_inc(taken, 1)

            @block.scalar
            def _(act):
                act.wait_ge(var_ready, 1)
                nc.scalar.activation(rs[:, 2, :], rs[:, 1, :], ACT.Sqrt).then_inc(root_ready, 1)

            @block.tensor
            def _(pe):
                for n in range(4):
                    pe.wait_ge(o_ready, n // 2 + 1)
                    for i in range(4):
                        mm = nc.tensor.transpose(core.ps[:, n, i * P:(i + 1) * P], sq[:, 4 * n + i, :], core.c("ident"))
                    mm.then_inc(turned, 1)


class OddBuffers:
    def __init__(self, core):
        self.nc = core.nc
        self.k, self.v = core.piece(0, 2), core.piece(2, 2)
        self.q = core.pool[:, 4, :].rearrange("p (t d) -> p t d", t=2)

    def more(self, stack):
        def sb(name, shape):
            return stack.enter_context(self.nc.sbuf_tensor(name, shape, F32))

        self.qT, self.kT = sb("qT1", [P, KD, LAT]), sb("kT1", [P, KD, CTX + LAT])
        self.o = sb("o1", [P, 2, DIFF_HEADS, 2 * HEAD])
        self.o_sq = sb("o_sq", [P, 2 * DIFF_HEADS])
        self.sub_gain = sb("sub_gain", [P, 2 * HEAD])
        self.neg_lam = sb("neg_lam", [P, 1])


def layer_odd(core, a, w):
    with ExitStack() as stack:
        w.more(stack)
        turn_odd(core, a, w)
        attend_odd(core, w)
        norm_heads(core, w)
        project_out(core, 1, "diff_w_out", [2, 3], lambda t: slice((t - 2) * P, (t - 1) * P))


def finish(core, a, out):
    nc = core.nc
    with Stage(nc, "final") as st:
        xn = core.xn
        gain = st.sb("gain", [P, D])
        gain_in, done, stored = (st.sem(n) for n in ("gain_in", "done", "stored"))
        with nc.Block() as block:
            @block.sync
            def _(sp):
                sp.dma_start(gain[:], a["final_norm"].rearrange("(o d) -> o d", o=1).to_broadcast([P, D])).then_inc(gain_in, 16)
                for i in range(2):
                    sp.wait_ge(done, i + 1)
                    sp.dma_start(out[0, i * P:(i + 1) * P, :], xn[:, i, :]).then_inc(stored, 16)
                sp.wait_ge(stored, 32)

            @block.vector
            def _(dve):
                dve.wait_ge(gain_in, 16)
                for i in range(2):
                    nc.vector.tensor_tensor(xn[:, i, :], xn[:, i, :], gain[:], ALU.mult).then_inc(done, 1)


def backbone(nc, a, out):
    with ExitStack() as ctx:
        core = Core(nc, ctx, a)
        modulation(core, a)
        layer_even(core, a)
        w = OddBuffers(core)
        with ExitStack() as stack:
            r = Routing(core, stack, a, 0, TILES)
            moe(core, a, 0, list(range(TILES)), r)
            combine_project(core, r, w)
        layer_odd(core, a, w)
        with ExitStack() as stack:
            r = Routing(core, stack, a, 1, 2)
            moe(core, a, 1, [2, 3], r)
            combine(core, r, 1, [2, 3])
        finish(core, a, out)


_INS = ["x", "c", "ctx", "c_ctx", "ada_w", "ada_b", "norm_mix", "norm_ffn", "ab_w_in", "ab_w_out", "na_rpb",
        "gqa_q_gain", "gqa_k_gain", "diff_w_in", "diff_w_out", "diff_lq1", "diff_lk1", "diff_lq2", "diff_lk2",
        "diff_sub_gain", "router_w", "router_bias", "expert_w_gate", "expert_w_up", "expert_w_down",
        "shared_w_gate", "shared_w_up", "shared_w_down", "final_norm"]
_OUT = (1, LAT, D)


def kernel(**inputs):
    import concourse.bacc as _bacc
    from concourse.bass_utils import run_bass_kernel_spmd as _run

    nc = _bacc.Bacc("TRN2", target_bir_lowering=False, num_devices=1)
    arrays, args = {}, {}
    for name in _INS + ["consts"]:
        v = constants() if name == "consts" else np.ascontiguousarray(inputs[name])
        arrays[f"in_{name}_dram"] = v
        args[name] = nc.dram_tensor(f"in_{name}_dram", v.shape, mybir.dt.from_np(v.dtype), kind="ExternalInput").ap()
    out = nc.dram_tensor("out_0_dram", _OUT, F32, kind="ExternalOutput").ap()
    backbone(nc, args, out)
    r = _run(nc, [arrays], core_ids=[0])
    return r.results[0]["out_0_dram"]
```
